# Optimizing a Trainium2 kernel written in Bass

```python
import jax
import jax.numpy as jnp
from jax import lax
import numpy as np
import jax, jax.numpy as jnp

D_MODEL = 1024
BATCH = 1
SEQ = 256
DEPTH = 1

CTX_LEN = 256
GRID_W = 64

POOL_WINDOWS = (2, 4, 8, 16)
POOL_GROUPS = len(POOL_WINDOWS)
POOL_GROUP_DIM = 128
POOL_WIDTH = POOL_GROUPS * POOL_GROUP_DIM

GLA_HEADS = 4
GLA_DK = D_MODEL // 2
GLA_DV = D_MODEL
GLA_HK = GLA_DK // GLA_HEADS
GLA_HV = GLA_DV // GLA_HEADS
GLA_GATE_RANK = 16
GLA_GATE_NORMALIZER = 16.0
GLA_CHUNK = 64

N_BRANCHES = 2
IN_WIDTHS = (POOL_WIDTH, GLA_DK, GLA_DK, GLA_DV, GLA_DV, N_BRANCHES * D_MODEL, 2 * GLA_GATE_RANK)
IN_SPLITS = tuple(int(s) for s in np.cumsum(IN_WIDTHS)[:-1])
D_IN = int(sum(IN_WIDTHS))

N_GROUPS = 4
EXPERTS_PER_GROUP = 8
N_EXPERTS = N_GROUPS * EXPERTS_PER_GROUP
TOP_K_IN_GROUP = 2
D_EXPERT = D_MODEL // 2

MOD_CHUNKS = 6
EPS = 1e-6


def _rmsnorm(x, g):
    xf = x.astype(jnp.float32)
    y = xf * lax.rsqrt(jnp.mean(xf * xf, axis=-1, keepdims=True) + EPS)
    return (y * g.astype(jnp.float32)).astype(x.dtype)

def _adaln(cond, w_mod, b_mod):
    return jnp.split(jnp.matmul(jax.nn.silu(cond), w_mod) + b_mod, MOD_CHUNKS, axis=-1)

def _heads(t, hd):
    b, l, _ = t.shape
    return t.reshape(b, l, GLA_HEADS, hd).transpose(0, 2, 1, 3)

def _flip(t):
    return jnp.flip(t, axis=2)

def _project(h, w_in, a2_f, ab_f, a2_b, ab_b):
    p = jnp.einsum('bld,de->ble', h, w_in)
    u, q, k, v, g, gates, lr = jnp.split(p, IN_SPLITS, axis=-1)
    lr_f, lr_b = jnp.split(lr, 2, axis=-1)
    la_f = jax.nn.log_sigmoid(jnp.matmul(lr_f, a2_f).astype(jnp.float32) + ab_f.astype(jnp.float32)) / GLA_GATE_NORMALIZER
    la_b = jax.nn.log_sigmoid(jnp.matmul(lr_b, a2_b).astype(jnp.float32) + ab_b.astype(jnp.float32)) / GLA_GATE_NORMALIZER
    return (u, _heads(q, GLA_HK) * (GLA_HK ** -0.5), _heads(k, GLA_HK), _heads(v, GLA_HV),
            _heads(la_f, GLA_HK), _heads(la_b, GLA_HK), g, gates)

def _centred_pool_minus_self(u):
    n, l, _ = u.shape
    uf = u.astype(jnp.float32)
    cs = jnp.concatenate([jnp.zeros((n, 1, POOL_WIDTH), jnp.float32), jnp.cumsum(uf, axis=1)], axis=1)
    t = np.arange(l)
    means = []
    for gi, w in enumerate(POOL_WINDOWS):
        lo = np.clip(t - w // 2, 0, l)
        hi = np.clip(t + w // 2, 0, l)
        cg = cs[..., gi * POOL_GROUP_DIM:(gi + 1) * POOL_GROUP_DIM]
        cnt = jnp.asarray((hi - lo)[:, None], jnp.float32)
        means.append((cg[:, hi] - cg[:, lo]) / cnt)
    return (jnp.concatenate(means, axis=-1) - uf).astype(u.dtype)

def _gla_chunked(q, k, v, log_a, s0):
    b, h, l, _ = q.shape
    dv = v.shape[-1]
    n = l // GLA_CHUNK

    def chunks(t):
        return t.astype(jnp.float32).reshape(b, h, n, GLA_CHUNK, t.shape[-1])

    qc, kc, vc, la = chunks(q), chunks(k), chunks(v), chunks(log_a)
    cum = jnp.cumsum(la, axis=3)
    last = cum[:, :, :, -1:, :]
    q_dec = qc * jnp.exp(cum)
    k_inv = kc * jnp.exp(-cum)
    k_rem = kc * jnp.exp(last - cum)
    lower = np.tril(np.ones((GLA_CHUNK, GLA_CHUNK), dtype=bool))
    scores = jnp.where(lower, jnp.einsum('bhnid,bhnjd->bhnij', q_dec, k_inv), 0.0)
    o_intra = jnp.einsum('bhnij,bhnjv->bhniv', scores, vc)
    decay = jnp.exp(last[:, :, :, 0, :])

    def step(state, inp):
        q_n, k_n, v_n, d_n = inp
        o_n = jnp.einsum('bhid,bhdv->bhiv', q_n, state)
        state = d_n[..., None] * state + jnp.einsum('bhid,bhiv->bhdv', k_n, v_n)
        return state, o_n

    xs = tuple(jnp.moveaxis(t, 2, 0) for t in (q_dec, k_rem, vc, decay))
    s_final, o_inter = lax.scan(step, s0, xs)
    o = o_intra + jnp.moveaxis(o_inter, 0, 2)
    return o.reshape(b, h, l, dv).astype(v.dtype), s_final

def _gla_final_state(k, v, log_a):
    cum = jnp.cumsum(log_a, axis=2)
    k_rem = k.astype(jnp.float32) * jnp.exp(cum[:, :, -1:, :] - cum)
    return jnp.einsum('bhtd,bhtv->bhdv', k_rem, v.astype(jnp.float32))

def _gla_bidirectional(q, k, v, la_f, la_b, s0_f, s0_b):
    o_f, _ = _gla_chunked(q, k, v, la_f, s0_f)
    o_b, _ = _gla_chunked(_flip(q), _flip(k), _flip(v), _flip(la_b), s0_b)
    return o_f + _flip(o_b)

def _mixer_out(pooled, o, g, gates, pool_w, pool_scale, gla_onorm_g, w_pool_br, w_gla_br, w_o):
    b, l, _ = pooled.shape
    y_pool = jnp.einsum('blgc,gce->blge', pooled.reshape(b, l, POOL_GROUPS, POOL_GROUP_DIM), pool_w)
    y_pool = jnp.matmul(y_pool.reshape(b, l, POOL_WIDTH) * pool_scale, w_pool_br)
    o = _rmsnorm(o, gla_onorm_g).transpose(0, 2, 1, 3).reshape(b, l, GLA_DV)
    y_gla = jnp.matmul(o * jax.nn.silu(g), w_gla_br)
    gate_pool, gate_gla = jnp.split(jax.nn.sigmoid(gates), N_BRANCHES, axis=-1)
    return jnp.matmul(gate_pool * y_pool + gate_gla * y_gla, w_o)

def _hier_moe(h, rg_w, rg_b, re_w, re_b, w1, w3, w2):
    b, l, d = h.shape
    t = h.reshape(b * l, d)
    grp_logits = (jnp.matmul(t, rg_w) + rg_b).astype(jnp.float32)
    grp_top, grp_idx = lax.top_k(grp_logits, 1)
    p_grp = jnp.exp(grp_top - jax.nn.logsumexp(grp_logits, axis=-1, keepdims=True))
    exp_logits = (jnp.matmul(t, re_w) + re_b).astype(jnp.float32).reshape(-1, N_GROUPS, EXPERTS_PER_GROUP)
    in_grp = jnp.einsum('tg,tge->te', jax.nn.one_hot(grp_idx[:, 0], N_GROUPS, dtype=jnp.float32), exp_logits)
    top_v, top_i = lax.top_k(in_grp, TOP_K_IN_GROUP)
    w = jax.nn.softmax(top_v, axis=-1) * p_grp
    expert_idx = grp_idx * EXPERTS_PER_GROUP + top_i
    combine = jnp.einsum('tk,tke->te', w, jax.nn.one_hot(expert_idx, N_EXPERTS, dtype=jnp.float32)).astype(h.dtype)
    out = jnp.zeros_like(t)
    for e in range(N_EXPERTS):
        hid = jax.nn.silu(jnp.matmul(t, w1[e])) * jnp.matmul(t, w3[e])
        out = out + combine[:, e:e + 1] * jnp.matmul(hid, w2[e])
    return out.reshape(b, l, d)

def first_inputs(seed: int = 0) -> dict:
    key = jax.random.key(seed)
    ks = jax.random.split(key, 32)
    d = D_MODEL

    def nrm(k, shape, scale):
        return jax.random.normal(k, shape, jnp.float32) * scale

    return {
        'x': nrm(ks[0], (BATCH, SEQ, d), 1.0),
        'c': nrm(ks[1], (BATCH, d), 1.0),
        'ctx': nrm(ks[2], (BATCH, CTX_LEN, d), 1.0),
        'c_ctx': nrm(ks[3], (d,), 1.0),
        'w_mod': nrm(ks[4], (DEPTH, d, MOD_CHUNKS * d), 0.5 * d ** -0.5),
        'b_mod': nrm(ks[5], (DEPTH, MOD_CHUNKS * d), 0.02),
        'norm1_g': 1.0 + nrm(ks[6], (DEPTH, d), 0.05),
        'norm2_g': 1.0 + nrm(ks[7], (DEPTH, d), 0.05),
        'w_in': nrm(ks[8], (DEPTH, d, D_IN), d ** -0.5),
        'gla_a2_f': nrm(ks[9], (DEPTH, GLA_GATE_RANK, GLA_DK), GLA_GATE_RANK ** -0.5),
        'gla_ab_f': nrm(ks[10], (DEPTH, GLA_DK), 0.5),
        'gla_a2_b': nrm(ks[11], (DEPTH, GLA_GATE_RANK, GLA_DK), GLA_GATE_RANK ** -0.5),
        'gla_ab_b': nrm(ks[12], (DEPTH, GLA_DK), 0.5),
        'gla_onorm_g': 1.0 + nrm(ks[13], (DEPTH, GLA_HV), 0.05),
        'pool_w': nrm(ks[14], (DEPTH, POOL_GROUPS, POOL_GROUP_DIM, POOL_GROUP_DIM), POOL_GROUP_DIM ** -0.5),
        'pool_scale': 1.0 + nrm(ks[15], (DEPTH, POOL_WIDTH), 0.1),
        'w_pool_br': nrm(ks[16], (DEPTH, POOL_WIDTH, d), POOL_WIDTH ** -0.5),
        'w_gla_br': nrm(ks[17], (DEPTH, GLA_DV, d), GLA_DV ** -0.5),
        'w_o': nrm(ks[18], (DEPTH, d, d), d ** -0.5),
        'router_grp_w': nrm(ks[19], (DEPTH, d, N_GROUPS), d ** -0.5),
        'router_grp_b': nrm(ks[20], (DEPTH, N_GROUPS), 0.01),
        'router_exp_w': nrm(ks[21], (DEPTH, d, N_EXPERTS), d ** -0.5),
        'router_exp_b': nrm(ks[22], (DEPTH, N_EXPERTS), 0.01),
        'moe_w1': nrm(ks[23], (DEPTH, N_EXPERTS, d, D_EXPERT), d ** -0.5),
        'moe_w3': nrm(ks[24], (DEPTH, N_EXPERTS, d, D_EXPERT), d ** -0.5),
        'moe_w2': nrm(ks[25], (DEPTH, N_EXPERTS, D_EXPERT, d), D_EXPERT ** -0.5),
        'final_norm_g': 1.0 + nrm(ks[26], (d,), 0.05),
    }

def first_block(x, c, ctx, c_ctx, w_mod, b_mod, norm1_g, norm2_g, w_in, gla_a2_f, gla_ab_f, gla_a2_b, gla_ab_b,
              gla_onorm_g, pool_w, pool_scale, w_pool_br, w_gla_br, w_o, router_grp_w, router_grp_b,
              router_exp_w, router_exp_b, moe_w1, moe_w3, moe_w2, final_norm_g):
    b, seq, d = x.shape
    rows = seq // GRID_W
    for i in range(DEPTH):
        proj_params = (w_in[i], gla_a2_f[i], gla_ab_f[i], gla_a2_b[i], gla_ab_b[i])
        mix_params = (pool_w[i], pool_scale[i], gla_onorm_g[i], w_pool_br[i], w_gla_br[i], w_o[i])
        moe_params = (router_grp_w[i], router_grp_b[i], router_exp_w[i], router_exp_b[i],
                      moe_w1[i], moe_w3[i], moe_w2[i])
        sh1, sc1, g1, sh2, sc2, g2 = [m[:, None, :] for m in _adaln(c, w_mod[i], b_mod[i])]
        csh1, csc1, cg1, csh2, csc2, cg2 = _adaln(c_ctx, w_mod[i], b_mod[i])

        hc = _rmsnorm(ctx, norm1_g[i]) * (1 + csc1) + csh1
        uc, qc, kc, vc, lfc, lbc, gc, gtc = _project(hc, *proj_params)
        st_f = _gla_final_state(kc, vc, lfc)
        st_b = _gla_final_state(_flip(kc), _flip(vc), _flip(lbc))

        hx = _rmsnorm(x, norm1_g[i]) * (1 + sc1) + sh1
        ux, qx, kx, vx, lfx, lbx, gx, gtx = _project(hx, *proj_params)
        pooled_x = _centred_pool_minus_self(ux.reshape(b * rows, GRID_W, POOL_WIDTH)).reshape(b, seq, POOL_WIDTH)
        ox = _gla_bidirectional(qx, kx, vx, lfx, lbx, st_f, st_b)
        x = x + g1 * _mixer_out(pooled_x, ox, gx, gtx, *mix_params)
        x = x + g2 * _hier_moe(_rmsnorm(x, norm2_g[i]) * (1 + sc2) + sh2, *moe_params)

        if i + 1 < DEPTH:
            zero_state = jnp.zeros_like(st_f)
            oc = _gla_bidirectional(qc, kc, vc, lfc, lbc, zero_state, zero_state)
            ctx = ctx + cg1 * _mixer_out(_centred_pool_minus_self(uc), oc, gc, gtc, *mix_params)
            ctx = ctx + cg2 * _hier_moe(_rmsnorm(ctx, norm2_g[i]) * (1 + csc2) + csh2, *moe_params)
    return _rmsnorm(x, final_norm_g)


DEPTH_2 = 2

HEAD_DIM = 64
N_MIXERS = 2
MOBA_HEADS = 16
MOBA_BLOCK = 256
MOBA_TOPK = 3
MOBA_Q_CHUNK = 32
DIL_GROUPS = ((128, 1), (512, 4), (2048, 16))
DIL_HEADS_PER_GROUP = 4
DIL_HEADS = DIL_HEADS_PER_GROUP * len(DIL_GROUPS)
DIL_BLOCK = 128
D_FF = 4 * D_MODEL
ROPE_THETA = 10000.0
LN_EPS = 1e-5
DEEPNORM_ALPHA = (2.0 * DEPTH_2) ** 0.25
DEEPNORM_BETA = (8.0 * DEPTH_2) ** -0.25
N_LAYERS_A = (DEPTH_2 + N_MIXERS - 1) // N_MIXERS
N_LAYERS_B = DEPTH_2 // N_MIXERS


def layer_norm(x, g, b):
    xf = x.astype(jnp.float32)
    mu = jnp.mean(xf, axis=-1, keepdims=True)
    var = jnp.mean(jnp.square(xf - mu), axis=-1, keepdims=True)
    y = (xf - mu) * lax.rsqrt(var + LN_EPS)
    return (y * g.astype(jnp.float32) + b.astype(jnp.float32)).astype(x.dtype)

def rotary_tables(seq, dtype):
    inv = 1.0 / (ROPE_THETA ** (jnp.arange(0, HEAD_DIM, 2, dtype=jnp.float32) / HEAD_DIM))
    ang = jnp.arange(seq, dtype=jnp.float32)[:, None] * inv[None, :]
    return jnp.cos(ang).astype(dtype), jnp.sin(ang).astype(dtype)

def apply_rotary(t, cos, sin):
    t1, t2 = jnp.split(t, 2, axis=-1)
    c = cos[None, :, None, :]
    s = sin[None, :, None, :]
    return jnp.concatenate([t1 * c - t2 * s, t2 * c + t1 * s], axis=-1)

def moba_attention(x, w_qkv, w_o, cos, sin):
    B, S, _ = x.shape
    H, dh, BLK, QC = MOBA_HEADS, HEAD_DIM, MOBA_BLOCK, MOBA_Q_CHUNK
    qkv = (x @ w_qkv).reshape(B, S, 3, H, dh)
    q = apply_rotary(qkv[:, :, 0], cos, sin) * (dh ** -0.5)
    k = apply_rotary(qkv[:, :, 1], cos, sin)
    v = qkv[:, :, 2]
    pad = (-S) % BLK
    Sp = S + pad
    nb = Sp // BLK
    padw = ((0, 0), (0, pad), (0, 0), (0, 0))
    q = jnp.pad(q, padw).transpose(0, 2, 1, 3)
    k = jnp.pad(k, padw).transpose(0, 2, 1, 3)
    v = jnp.pad(v, padw).transpose(0, 2, 1, 3)
    k_blk = k.reshape(B, H, nb, BLK, dh)
    v_blk = v.reshape(B, H, nb, BLK, dh)
    k_mean = jnp.mean(k_blk.astype(jnp.float32), axis=3).astype(k.dtype)

    gate = jnp.einsum('bhsd,bhnd->bhsn', q, k_mean).astype(jnp.float32)
    q_block = jnp.arange(Sp) // BLK
    past = jnp.arange(nb)[None, :] < q_block[:, None]
    gate = jnp.where(past[None, None], gate, -jnp.inf)
    kk = min(MOBA_TOPK, nb)
    sel_score, sel_idx = lax.top_k(gate, kk)
    sel_valid = jnp.isfinite(sel_score)

    nc = Sp // QC
    q_c = q.reshape(B, H, nc, QC, dh).transpose(2, 0, 1, 3, 4)
    idx_c = sel_idx.reshape(B, H, nc, QC, kk).transpose(2, 0, 1, 3, 4)
    val_c = sel_valid.reshape(B, H, nc, QC, kk).transpose(2, 0, 1, 3, 4)
    b_ix = jnp.arange(B)[:, None, None, None]
    h_ix = jnp.arange(H)[None, :, None, None]
    key_off = jnp.arange(BLK)

    def one_chunk(args):
        c, qc, idx, valid = args
        kg = k_blk[b_ix, h_ix, idx]
        vg = v_blk[b_ix, h_ix, idx]
        s_past = jnp.einsum('bhqd,bhqnkd->bhqnk', qc, kg).astype(jnp.float32)
        s_past = jnp.where(valid[..., None], s_past, -jnp.inf).reshape(B, H, QC, kk * BLK)
        start = c * QC
        blk = start // BLK
        k_own = lax.dynamic_index_in_dim(k_blk, blk, axis=2, keepdims=False)
        v_own = lax.dynamic_index_in_dim(v_blk, blk, axis=2, keepdims=False)
        s_own = jnp.einsum('bhqd,bhkd->bhqk', qc, k_own).astype(jnp.float32)
        q_off = start % BLK + jnp.arange(QC)
        causal = key_off[None, :] <= q_off[:, None]
        s_own = jnp.where(causal[None, None], s_own, -jnp.inf)
        p = jax.nn.softmax(jnp.concatenate([s_past, s_own], axis=-1), axis=-1).astype(v.dtype)
        p_past = p[..., :kk * BLK].reshape(B, H, QC, kk, BLK)
        p_own = p[..., kk * BLK:]
        return (jnp.einsum('bhqnk,bhqnkd->bhqd', p_past, vg)
                + jnp.einsum('bhqk,bhkd->bhqd', p_own, v_own))

    out = lax.map(one_chunk, (jnp.arange(nc, dtype=jnp.int32), q_c, idx_c, val_c))
    out = out.transpose(1, 0, 3, 2, 4).reshape(B, Sp, H * dh)[:, :S]
    return out @ w_o

def dilated_group(q, k, v, window, dilation):
    B, S, Hg, dh = q.shape
    span = window // dilation
    WB = DIL_BLOCK
    assert span <= WB
    L = S // dilation
    Lp = -(-L // WB) * WB
    nblk = Lp // WB

    def to_blocks(t):
        t = t.reshape(B, L, dilation, Hg, dh).transpose(0, 2, 1, 3, 4)
        t = jnp.pad(t, ((0, 0), (0, 0), (0, Lp - L), (0, 0), (0, 0)))
        return t.reshape(B, dilation, nblk, WB, Hg, dh)

    def with_prev(t):
        prev = jnp.pad(t, ((0, 0), (0, 0), (1, 0), (0, 0), (0, 0), (0, 0)))[:, :, :-1]
        return jnp.concatenate([prev, t], axis=3)

    qb = to_blocks(q)
    kw = with_prev(to_blocks(k))
    vw = with_prev(to_blocks(v))
    s = jnp.einsum('brnqhd,brnkhd->brnhqk', qb, kw).astype(jnp.float32)
    qi = jnp.arange(nblk)[:, None, None] * WB + jnp.arange(WB)[None, :, None]
    ki = jnp.arange(nblk)[:, None, None] * WB - WB + jnp.arange(2 * WB)[None, None, :]
    dist = qi - ki
    mask = (dist >= 0) & (dist <= span) & (ki >= 0)
    s = jnp.where(mask[None, None, :, None], s, -jnp.inf)
    lse = jax.nn.logsumexp(s, axis=-1)
    p = jnp.exp(s - lse[..., None]).astype(v.dtype)
    o = jnp.einsum('brnhqk,brnkhd->brnqhd', p, vw)
    o = o.reshape(B, dilation, Lp, Hg, dh)[:, :, :L].transpose(0, 2, 1, 3, 4).reshape(B, S, Hg, dh)
    lse = lse.transpose(0, 1, 2, 4, 3).reshape(B, dilation, Lp, Hg)[:, :, :L]
    lse = lse.transpose(0, 2, 1, 3).reshape(B, S, Hg)
    return o, lse

def dilated_attention(x, w_qkv, w_o, cos, sin):
    B, S, _ = x.shape
    G, Hg, dh = len(DIL_GROUPS), DIL_HEADS_PER_GROUP, HEAD_DIM
    qkv = (x @ w_qkv).reshape(B, S, 3, DIL_HEADS, dh)
    q = apply_rotary(qkv[:, :, 0], cos, sin) * (dh ** -0.5)
    k = apply_rotary(qkv[:, :, 1], cos, sin)
    v = qkv[:, :, 2]
    outs, lses = [], []
    for g, (window, dilation) in enumerate(DIL_GROUPS):
        hs = slice(g * Hg, (g + 1) * Hg)
        o_g, lse_g = dilated_group(q[:, :, hs], k[:, :, hs], v[:, :, hs], window, dilation)
        outs.append(o_g)
        lses.append(lse_g)
    alpha = jax.nn.softmax(jnp.stack(lses, axis=0), axis=0).astype(x.dtype)
    o = jnp.stack(outs, axis=0) * alpha[..., None]
    o = o.transpose(1, 2, 0, 3, 4).reshape(B, S, G * Hg * dh)
    return o @ w_o

def sq_relu_mlp(x, w_in, w_out):
    return jnp.square(jax.nn.relu(x @ w_in)) @ w_out

def second_inputs(seed: int = 0) -> dict:
    key = jax.random.key(seed)
    ks = jax.random.split(key, 12)
    f32 = jnp.float32
    moba_w = MOBA_HEADS * HEAD_DIM
    dil_w = DIL_HEADS * HEAD_DIM
    x = jax.random.normal(ks[0], (BATCH, SEQ, D_MODEL), f32)
    moba_w_qkv = jax.random.normal(ks[1], (N_LAYERS_A, D_MODEL, 3 * moba_w), f32) * D_MODEL ** -0.5
    moba_w_o = jax.random.normal(ks[2], (N_LAYERS_A, moba_w, D_MODEL), f32) * (moba_w ** -0.5 * DEEPNORM_BETA)
    dil_w_qkv = jax.random.normal(ks[3], (N_LAYERS_B, D_MODEL, 3 * dil_w), f32) * D_MODEL ** -0.5
    dil_w_o = jax.random.normal(ks[4], (N_LAYERS_B, dil_w, D_MODEL), f32) * (dil_w ** -0.5 * DEEPNORM_BETA)
    mlp_w_in = jax.random.normal(ks[5], (DEPTH_2, D_MODEL, D_FF), f32) * D_MODEL ** -0.5
    mlp_w_out = jax.random.normal(ks[6], (DEPTH_2, D_FF, D_MODEL), f32) * (D_FF ** -0.5 * DEEPNORM_BETA)
    ln_mix_g = 1.0 + 0.02 * jax.random.normal(ks[7], (DEPTH_2, D_MODEL), f32)
    ln_mix_b = 0.02 * jax.random.normal(ks[8], (DEPTH_2, D_MODEL), f32)
    ln_mlp_g = 1.0 + 0.02 * jax.random.normal(ks[9], (DEPTH_2, D_MODEL), f32)
    ln_mlp_b = 0.02 * jax.random.normal(ks[10], (DEPTH_2, D_MODEL), f32)
    return {"x": x, "moba_w_qkv": moba_w_qkv, "moba_w_o": moba_w_o,
            "dil_w_qkv": dil_w_qkv, "dil_w_o": dil_w_o,
            "mlp_w_in": mlp_w_in, "mlp_w_out": mlp_w_out,
            "ln_mix_g": ln_mix_g, "ln_mix_b": ln_mix_b,
            "ln_mlp_g": ln_mlp_g, "ln_mlp_b": ln_mlp_b}

def second_block(x, moba_w_qkv, moba_w_o, dil_w_qkv, dil_w_o, mlp_w_in, mlp_w_out,
              ln_mix_g, ln_mix_b, ln_mlp_g, ln_mlp_b):
    S = x.shape[1]
    cos, sin = rotary_tables(S, x.dtype)
    h = x
    for i in range(DEPTH_2):
        j = i // N_MIXERS
        if i % N_MIXERS == 0:
            mix = moba_attention(h, moba_w_qkv[j], moba_w_o[j], cos, sin)
        else:
            mix = dilated_attention(h, dil_w_qkv[j], dil_w_o[j], cos, sin)
        h = layer_norm(DEEPNORM_ALPHA * h + mix, ln_mix_g[i], ln_mix_b[i])
        h = layer_norm(DEEPNORM_ALPHA * h + sq_relu_mlp(h, mlp_w_in[i], mlp_w_out[i]),
                       ln_mlp_g[i], ln_mlp_b[i])
    return h


def setup_inputs(seed=0):
    out = dict(first_inputs(seed))
    for name, value in second_inputs(seed + 1).items():
        if name != "x":
            out[name + "_2"] = value
    return out


def reference(
    x, c, ctx, c_ctx, w_mod, b_mod, norm1_g, norm2_g, w_in, gla_a2_f, gla_ab_f, gla_a2_b,
    gla_ab_b, gla_onorm_g, pool_w, pool_scale, w_pool_br, w_gla_br, w_o, router_grp_w,
    router_grp_b, router_exp_w, router_exp_b, moe_w1, moe_w3, moe_w2, final_norm_g,
    moba_w_qkv_2, moba_w_o_2, dil_w_qkv_2, dil_w_o_2, mlp_w_in_2, mlp_w_out_2, ln_mix_g_2,
    ln_mix_b_2, ln_mlp_g_2, ln_mlp_b_2,
):
    x = first_block(
        x, c, ctx, c_ctx, w_mod, b_mod, norm1_g, norm2_g, w_in, gla_a2_f, gla_ab_f, gla_a2_b,
        gla_ab_b, gla_onorm_g, pool_w, pool_scale, w_pool_br, w_gla_br, w_o, router_grp_w,
        router_grp_b, router_exp_w, router_exp_b, moe_w1, moe_w3, moe_w2, final_norm_g,
    )
    return second_block(
        x, moba_w_qkv_2, moba_w_o_2, dil_w_qkv_2, dil_w_o_2, mlp_w_in_2, mlp_w_out_2,
        ln_mix_g_2, ln_mix_b_2, ln_mlp_g_2, ln_mlp_b_2,
    )


_drawn_inputs = setup_inputs


def setup_inputs(seed=0):
    import zlib

    import numpy as np

    out = dict(_drawn_inputs(seed))
    spreads = {}
    factors = {'c_ctx': 3.33,
     'norm1_g': 3.456,
     'gla_a2_f': 3.613,
     'gla_a2_b': 3.747,
     'gla_onorm_g': 6.762,
     'pool_scale': 3.187,
     'router_grp_b': 64.0,
     'router_exp_b': 64.0,
     'norm2_g': 8.0}
    for name, (base, spread) in spreads.items():
        noise = np.random.default_rng([zlib.crc32(name.encode()), seed]).standard_normal(out[name].shape)
        drawn = base * np.exp(spread * noise) if base else spread * noise
        out[name] = jnp.asarray(drawn.astype(out[name].dtype))
    for name, factor in factors.items():
        out[name] = (out[name] * factor).astype(out[name].dtype)
    return out
```

```python
import numpy as np

import concourse.bass as bass
from concourse import mybir
from contextlib import ExitStack

P = 128
D = 1024
KT = D // P
T = 256
TT = T // P
CH = 64
NCH = T // CH
NH = 4
HV = 256
DK = NH * P
RANK = 16
POOLG = 4
WINDOWS = (2, 4, 8, 16)
NE, NG, EG = 32, 4, 8
DE = 512
FF = 4096
SLAB = 4096
HD = 64
MOBA_H, DIL_H, DIL_SLOTS = 16, 12, 4
DIL = ((128, 1), (512, 4), (2048, 16))
EPS, LN_EPS = 1e-6, 1e-5
ALPHA = 4.0 ** 0.25
GATE_NORM = 16.0
NEG = -1e30
SC_W = 384


def constants():
    s, t = np.arange(P)[:, None], np.arange(P)[None, :]
    chunk = (s // CH) == (t // CH)
    inv = 1.0 / GATE_NORM
    parts = {
        "ident": s == t,
        "ones": np.ones((P, P)),
        "cum_f": (chunk & (s <= t)) * inv, "cum_b": (chunk & (s >= t)) * inv,
        "rem_f": (chunk & (s > t)) * inv, "rem_b": (chunk & (s < t)) * inv,
        "suf": (s > t) * inv, "pre": (s < t) * inv, "all": np.full((P, P), inv),
    }
    for g, w in enumerate(WINDOWS):
        lo = np.clip(t % CH - w // 2, 0, CH)
        hi = np.clip(t % CH + w // 2, 0, CH)
        inside = chunk & (s % CH >= lo) & (s % CH < hi)
        parts[f"pool{g}"] = inside / (hi - lo) - (s == t)
    half = HD // 2
    rot = np.zeros((P, P))
    for i in range(P):
        if i % HD < half:
            rot[i + half, i] = -1.0
        else:
            rot[i - half, i] = 1.0
    parts["rot"] = rot
    freq = (1.0 / (10000.0 ** (np.arange(0, HD, 2, dtype=np.float32) / HD))).astype(np.float32)
    ang = np.arange(T, dtype=np.float32)[:, None] * freq[None, :]
    parts["cos"] = np.tile(np.cos(ang).astype(np.float32).T, (4, 1))
    parts["sin"] = np.tile(np.sin(ang).astype(np.float32).T, (4, 1))
    parts["sel"] = (s[:, :1] % 32 == np.arange(2)[None, :]) * 1.0
    parts["sel"] = np.broadcast_to(parts["sel"], (P, 2))
    parts["zero"] = np.zeros((P, P))
    parts["desc4"] = np.broadcast_to(np.arange(4, 0, -1.0), (P, 4))
    parts["desc8"] = np.broadcast_to(np.arange(8, 0, -1.0), (P, 8))
    at, cols, n = {}, [], 0
    for name, a in parts.items():
        a = np.asarray(a, np.float32)
        at[name] = (n, a.shape[1])
        cols.append(a)
        n += a.shape[1]
    return at, np.ascontiguousarray(np.concatenate(cols, 1), np.float32)


def score_masks():
    out = []
    for span, dil in ((T, 1),) + tuple((w // d, d) for w, d in DIL):
        q, k = np.arange(T)[:, None], np.arange(T)[None, :]
        dist = q - k
        ok = (dist >= 0) & (dist % dil == 0) & (dist // dil <= span)
        m = np.where(ok, 0.0, NEG).astype(np.float32)
        out.append(np.concatenate([m[:P, :P], m[P:, :]], 1))
    return np.ascontiguousarray(np.stack(out, 1), np.float32)


CONST_AT, _ = constants()


VEC_ROWS = (("c", KT), ("c_ctx", KT), ("b_mod", 6 * KT), ("norm1_g", KT), ("norm2_g", KT),
            ("final_norm_g", KT), ("pool_scale", POOLG), ("gla_onorm_g", HV // P))
LN_ROWS = (("ln_mix_g_2", 2 * KT), ("ln_mix_b_2", 2 * KT), ("ln_mlp_g_2", 2 * KT), ("ln_mlp_b_2", 2 * KT))
COL, _n = {}, 0
for _name, _k in VEC_ROWS + LN_ROWS:
    COL[_name] = (_n, _k)
    _n += _k
NVEC = sum(k for _, k in VEC_ROWS)
NLN = sum(k for _, k in LN_ROWS)

SETS = ([(h,) for h in range(MOBA_H)], [tuple(j + DIL_SLOTS * g for g in range(3)) for j in range(DIL_SLOTS)])


def slab_plan():
    order = [("mod", s) for s in range(4)]
    order += [("w_in", 2), ("w_in", 3), ("w_in", 4), ("w_in", 1), ("w_in", 0), ("w_in", 5), ("w_in", 6)]
    order += [("w_in", s) for s in range(7, 11)]
    order += [("mod", s) for s in range(4, 12)]
    order += [("pool_br", 0), ("gla_br", 0), ("gla_br", 1), ("w_o", 0), ("w_o", 1)]
    order += [("moe", s) for s in range(3 * NE)]
    for l in range(2):
        order += [(f"qkv{l}", s) for s in range(6 if l == 0 else 5)]
        order += [(f"proj{l}", s) for s in range(2)]
        order += [(f"ff_in{l}", s) for s in range(FF // 512)]
        order += [(f"ff_out{l}", s) for s in range(FF // 512)]
    return {key: n for n, key in enumerate(order)}


def bank_plan():
    order = [("vectors", 0, "V")]
    order += [("x_tiles", i, "A") for i in range(4)] + [("c_tiles", i, "V") for i in range(4)]
    for s in range(4):
        order += [("mod_rows", s, "A"), ("mod_cols", s, "V")]
    order += [("norm", 0, "A"), ("norm", 1, "A")]
    order += [("lr", i, "A") for i in range(2)]
    order += [("z", i, "V") for i in range(8)]
    order += [("cum", i, "A") for i in range(4)]
    order += [("remx", i, "A") for i in range(4)]
    order += [("remc", i, "A") for i in range(4)]
    order += [("kT", i, "V") for i in range(2)] + [("kc", i, "V") for i in range(2)] + [("ktok", i, "V") for i in range(2)]
    for s in range(2):
        order += [("v", 4 * s + i, "A") for i in range(4)]
    order += [("qT", i, "V") for i in range(2)]
    for h in range(NH):
        order += [("s0", h, "A"), ("sT", h, "V")]
        order += [("kv", (h, n, d), "V") for n in range(NCH - 1) for d in range(2)]
        order += [("o", h, "A")]
    order += [("u", i, "A") for i in range(2)] + [("pool", i, "V") for i in range(2)] + [("y1", i, "V") for i in range(2)]
    order += [("g", i, "A") for i in range(4)]
    order += [("oT", i, "V") for i in range(4)]
    order += [("gate", i, "A") for i in range(8)]
    for s in range(4, 12):
        order += [("mod_rows", s, "A"), ("mod_cols", s, "V")]
    order += [("ypool", i, "V") for i in range(4)]
    order += [("ygla", i, "V") for i in range(4)]
    order += [("mix", i, "V") for i in range(4)]
    order += [("norm", 2, "A")]
    order += [("router", 0, "V")]
    order += [("comb", i, "A") for i in range(NE // 2)]
    order += [("moe", 4 * e + i, "A" if i < 2 else "V") for e in range(NE) for i in range(4)]
    order += [("norm", 3, "A")]
    for l in range(2):
        nt = 8 if l == 0 else 6
        order += [(f"qk{l}", i, "A") for i in range(nt)]
        order += [(f"rot{l}", i, "V") for i in range(nt)]
        order += [(f"val{l}", i, "A") for i in range(4)]
        sets = SETS[l]
        order += [(f"sc{l}", (0, j), "V") for j in range(len(sets[0]))]
        for i in range(len(sets)):
            if i + 1 < len(sets):
                order += [(f"sc{l}", (i + 1, j), "V") for j in range(len(sets[i]))]
            for j in range(len(sets[i])):
                order += [(f"pt{l}", (i, j), "A")]
            for j in range(len(sets[i])):
                order += [(f"pv{l}", (i, j), "A")]
        order += [(f"proj{l}", i, "V") for i in range(4)]
        order += [("mean", 2 * l, "V"), ("norm", 4 + 2 * l, "A")]
        order += [(f"ff{l}", i, "A") for i in range(FF // 256)]
        order += [("mean", 2 * l + 1, "V"), ("norm", 5 + 2 * l, "A")]
    order += [("out", i, "A") for i in range(4)]
    return order


SLAB_AT = slab_plan()
_ORDER = bank_plan()
SLABS = list(SLAB_AT)
BANK_AT = {(name, i): n for n, (name, i, _) in enumerate(_ORDER)}
OWNER = [o for _, _, o in _ORDER]


def build(nc, a, out):
    F32 = mybir.dt.float32
    U32 = mybir.dt.uint32
    ALU = mybir.AluOpType
    ACT = mybir.ActivationFunctionType
    AX = mybir.AxisListType

    ctx = ExitStack()
    with ctx:
        def sem(name):
            return ctx.enter_context(nc.semaphore(name))

        def sb(name, shape):
            return ctx.enter_context(nc.sbuf_tensor(name, shape, F32))

        NC = sum(w for _, w in CONST_AT.values())
        const = sb("const", [P, NC])

        def C(name):
            o, w = CONST_AT[name]
            return const[:, o:o + w]

        ident, ones = C("ident"), C("ones")
        K1 = 1024
        ARENA = 45 * K1
        arena = sb("arena", [P, ARENA])

        def at(o, *dims):
            n = int(np.prod(dims))
            assert o + n <= ARENA
            names = " ".join(f"x{i}" for i in range(len(dims)))
            v = arena[:, o:o + n]
            if len(dims) == 1:
                return v
            return v.rearrange(f"p ({names}) -> p {names}", **{f"x{i}": d for i, d in enumerate(dims)})

        RING = 4
        slot = [at(SLAB * i, SLAB) for i in range(RING)]
        xT = at(16 * K1, KT, T)
        hT = at(18 * K1, KT, T)
        sq = at(20 * K1, KT, T)
        cT = at(22 * K1, KT, T)
        L = at(24 * K1, 8, DK)
        S = at(24 * K1, 2, NCH, HV)
        sTm = at(26 * K1, 4, P)
        y1 = at(27 * K1, POOLG, T)
        dec = at(28 * K1, 2, 2, NH, T)
        xtok = at(28 * K1, TT, D)
        ctok = at(30 * K1, TT, D)
        gates = at(28 * K1, 2 * KT, T)
        remx = at(32 * K1, 2, TT, DK)
        remc = at(34 * K1, 2, TT, DK)
        ktok = at(36 * K1, TT, DK)
        kT = at(37 * K1, NH, T)
        vx = at(38 * K1, TT, D)
        vc = at(40 * K1, TT, D)
        gT = at(40 * K1, KT, T)
        otok = at(42 * K1, TT, D)
        utok = at(22 * K1, TT, DK)
        pooled = at(23 * K1, POOLG, T)
        mod_row = at(44 * K1, 2, 512)
        az = at(20 * K1, DK)
        ez = at(20 * K1 + DK, DK)
        comb_bc = at(22 * K1, NE, T)
        hid = at(30 * K1, 2, 4, T)
        silu1 = at(32 * K1, 2, 4, T)
        qk_raw = at(22 * K1, 16, T)
        qk = at(26 * K1, 16, T)
        vt = at(30 * K1, TT, D)
        attT = at(32 * K1, KT, T)
        sc = at(34 * K1, 2, 3, SC_W)
        pT = at(37 * K1, 3, SC_W)
        masks = at(39 * K1, 4, SC_W)
        hff = at(22 * K1, FF // P, T)

        w_lr = sb("w_lr", [P, KT, 2 * RANK])
        w_pool = sb("w_pool", [P, POOLG, P])
        w_rt = sb("w_rt", [P, KT, NG + NE])
        a2 = at(42 * K1, 2, DK)[0:RANK]
        ab = at(43 * K1, 2, DK)[0:1]
        rb = sb("rb", [1, NG + NE])
        rows = sb("rows", [P, 2, P])
        cols = sb("cols", [P, NVEC + NLN])
        scol = sb("scol", [P, KT, 32])
        mod = sb("mod", [P, 6 * KT, 2])
        scale1 = sb("scale1", [P, 3, KT])
        std = sb("std", [P, T])
        lrT = at(36 * K1, 4, T)[0:RANK]
        decay = sb("decay", [P, 2, NH, NCH])
        oss = sb("oss", [P, TT, NH])
        orstd = sb("orstd", [P, TT, NH])
        oeps = sb("eps", [P, 2])
        lg = sb("lg", [P, TT, NG + NE])
        r4 = sb("r4", [P, 4, TT, NG])
        r8 = sb("r8", [P, 6, TT, EG])
        r1 = sb("r1", [P, 12, TT])
        r32 = sb("r32", [P, TT, NG, EG])
        comb = sb("comb", [P, TT, NE])
        mx = sb("mx", [P, 2, TT])
        ssum = sb("ssum", [P, 2, TT])
        rsum = sb("rsum", [P, 2, TT])

        RB = 4
        OPENED = 2
        ring = ctx.enter_context(nc.psum_tensor("ring", [P, RB, 512], F32))
        acc = ctx.enter_context(nc.psum_tensor("acc", [P, KT, T], F32))

        consts_in = sem("consts_in")
        smalls_in = sem("smalls_in")
        tokens_in = sem("tokens_in")
        masks_in = sem("masks_in")
        landed = [sem(f"slab_landed{i}") for i in range(RING)]
        used = sem("slab_used")
        bank_full = sem("bank_full")
        freed = {"V": sem("bank_freed_by_vector"), "A": sem("bank_freed_by_scalar")}
        v_step = sem("vector_step")
        a_step = sem("scalar_step")
        names = "ff_ready scol_zero scol_ready sq_ready rstd_read h_ready ez_ready ostd_ready on_ready z_ready resid_ready lg_diff rexp_ready comb_ready rot_ready max_ready exp_ready p_ready out_stored eps_ready".split()
        G = {n: sem(n) for n in names}

        def bank_of(name, i):
            return ring[:, BANK_AT[name, i] % RB, :]

        def freed_by(g):
            return freed[OWNER[g]], sum(o == OWNER[g] for o in OWNER[:g + 1])

        def moved(eng, name, i):
            eng.wait_ge(*freed_by(BANK_AT[name, i]))

        def last_pt(k):
            l, i = (0, k) if k < len(SETS[0]) else (1, k - len(SETS[0]))
            return f"pt{l}", (i, len(SETS[l][i]) - 1)

        def slab_freed(n):
            name, s = SLABS[n]
            if name == "moe":
                e, j = divmod(s, 3)
                return (used, OPENED + e + 1) if j == 2 else (bank_full, BANK_AT["moe", 4 * e + 2 * j + 1] + 1)
            if name[:-1] == "ff_out":
                return used, OPENED + NE + (FF // 512) * int(name[-1]) + s + 1
            if name == "w_in":
                bank_use = {0: ("u", 1), 1: ("qT", 1), 2: ("kc", 1), 3: ("v", 3), 4: ("v", 7), 5: ("g", 1), 6: ("g", 3)}.get(s)
                bank_use = bank_use or ("gate", 2 * (s - 7) + 1)
            elif name == "mod":
                bank_use = ("mod_rows", s)
            elif name[:-1] == "qkv":
                nt = 8 if name[-1] == "0" else 6
                bank_use = ("qk" + name[-1], 2 * s + 1) if s < nt // 2 else ("val" + name[-1], 3)
            elif name[:-1] == "ff_in":
                bank_use = ("ff" + name[-1], 2 * s + 1)
            elif name == "pool_br":
                bank_use = ("ypool", 3)
            else:
                bank_use = ({"gla_br": "ygla", "w_o": "mix"}.get(name, name), 2 * s + 1)
            return bank_full, BANK_AT[bank_use] + 1

        def w_in(s):
            return a["w_in"][0][:, 512 * s:512 * s + 512].rearrange("(k p) n -> p k n", p=P)

        def slab_source(name, s):
            if name == "mod":
                return a["w_mod"][0][:, 512 * s:512 * s + 512].rearrange("(k p) n -> p k n", p=P)
            if name == "w_in":
                return w_in(s)
            if name == "pool_br":
                return a["w_pool_br"][0].rearrange("(k p) n -> p k n", p=P)
            if name in ("gla_br", "w_o"):
                w = a["w_gla_br" if name == "gla_br" else "w_o"][0]
                return w[:, 512 * s:512 * s + 512].rearrange("(k p) n -> p k n", p=P)
            l = int(name[-1])
            if name[:-1] == "qkv":
                w = a[("moba", "dil")[l] + "_w_qkv_2"][0]
                return w[:, 512 * s:min(512 * s + 512, w.shape[1])].rearrange("(k p) n -> p k n", p=P)
            if name[:-1] == "proj":
                w = a[("moba", "dil")[l] + "_w_o_2"][0]
                return w[:, 512 * s:512 * s + 512].rearrange("(k p) n -> p k n", p=P)
            if name[:-1] == "ff_in":
                return a["mlp_w_in_2"][l][:, 512 * s:512 * s + 512].rearrange("(k p) n -> p k n", p=P)
            return a["mlp_w_out_2"][l][512 * s:512 * s + 512, :].rearrange("(k p) n -> p k n", p=P)

        def view(n, k, w):
            return slot[n % RING][:, 0:k * w].rearrange("p (k n) -> p k n", k=k)

        block = ctx.enter_context(nc.Block())

        @block.sync
        def _(sp):
            def load(n, src):
                if n >= RING:
                    sp.wait_ge(*slab_freed(n - RING))
                sp.dma_start(view(n, src.shape[1], src.shape[2]), src).then_inc(landed[n % RING], 16)

            def expert_source(j, e):
                w = a[("moe_w1", "moe_w3", "moe_w2")[j]][0]
                return w[bass.ds(e, 1), :, :].rearrange("e (k p) n -> p (e k) n", p=P)

            moe0, n_moe, per = SLAB_AT["moe", 0], 3 * NE, 12
            for (name, s), n in SLAB_AT.items():
                if name != "moe":
                    load(n, slab_source(name, s))
                elif s < RING or s >= n_moe - per + RING:
                    load(n, expert_source(s % 3, s // 3))
                elif s == RING:
                    with sp.Fori(0, NE // 4 - 1) as it:
                        for j in range(RING, RING + per):
                            what, before = slab_freed(moe0 + j - RING)
                            sp.wait_ge(what, it * (4 if what is used else 16) + before)
                            src = expert_source(j % 3, it * 4 + j // 3)
                            sp.dma_start(view(moe0 + j, src.shape[1], src.shape[2]), src).then_inc(landed[(moe0 + j) % RING], 16)
            for tt in range(TT):
                moved(sp, "out", 2 * tt + 1)
                sp.dma_start(out[0][tt * P:(tt + 1) * P, :], xtok[:, tt, :]).then_inc(G["out_stored"], 16)
            sp.wait_ge(G["out_stored"], 16 * TT)

        SMALLS = []

        @block.scalar
        def _(act):
            n_step = [0]

            def link(ins):
                n_step[0] += 1
                ins.then_inc(a_step, 1)
                act.wait_ge(a_step, n_step[0])

            def take(name, i):
                act.wait_ge(bank_full, BANK_AT[name, i] + 1)
                return bank_of(name, i)

            def free(ins):
                ins.then_inc(freed["A"], 1)

            act.dma_start(const[:, :], a["consts"]).then_inc(consts_in, 16)

            def small(dst, src):
                act.dma_start(dst, src).then_inc(smalls_in, 16)
                SMALLS.append(1)

            for table, r, base in ((VEC_ROWS, 0, 0), (LN_ROWS, 1, NVEC)):
                for name, n in table:
                    o = COL[name][0] - base
                    src = a[name]
                    while len(src.shape) > 1 and src.shape[0] == 1:
                        src = src[0]
                    if len(src.shape) == 2:
                        src = src.rearrange("l (r p) -> (l r) p", p=P)
                    else:
                        src = src.rearrange("(r p) -> r p", p=P)
                    small(rows[o:o + n, r, :], src)
            for tt in range(TT):
                act.dma_start(xtok[:, tt, :], a["x"][0][tt * P:(tt + 1) * P, :]).then_inc(tokens_in, 16)
                act.dma_start(ctok[:, tt, :], a["ctx"][0][tt * P:(tt + 1) * P, :]).then_inc(tokens_in, 16)
            small(w_lr[:, :, :], a["w_in"][0][:, 5632:5664].rearrange("(k p) n -> p k n", p=P))
            small(w_pool[:, :, :], a["pool_w"][0].rearrange("g c e -> c g e"))
            small(w_rt[:, :, 0:NG], a["router_grp_w"][0].rearrange("(k p) n -> p k n", p=P))
            small(w_rt[:, :, NG:], a["router_exp_w"][0].rearrange("(k p) n -> p k n", p=P))
            for d, name in enumerate("fb"):
                small(a2[:, d, :], a["gla_a2_" + name][0])
                small(ab[0:1, d, :], a["gla_ab_" + name])
            small(rb[0:1, 0:NG], a["router_grp_b"])
            small(rb[0:1, NG:], a["router_exp_b"])

            def square(src, k):
                act.activation(sq, src, ACT.Square).then_inc(G["sq_ready"], 1)

            def norm_std(k, eps):
                b = take("norm", k)
                ins = act.activation(std[:, :], b[:, 0:T], ACT.Sqrt, bias=oeps[:, eps:eps + 1], scale=1.0 / D)
                ins.then_inc(freed["A"], 1)

            def mod_rows(s):
                b = take("mod_rows", s)
                ins = act.activation(mod_row[:, s % 2, :], b, ACT.Copy)
                ins.then_inc(freed["A"], 1)

            moved(act, "vectors", 0)
            act.wait_ge(G["scol_zero"], 1)
            act.activation(scol[:, :, 0:2], cols[:, 0:2 * KT].rearrange("p (r k) -> p k r", r=2), ACT.Silu).then_inc(G["scol_ready"], 1)
            for i in range(4):
                tt, q = divmod(i, 2)
                b = take("x_tiles", i).rearrange("p (k t) -> p k t", k=4)
                ins = act.activation(xT[:, 4 * q:4 * q + 4, tt * P:(tt + 1) * P], b, ACT.Copy)
                ins.then_inc(freed["A"], 1)
            for s in range(4):
                mod_rows(s)
            act.wait_ge(G["eps_ready"], 1)
            moved(act, "c_tiles", 3)
            square(cT, 0)
            norm_std(0, 0)
            act.wait_ge(G["rstd_read"], 1)
            moved(act, "x_tiles", 3)
            square(xT, 1)
            norm_std(1, 0)
            for i in range(2):
                b = take("lr", i)
                ins = act.activation(lrT[:, 2 * i:2 * i + 2, :], b[0:RANK, :].rearrange("p (d t) -> p d t", d=2), ACT.Copy)
                ins.then_inc(freed["A"], 1)
            for i in range(8):
                b = take("z", i)
                if i:
                    moved(act, "z", i - 1)
                link(act.activation(az, b, ACT.Abs))
                link(act.activation(ez, az, ACT.Exp, scale=-1.0))
                act.activation(ez, ez, ACT.Ln, bias=1.0).then_inc(G["ez_ready"], 1)
            for i in range(4):
                d, hp = divmod(i, 2)
                b = take("cum", i).rearrange("p (h t) -> p h t", h=2)
                act.activation(dec[:, 0, d, 2 * hp:2 * hp + 2, :], b, ACT.Exp)
                ins = act.activation(dec[:, 1, d, 2 * hp:2 * hp + 2, :], b, ACT.Exp, scale=-1.0)
                ins.then_inc(freed["A"], 1)
            for name, dst in (("remx", remx), ("remc", remc)):
                for i in range(4):
                    d, tt = divmod(i, 2)
                    ins = act.activation(dst[:, d, tt, :], take(name, i), ACT.Exp)
                    ins.then_inc(freed["A"], 1)
            for s in range(2):
                for i in range(4):
                    dst = (vx, vc)[i // 2]
                    ins = act.activation(dst[:, i % 2, 512 * s:512 * s + 512], take("v", 4 * s + i), ACT.Copy)
                    ins.then_inc(freed["A"], 1)
            for h in range(NH):
                b = take("s0", h).rearrange("p (d v) -> p d v", d=2)
                if h:
                    act.wait_ge(bank_full, BANK_AT["o", h - 1] + 1)
                act.activation(S[:, 0, 0, :], b[:, 0, :], ACT.Copy)
                ins = act.activation(S[:, 1, NCH - 1, :], b[:, 1, :], ACT.Copy)
                ins.then_inc(freed["A"], 1)
                b = take("o", h).rearrange("p (a v) -> p a v", a=TT)
                ins = act.activation(otok[:, :, h * HV:(h + 1) * HV], b, ACT.Copy)
                ins.then_inc(freed["A"], 1)
                moved(act, "o", h)
                for tt in range(TT):
                    link(act.activation(sq[:, 0, :], otok[:, tt, h * HV:(h + 1) * HV], ACT.Square, accum_out=oss[:, tt, h:h + 1]))
            act.activation(orstd[:, :, :], oss[:, :, :], ACT.Sqrt, bias=oeps[:, 0:1], scale=1.0 / HV).then_inc(G["ostd_ready"], 1)
            for i in range(2):
                ins = act.activation(utok[:, i, :], take("u", i), ACT.Copy)
                ins.then_inc(freed["A"], 1)
            for i in range(4):
                ins = act.activation(gT[:, 2 * i:2 * i + 2, :], take("g", i).rearrange("p (k t) -> p k t", k=2), ACT.Silu)
                ins.then_inc(freed["A"], 1)
            for i in range(8):
                ins = act.activation(gates[:, 2 * i:2 * i + 2, :], take("gate", i).rearrange("p (k t) -> p k t", k=2), ACT.Sigmoid)
                ins.then_inc(freed["A"], 1)
            for s in range(4, 12):
                mod_rows(s)
            act.wait_ge(G["resid_ready"], 1)
            square(xT, 2)
            norm_std(2, 0)
            act.wait_ge(G["lg_diff"], 1)
            act.activation(r4[:, 1, :, :], r4[:, 0, :, :], ACT.Exp).then_inc(G["rexp_ready"], 1)
            act.wait_ge(G["lg_diff"], 2)
            act.activation(r1[:, 6, :], r1[:, 5, :], ACT.Exp).then_inc(G["rexp_ready"], 1)
            for i in range(NE // 2):
                ins = act.activation(comb_bc[:, 2 * i:2 * i + 2, :], take("comb", i).rearrange("p (k t) -> p k t", k=2), ACT.Copy)
                ins.then_inc(freed["A"], 1)
            m0 = BANK_AT["moe", 0]
            v0, a0 = (sum(o == w for o in OWNER[:m0]) for w in "VA")
            with act.Fori(0, NE // 4) as it:
                for j in range(4):
                    for i in range(2):
                        act.wait_ge(bank_full, it * 16 + (m0 + 4 * j + i + 1))
                        b = ring[:, (m0 + 4 * j + i) % RB, :].rearrange("p (k t) -> p k t", k=2)
                        if i == 0:
                            act.wait_ge(freed["V"], it * 8 + (v0 + 2 * (j - 1)))
                        ins = act.activation(silu1[:, j % 2, 2 * i:2 * i + 2, :], b, ACT.Silu)
                        ins.then_inc(freed["A"], 1)
            act.wait_ge(G["resid_ready"], 2)
            square(xT, 3)
            norm_std(3, 0)
            act.dma_start(masks, a["masks"]).then_inc(masks_in, 16)
            hq = [0]
            for l in range(2):
                nt = 8 if l == 0 else 6
                for i in range(nt):
                    ins = act.activation(qk_raw[:, 2 * i:2 * i + 2, :], take(f"qk{l}", i).rearrange("p (k t) -> p k t", k=2), ACT.Copy)
                    ins.then_inc(freed["A"], 1)
                for i in range(4):
                    tt, s = i // 2, i % 2
                    w = 512 if l == 0 or s == 0 else 256
                    ins = act.activation(vt[:, tt, 512 * s:512 * s + w], take(f"val{l}", i)[:, 0:w], ACT.Copy)
                    ins.then_inc(freed["A"], 1)
                sets = SETS[l]
                m0_ = 0 if l == 0 else len(SETS[0])

                def exps(i):
                    k = m0_ + i
                    act.wait_ge(G["max_ready"], k + 1)
                    n = len(sets[i])
                    s_ = sc[:, k % 2, 0:n, :]
                    act.activation(s_[:, :, 0:P], s_[:, :, 0:P], ACT.Exp, scale=HD ** -0.5, bias=mx[:, k % 2, 0:1],
                                   accum_out=ssum[:, k % 2, 0:1])
                    act.activation(s_[:, :, P:SC_W], s_[:, :, P:SC_W], ACT.Exp, scale=HD ** -0.5, bias=mx[:, k % 2, 1:2],
                                   accum_out=ssum[:, k % 2, 1:2]).then_inc(G["exp_ready"], 1)

                exps(0)
                for i in range(len(sets)):
                    if i + 1 < len(sets):
                        exps(i + 1)
                    for j in range(len(sets[i])):
                        ins = act.activation(pT[:, j, :], take(f"pt{l}", (i, j))[:, 0:SC_W], ACT.Copy)
                        ins.then_inc(freed["A"], 1)
                    for j, h in enumerate(sets[i]):
                        o = HD * (h % 2)
                        b = take(f"pv{l}", (i, j))
                        ins = act.activation(attT[o:o + HD, h // 2, :], b[o:o + HD, 0:T], ACT.Copy)
                        ins.then_inc(freed["A"], 1)
                for half in range(2):
                    moved(act, "mean", 2 * l + half)
                    square(xT, 0)
                    norm_std(4 + 2 * l + half, 1)
                    for i in range(FF // 256 if half == 0 else 0):
                        b = take(f"ff{l}", i).rearrange("p (k t) -> p k t", k=2)
                        act.activation(hff[:, 2 * i:2 * i + 2, :], b, ACT.Relu).then_inc(freed["A"], 1)
            for i in range(4):
                tt, q = divmod(i, 2)
                ins = act.activation(xtok[:, tt, 512 * q:512 * q + 512], take("out", i), ACT.Copy)
                ins.then_inc(freed["A"], 1)

        NSM = len(SMALLS)

        @block.vector
        def _(dve):
            n_step = [0]

            def link(ins):
                n_step[0] += 1
                ins.then_inc(v_step, 1)
                dve.wait_ge(v_step, n_step[0])

            def take(name, i):
                dve.wait_ge(bank_full, BANK_AT[name, i] + 1)
                return bank_of(name, i)

            dve.memset(scol[:, :, :], 0.0).then_inc(G["scol_zero"], 1)
            dve.memset(oeps[:, 0:1], EPS)
            dve.memset(oeps[:, 1:2], LN_EPS).then_inc(G["eps_ready"], 1)
            b = take("vectors", 0)
            ins = dve.tensor_copy(cols[:, :], b[:, 0:NVEC + NLN])
            ins.then_inc(freed["V"], 1)

            def col(name, k, n=1):
                o = COL[name][0] + k
                return cols[:, o:o + n]

            for i in range(4):
                tt, q = divmod(i, 2)
                b = take("c_tiles", i).rearrange("p (k t) -> p k t", k=4)
                ins = dve.tensor_copy(cT[:, 4 * q:4 * q + 4, tt * P:(tt + 1) * P], b)
                ins.then_inc(freed["V"], 1)

            moved(dve, "vectors", 0)

            def mod_cols(s):
                b = take("mod_cols", s)
                ins = dve.tensor_tensor(mod[:, 4 * s:4 * s + 4, :], b[:, 0:8].rearrange("p (k r) -> p k r", r=2),
                                        col("b_mod", 4 * s, 4).unsqueeze(2).to_broadcast([P, 4, 2]), ALU.add)
                ins.then_inc(freed["V"], 1)

            for s in range(4):
                mod_cols(s)
            moved(dve, "mod_cols", 3)

            def gain(k, name, chunk, r):
                dve.scalar_tensor_tensor(scale1[:, k, :], mod[:, KT * chunk:KT * chunk + KT, r], 1.0, col(name, 0, KT),
                                         ALU.add, ALU.mult).then_inc(v_step, 1)
                n_step[0] += 1

            gain(0, "norm1_g", 1, 0)
            gain(1, "norm1_g", 1, 1)
            dve.wait_ge(v_step, n_step[0])

            def normed(k, src, dst, scale, shift):
                moved(dve, "norm", k)
                link(dve.reciprocal(std[:, :], std[:, :]))
                link(dve.tensor_tensor(sq, src, std[:, :].unsqueeze(1).to_broadcast([P, KT, T]), ALU.mult))
                for kt in range(KT):
                    if shift is None:
                        ins = dve.tensor_scalar(dst[:, kt, :], sq[:, kt, :], scale(kt), None, ALU.mult)
                    else:
                        ins = dve.tensor_scalar(dst[:, kt, :], sq[:, kt, :], scale(kt), shift(kt), ALU.mult, ALU.add)
                    ins.then_inc(G["h_ready"], 1)
                dve.wait_ge(G["h_ready"], KT * (k + 1))

            normed(0, cT, cT, lambda kt: scale1[:, 1, kt:kt + 1], lambda kt: mod[:, kt, 1:2])
            dve.sem_inc(G["rstd_read"], 1)
            normed(1, xT, hT, lambda kt: scale1[:, 0, kt:kt + 1], lambda kt: mod[:, kt, 0:1])

            for i in range(8):
                b = take("z", i)
                dve.wait_ge(G["ez_ready"], i + 1)
                ins = dve.scalar_tensor_tensor(L[:, i, :], b, 0.0, ez, ALU.min, ALU.subtract)
                ins.then_inc(freed["V"], 1)
            for i in range(2):
                ins = dve.tensor_copy(kT[:, 2 * i:2 * i + 2, :], take("kT", i).rearrange("p (h t) -> p h t", h=2))
                ins.then_inc(freed["V"], 1)
            moved(dve, "kT", 1)
            moved(dve, "cum", 3)
            for d in range(2):
                o = CH - 1 if d == 0 else 0
                dve.tensor_copy(decay[:, d, :, :], dec[:, 0, d, :, :].rearrange("p h (n t) -> p h n t", n=NCH)[:, :, :, o])
                link(dve.tensor_tensor(dec[:, 1, d, :, :], dec[:, 1, d, :, :], kT, ALU.mult))
            for i in range(2):
                b = take("kc", i)
                moved(dve, "remc", 3)
                link(dve.tensor_tensor(remc[:, 0, i, :], remc[:, 0, i, :], b, ALU.mult))
                ins = dve.tensor_tensor(remc[:, 1, i, :], remc[:, 1, i, :], b, ALU.mult)
                ins.then_inc(freed["V"], 1)
            for i in range(2):
                b = take("ktok", i)
                moved(dve, "remx", 3)
                link(dve.tensor_tensor(remx[:, 0, i, :], remx[:, 0, i, :], b, ALU.mult))
                ins = dve.tensor_tensor(remx[:, 1, i, :], remx[:, 1, i, :], b, ALU.mult)
                ins.then_inc(freed["V"], 1)
            for i in range(2):
                b = take("qT", i).rearrange("p (h t) -> p h t", h=2)
                for d in range(2):
                    v = dec[:, 0, d, 2 * i:2 * i + 2, :]
                    ins = dve.scalar_tensor_tensor(v, b, float(np.float32(P ** -0.5)), v, ALU.mult, ALU.mult)
                ins.then_inc(freed["V"], 1)
            moved(dve, "ktok", 1)
            dve.wait_ge(bank_full, BANK_AT["remc", 3] + 1)
            link(dve.memset(sTm, 0.0))
            for h in range(NH):
                b = take("sT", h).rearrange("p (c i) -> p c i", c=4)
                if h:
                    dve.wait_ge(bank_full, BANK_AT["o", h - 1] + 1)
                for c in range(4):
                    m = C("cum_f" if c < 2 else "cum_b").bitcast(U32)
                    ins = dve.copy_predicated(sTm[:, c, :], m, b[:, c, :])
                ins.then_inc(freed["V"], 1)
                moved(dve, "s0", h)
                for n in range(NCH - 1):
                    f, r = n, NCH - 1 - n
                    for d, c, to in ((0, f, f + 1), (1, r, r - 1)):
                        b = take("kv", (h, n, d))[:, 0:HV]
                        if n:
                            moved(dve, "kv", (h, n - 1, d))
                        ins = dve.scalar_tensor_tensor(S[:, d, to, :], S[:, d, c, :], decay[:, d, h, c:c + 1], b, ALU.mult, ALU.add)
                        ins.then_inc(freed["V"], 1)
            dve.wait_ge(G["ostd_ready"], 1)
            link(dve.reciprocal(orstd[:, :, :], orstd[:, :, :]))
            for tt in range(TT):
                v = otok[:, tt, :].rearrange("p (h v) -> p h v", h=NH)
                dve.tensor_tensor(v, v, orstd[:, tt, :].unsqueeze(2).to_broadcast([P, NH, HV]), ALU.mult).then_inc(G["on_ready"], 1)
            for i in range(2):
                ins = dve.tensor_copy(pooled[:, 2 * i:2 * i + 2, :], take("pool", i).rearrange("p (g t) -> p g t", g=2))
                ins.then_inc(freed["V"], 1)
            for i in range(2):
                b = take("y1", i).rearrange("p (g t) -> p g t", g=2)
                dve.tensor_scalar(y1[:, 2 * i, :], b[:, 0, :], col("pool_scale", 2 * i), None, ALU.mult)
                ins = dve.tensor_scalar(y1[:, 2 * i + 1, :], b[:, 1, :], col("pool_scale", 2 * i + 1), None, ALU.mult)
                ins.then_inc(freed["V"], 1)
            for i in range(4):
                tt, q = divmod(i, 2)
                b = take("oT", i).rearrange("p (k r t) -> p k r t", k=2, r=2)
                moved(dve, "g", 3)
                for r in range(2):
                    v = gT[:, 4 * q:4 * q + 4, tt * P:(tt + 1) * P].rearrange("p (k r) t -> p k r t", r=2)[:, :, r, :]
                    ins = dve.scalar_tensor_tensor(v, b[:, :, r, :], col("gla_onorm_g", r), v, ALU.mult, ALU.mult)
                ins.then_inc(freed["V"], 1)
            for s in range(4, 12):
                mod_cols(s)
            moved(dve, "mod_cols", 11)
            gain(2, "norm2_g", 4, 0)
            moved(dve, "gate", 7)
            for i in range(4):
                b = take("ypool", i).rearrange("p (k t) -> p k t", k=2)
                ins = dve.tensor_tensor(sq[:, 2 * i:2 * i + 2, :], b, gates[:, 2 * i:2 * i + 2, :], ALU.mult)
                ins.then_inc(freed["V"], 1)
            for i in range(4):
                b = take("ygla", i).rearrange("p (k t) -> p k t", k=2)
                v = gates[:, KT + 2 * i:KT + 2 * i + 2, :]
                ins = dve.tensor_tensor(v, b, v, ALU.mult)
                ins.then_inc(freed["V"], 1)
                moved(dve, "ygla", i)
                z = sq[:, 2 * i:2 * i + 2, :]
                dve.tensor_tensor(z, z, v, ALU.add).then_inc(G["z_ready"], 1)
            for i in range(4):
                b = take("mix", i).rearrange("p (k t) -> p k t", k=2)
                for r in range(2):
                    kt = 2 * i + r
                    ins = dve.scalar_tensor_tensor(xT[:, kt, :], b[:, r, :], mod[:, 2 * KT + kt, 0:1], xT[:, kt, :], ALU.mult, ALU.add)
                ins.then_inc(freed["V"], 1)
            moved(dve, "mix", 3)
            dve.sem_inc(G["resid_ready"], 1)
            normed(2, xT, hT, lambda kt: scale1[:, 2, kt:kt + 1], lambda kt: mod[:, 3 * KT + kt, 0:1])

            b = take("router", 0)[:, 0:TT * (NG + NE)].rearrange("p (a n) -> p a n", a=TT)
            ins = dve.tensor_copy(lg[:, :, :], b)
            ins.then_inc(freed["V"], 1)
            moved(dve, "router", 0)

            def bc(ap, n):
                return ap.unsqueeze(2).to_broadcast([P, TT, n])

            def first_max(vals, n, m, eq, key, km):
                link(dve.tensor_reduce(m, vals, AX.X, ALU.max))
                link(dve.tensor_tensor(eq, vals, bc(m, n), ALU.is_equal))
                d = C(f"desc{n}").unsqueeze(1).to_broadcast([P, TT, n])
                link(dve.tensor_tensor(key, eq, d, ALU.mult))
                link(dve.tensor_reduce(km, key, AX.X, ALU.max))
                link(dve.tensor_tensor(eq, d, bc(km, n), ALU.is_equal))

            lgg = lg[:, :, 0:NG]
            first_max(lgg, NG, r1[:, 0, :], r4[:, 2, :, :], r4[:, 3, :, :], r1[:, 1, :])
            dve.tensor_tensor(r4[:, 0, :, :], lgg, bc(r1[:, 0, :], NG), ALU.subtract).then_inc(G["lg_diff"], 1)
            grp = r4[:, 2, :, :]
            lge = lg[:, :, NG:].rearrange("p a (g e) -> p a g e", g=NG)
            for tt in range(TT):
                link(dve.tensor_tensor(r32[:, tt, :, :], lge[:, tt, :, :], grp[:, tt, :].unsqueeze(2).to_broadcast([P, NG, EG]), ALU.mult))
            ing = r8[:, 0, :, :]
            for tt in range(TT):
                link(dve.tensor_reduce(ing[:, tt, :], r32[:, tt, :, :].rearrange("p g e -> p e g"), AX.X, ALU.add))
            one, two = r8[:, 1, :, :], r8[:, 2, :, :]
            first_max(ing, EG, r1[:, 2, :], one, r8[:, 3, :, :], r1[:, 3, :])
            link(dve.scalar_tensor_tensor(r8[:, 4, :, :], one, -3.0e38, ing, ALU.mult, ALU.add))
            first_max(r8[:, 4, :, :], EG, r1[:, 4, :], two, r8[:, 3, :, :], r1[:, 3, :])
            dve.tensor_tensor(r1[:, 5, :], r1[:, 4, :], r1[:, 2, :], ALU.subtract).then_inc(G["lg_diff"], 1)
            dve.wait_ge(G["rexp_ready"], 2)
            link(dve.tensor_reduce(r1[:, 7, :], r4[:, 1, :, :], AX.X, ALU.add))
            link(dve.scalar_tensor_tensor(r1[:, 8, :], r1[:, 6, :], 1.0, r1[:, 7, :], ALU.add, ALU.mult))
            link(dve.reciprocal(r1[:, 9, :], r1[:, 8, :]))
            link(dve.tensor_tensor(r1[:, 10, :], r1[:, 9, :], r1[:, 6, :], ALU.mult))
            link(dve.tensor_tensor(one, one, bc(r1[:, 9, :], EG), ALU.mult))
            link(dve.tensor_tensor(two, two, bc(r1[:, 10, :], EG), ALU.mult))
            link(dve.tensor_tensor(one, one, two, ALU.add))
            for tt in range(TT):
                dve.tensor_tensor(comb[:, tt, :].rearrange("p (g e) -> p g e", g=NG), one[:, tt, :].unsqueeze(1).to_broadcast([P, NG, EG]),
                                  grp[:, tt, :].unsqueeze(2).to_broadcast([P, NG, EG]), ALU.mult).then_inc(G["comb_ready"], 1)
            moved(dve, "comb", NE // 2 - 1)
            m0 = BANK_AT["moe", 0]
            v0, a0 = (sum(o == w for o in OWNER[:m0]) for w in "VA")
            with dve.Fori(0, NE // 4) as it:
                for j in range(4):
                    dve.wait_ge(used, it * 4 + (j + OPENED - 1))
                    cb = comb_bc[:, bass.ds(it * 4 + j, 1), :].to_broadcast([P, 2, T])
                    for i in range(2):
                        dve.wait_ge(freed["A"], it * 8 + (a0 + 2 * j + i + 1))
                        s_ = silu1[:, j % 2, 2 * i:2 * i + 2, :]
                        dve.tensor_tensor(s_, s_, cb, ALU.mult).then_inc(v_step, 1)
                    for i in range(2):
                        dve.wait_ge(bank_full, it * 16 + (m0 + 4 * j + 2 + i + 1))
                        dve.wait_ge(v_step, it * 8 + (n_step[0] + 2 * j + i + 1))
                        b = ring[:, (m0 + 4 * j + 2 + i) % RB, :].rearrange("p (k t) -> p k t", k=2)
                        ins = dve.tensor_tensor(hid[:, j % 2, 2 * i:2 * i + 2, :], silu1[:, j % 2, 2 * i:2 * i + 2, :], b, ALU.mult)
                        ins.then_inc(freed["V"], 1)
            n_step[0] += 2 * NE
            dve.wait_ge(*slab_freed(SLAB_AT["moe", 3 * NE - 1]))
            for kt in range(KT):
                ins = dve.scalar_tensor_tensor(xT[:, kt, :], acc[:, kt, :], mod[:, 5 * KT + kt, 0:1], xT[:, kt, :], ALU.mult, ALU.add)
            ins.then_inc(G["resid_ready"], 1)
            dve.wait_ge(G["resid_ready"], 2)
            normed(3, xT, xT, lambda kt: col("final_norm_g", kt), None)

            def centred(k):
                b = take("mean", k)[:, 0:T].unsqueeze(1).to_broadcast([P, KT, T])
                ins = dve.scalar_tensor_tensor(xT, b, -1.0 / D, xT, ALU.mult, ALU.add)
                ins.then_inc(freed["V"], 1)

            for l in range(2):
                nt = 8 if l == 0 else 6
                ntile = 2 * nt
                moved(dve, f"qk{l}", nt - 1)
                ct = C("cos").unsqueeze(1)
                st = C("sin").unsqueeze(1)
                for i in range(nt):
                    b = take(f"rot{l}", i).rearrange("p (k t) -> p k t", k=2)
                    r_, q_ = qk_raw[:, 2 * i:2 * i + 2, :], qk[:, 2 * i:2 * i + 2, :]
                    dve.tensor_tensor(r_, r_, ct.to_broadcast([P, 2, T]), ALU.mult)
                    ins = dve.tensor_tensor(q_, b, st.to_broadcast([P, 2, T]), ALU.mult)
                    ins.then_inc(freed["V"], 1)
                    moved(dve, f"rot{l}", i)
                    dve.tensor_tensor(q_, q_, r_, ALU.add).then_inc(G["rot_ready"], 1)
                sets = SETS[l]
                k0 = 0 if l == 0 else len(SETS[0])
                if l == 0:
                    dve.wait_ge(masks_in, 16)

                def maxes(i):
                    k = k0 + i
                    n = len(sets[i])
                    s_ = sc[:, k % 2, 0:n, :]
                    for j in range(n):
                        b = take(f"sc{l}", (i, j))[:, 0:SC_W]
                        if k >= 2 and j == 0:
                            moved(dve, *last_pt(k - 2))
                        ins = dve.tensor_tensor(s_[:, j, :], b, masks[:, 0 if l == 0 else 1 + j, :], ALU.add)
                        ins.then_inc(freed["V"], 1)
                    moved(dve, f"sc{l}", (i, n - 1))
                    dve.tensor_reduce(mx[:, k % 2, 0:1], s_[:, :, 0:P], AX.XY, ALU.max)
                    link(dve.tensor_reduce(mx[:, k % 2, 1:2], s_[:, :, P:SC_W], AX.XY, ALU.max))
                    dve.tensor_scalar(mx[:, k % 2, :], mx[:, k % 2, :], -(HD ** -0.5), None, ALU.mult).then_inc(G["max_ready"], 1)

                def probs(i):
                    k = k0 + i
                    n = len(sets[i])
                    s_ = sc[:, k % 2, 0:n, :]
                    dve.wait_ge(G["exp_ready"], k + 1)
                    link(dve.reciprocal(rsum[:, k % 2, :], ssum[:, k % 2, :]))
                    dve.tensor_scalar(s_[:, :, 0:P], s_[:, :, 0:P], rsum[:, k % 2, 0:1], None, ALU.mult)
                    dve.tensor_scalar(s_[:, :, P:SC_W], s_[:, :, P:SC_W], rsum[:, k % 2, 1:2], None, ALU.mult).then_inc(G["p_ready"], 1)

                maxes(0)
                for i in range(len(sets)):
                    if i + 1 < len(sets):
                        maxes(i + 1)
                    probs(i)
                for i in range(4):
                    b = take(f"proj{l}", i).rearrange("p (k t) -> p k t", k=2)
                    v = xT[:, 2 * i:2 * i + 2, :]
                    ins = dve.scalar_tensor_tensor(v, v, ALPHA, b, ALU.mult, ALU.add)
                    ins.then_inc(freed["V"], 1)
                moved(dve, f"proj{l}", 3)
                dve.sem_inc(G["resid_ready"], 1)
                centred(2 * l)
                normed(4 + 2 * l, xT, xT, lambda kt: col("ln_mix_g_2", KT * l + kt), lambda kt: col("ln_mix_b_2", KT * l + kt))
                for i in range(FF // 256):
                    moved(dve, f"ff{l}", i)
                    v = hff[:, 2 * i:2 * i + 2, :]
                    dve.tensor_tensor(v, v, v, ALU.mult).then_inc(G["ff_ready"], 1)
                dve.wait_ge(*slab_freed(SLAB_AT[f"ff_out{l}", FF // 512 - 1]))
                ins = dve.scalar_tensor_tensor(xT, xT, ALPHA, acc[:, :, :], ALU.mult, ALU.add)
                ins.then_inc(G["resid_ready"], 1)
                dve.wait_ge(G["resid_ready"], 4 + 2 * l)
                centred(2 * l + 1)
                normed(5 + 2 * l, xT, xT, lambda kt: col("ln_mlp_g_2", KT * l + kt), lambda kt: col("ln_mlp_b_2", KT * l + kt))

        @block.tensor
        def _(pe):
            def bank(name, i):
                g = BANK_AT[name, i]
                if g >= RB:
                    pe.wait_ge(*freed_by(g - RB))
                return bank_of(name, i)

            def arrive(name, s, k, w):
                n = SLAB_AT[name, s]
                pe.wait_ge(landed[n % RING], 16 * (n // RING + 1))
                return view(n, k, w)

            def full(ins):
                ins.then_inc(bank_full, 1)

            def done(ins):
                ins.then_inc(used, 1)

            def turn(name, i, src, tt, q):
                b = bank(name, i)
                for j in range(4):
                    kt = 4 * q + j
                    ins = pe.transpose(b[:, j * P:(j + 1) * P], src[:, tt, kt * P:(kt + 1) * P], ident)
                full(ins)

            def fmajor(b, w, x, m0, n, ks=KT):
                for j in range(n):
                    for kt in range(ks):
                        ins = pe.matmul(b[:, j * T:(j + 1) * T], w[:, kt, m0 + j * P:m0 + (j + 1) * P], x[:, kt, :],
                                        start=(kt == 0), stop=(kt == ks - 1))
                return ins

            def tmajor(b, w, x, tt, ks=KT, n=512):
                for kt in range(ks):
                    ins = pe.matmul(b[:, 0:n], x[:, kt, tt * P:(tt + 1) * P], w[:, kt, 0:n], start=(kt == 0), stop=(kt == ks - 1))
                return ins

            pe.wait_ge(consts_in, 16)
            pe.wait_ge(smalls_in, 16 * NSM)
            b = bank("vectors", 0)
            pe.transpose(b[:, 0:NVEC], rows[0:NVEC, 0, :], ident[0:NVEC, 0:NVEC])
            full(pe.transpose(b[:, NVEC:NVEC + NLN], rows[0:NLN, 1, :], ident[0:NLN, 0:NLN]))
            pe.wait_ge(tokens_in, 16 * 2 * TT)
            for i in range(4):
                turn("x_tiles", i, xtok, *divmod(i, 2))
            for i in range(4):
                turn("c_tiles", i, ctok, *divmod(i, 2))

            def modulate(s):
                if s == 0:
                    pe.wait_ge(G["scol_ready"], 1)
                w = arrive("mod", s, KT, 512)
                b = bank("mod_rows", s)
                for half in range(2):
                    for g in range(4):
                        kt = 4 * half + g
                        ins = pe.matmul(b[32 * g:32 * g + 32, :], scol[:, kt, :], w[:, kt, :], start=(half == 0), stop=(half == 1))
                ins.then_inc(bank_full, 1)
                moved(pe, "mod_rows", s)
                b = bank("mod_cols", s)
                for j in range(4):
                    ins = pe.matmul(b[:, 2 * j:2 * j + 2], mod_row[:, s % 2, j * P:(j + 1) * P], C("sel"), start=True, stop=True)
                full(ins)

            for s in range(4):
                modulate(s)

            def norm_sum(name, k, src):
                b = bank(name, k)
                for kt in range(KT):
                    ins = pe.matmul(b[:, 0:T], ones, src[:, kt, :], start=(kt == 0), stop=(kt == KT - 1))
                full(ins)

            for k in range(2):
                pe.wait_ge(G["sq_ready"], k + 1)
                norm_sum("norm", k, sq)
            pe.wait_ge(G["h_ready"], 2 * KT)
            for i, src in enumerate((hT, cT)):
                b = bank("lr", i)
                for d in range(2):
                    for kt in range(KT):
                        ins = pe.matmul(b[0:RANK, d * T:(d + 1) * T], w_lr[:, kt, d * RANK:(d + 1) * RANK], src[:, kt, :],
                                        start=(kt == 0), stop=(kt == KT - 1))
                full(ins)
            moved(pe, "lr", 1)
            for i in range(8):
                st, tt = divmod(i, 2)
                d = st % 2
                b = bank("z", i)
                pe.matmul(b, lrT[:, st, tt * P:(tt + 1) * P], a2[:, d, :], start=True, stop=False)
                full(pe.matmul(b, ones[0:1, :], ab[0:1, d, :], start=False, stop=True))
            moved(pe, "z", 3)
            for i in range(4):
                d, hp = divmod(i, 2)
                b = bank("cum", i)
                for j in range(2):
                    for tt in range(TT):
                        h = 2 * hp + j
                        ins = pe.matmul(b[:, j * T + tt * P:j * T + (tt + 1) * P], L[:, 2 * d + tt, h * P:(h + 1) * P],
                                        C("cum_" + "fb"[d]), start=True, stop=True)
                full(ins)
            for i in range(4):
                d, tt = divmod(i, 2)
                full(pe.matmul(bank("remx", i), C("rem_" + "fb"[d]), L[:, 2 * d + tt, :], start=True, stop=True))
            moved(pe, "z", 7)
            for i in range(4):
                d, tt = divmod(i, 2)
                b = bank("remc", i)
                other = (d == 0 and tt == 0) or (d == 1 and tt == 1)
                ins = pe.matmul(b, C(("suf", "pre")[d]), L[:, 4 + 2 * d + tt, :], start=True, stop=not other)
                if other:
                    ins = pe.matmul(b, C("all"), L[:, 4 + 2 * d + 1 - tt, :], start=False, stop=True)
                full(ins)
            w = arrive("w_in", 2, KT, 512)
            for i in range(2):
                full(fmajor(bank("kT", i), w, hT, 2 * i * P, 2))
            for i in range(2):
                ins = tmajor(bank("kc", i), w, cT, i)
                full(ins)
            moved(pe, "kT", 1)
            for i in range(2):
                b = bank("ktok", i)
                for h in range(NH):
                    ins = pe.transpose(b[:, h * P:(h + 1) * P], kT[:, h, i * P:(i + 1) * P], ident)
                full(ins)
            for s in range(2):
                w = arrive("w_in", 3 + s, KT, 512)
                for i in range(4):
                    ins = tmajor(bank("v", 4 * s + i), w, (hT, cT)[i // 2], i % 2)
                    full(ins)
            w = arrive("w_in", 1, KT, 512)
            for i in range(2):
                ins = fmajor(bank("qT", i), w, hT, 2 * i * P, 2)
                full(ins)
            moved(pe, "v", 7)
            moved(pe, "ktok", 1)
            moved(pe, "qT", 1)
            for h in range(NH):
                hk, hv = slice(h * P, (h + 1) * P), slice(h * HV, (h + 1) * HV)
                b = bank("s0", h)
                for d in range(2):
                    for tt in range(TT):
                        ins = pe.matmul(b[:, d * HV:(d + 1) * HV], remc[:, d, tt, hk], vc[:, tt, hv], start=(tt == 0), stop=(tt == 1))
                full(ins)
                b = bank("sT", h)
                for d in range(2):
                    for tt in range(TT):
                        t_ = slice(tt * P, (tt + 1) * P)
                        ins = pe.matmul(b[:, (2 * d + tt) * P:(2 * d + tt + 1) * P], dec[:, 1, d, h, t_], dec[:, 0, d, h, t_],
                                        start=True, stop=True)
                full(ins)
                for n in range(NCH - 1):
                    for d in range(2):
                        c = n if d == 0 else NCH - 1 - n
                        tt, o = c // 2, CH * (c % 2)
                        b = bank("kv", (h, n, d))
                        full(pe.matmul(b[:, 0:HV], remx[o:o + CH, d, tt, hk], vx[o:o + CH, tt, hv], start=True, stop=True))
                moved(pe, "sT", h)
                moved(pe, "kv", (h, NCH - 2, 1))
                moved(pe, "s0", h)
                b = bank("o", h)
                for tt in range(TT):
                    bo = b[:, tt * HV:(tt + 1) * HV]
                    for d in range(2):
                        pe.matmul(bo, sTm[:, 2 * d + tt, :], vx[:, tt, hv], start=(d == 0), stop=False, skip_group_check=True)
                    for d in range(2):
                        for c in range(2):
                            n = 2 * tt + c
                            ins = pe.matmul(b[CH * c:CH * (c + 1), tt * HV:(tt + 1) * HV], dec[:, 0, d, h, n * CH:(n + 1) * CH],
                                            S[:, d, n, :], start=False, stop=(d == 1), skip_group_check=True)
                full(ins)
            w = arrive("w_in", 0, KT, 512)
            for i in range(2):
                ins = tmajor(bank("u", i), w, hT, i)
                full(ins)
            moved(pe, "u", 1)
            for i in range(2):
                b = bank("pool", i)
                for j in range(2):
                    g = 2 * i + j
                    for tt in range(TT):
                        ins = pe.matmul(b[:, j * T + tt * P:j * T + (tt + 1) * P], utok[:, tt, g * P:(g + 1) * P], C(f"pool{g}"),
                                        start=True, stop=True)
                full(ins)
            moved(pe, "pool", 1)
            for i in range(2):
                b = bank("y1", i)
                for j in range(2):
                    g = 2 * i + j
                    ins = pe.matmul(b[:, j * T:(j + 1) * T], w_pool[:, g, :], pooled[:, g, :], start=True, stop=True)
                full(ins)
            for s in range(2):
                w = arrive("w_in", 5 + s, KT, 512)
                for i in range(2):
                    ins = fmajor(bank("g", 2 * s + i), w, hT, 2 * i * P, 2)
                    full(ins)
            pe.wait_ge(G["on_ready"], 2)
            for i in range(4):
                turn("oT", i, otok, *divmod(i, 2))
            for s in range(4):
                w = arrive("w_in", 7 + s, KT, 512)
                for i in range(2):
                    ins = fmajor(bank("gate", 2 * s + i), w, hT, 2 * i * P, 2)
                    full(ins)
            for s in range(4, 12):
                modulate(s)
            w = arrive("pool_br", 0, POOLG, D)
            moved(pe, "y1", 1)
            for i in range(4):
                ins = fmajor(bank("ypool", i), w, y1, 2 * i * P, 2, ks=POOLG)
                full(ins)
            moved(pe, "oT", 3)
            for s in range(2):
                w = arrive("gla_br", s, KT, 512)
                for i in range(2):
                    ins = fmajor(bank("ygla", 2 * s + i), w, gT, 2 * i * P, 2)
                    full(ins)
            pe.wait_ge(G["z_ready"], 4)
            for s in range(2):
                w = arrive("w_o", s, KT, 512)
                for i in range(2):
                    ins = fmajor(bank("mix", 2 * s + i), w, sq, 2 * i * P, 2)
                    full(ins)
            pe.wait_ge(G["sq_ready"], 3)
            norm_sum("norm", 2, sq)
            pe.wait_ge(G["h_ready"], 3 * KT)
            b = bank("router", 0)
            for tt in range(TT):
                br = b[:, tt * (NG + NE):(tt + 1) * (NG + NE)]
                for kt in range(KT):
                    pe.matmul(br, hT[:, kt, tt * P:(tt + 1) * P], w_rt[:, kt, :], start=(kt == 0), stop=False)
                ins = pe.matmul(br, ones[0:1, :], rb[0:1, :], start=False, stop=True)
            full(ins)
            pe.wait_ge(G["comb_ready"], 2)
            for i in range(NE // 2):
                b = bank("comb", i)
                for j in range(2):
                    for tt in range(TT):
                        e = 2 * i + j
                        ins = pe.matmul(b[:, j * T + tt * P:j * T + (tt + 1) * P], comb[:, tt, e:e + 1].to_broadcast([P, P]), ident,
                                        start=True, stop=True)
                full(ins)

            def open_acc(k):
                for j in range(4):
                    ins = pe.matmul(acc[:, 2 * j:2 * j + 2, :], zrow, zmov, start=True, stop=False, skip_group_check=True)
                ins.then_inc(used, OPENED)

            zrow, zmov = C("zero")[:, 0:P], hT[:, 0:2, :]
            open_acc(0)
            m0, s0 = BANK_AT["moe", 0], SLAB_AT["moe", 0]
            fv, fa = (sum(o == w for o in OWNER[:m0]) for w in "VA")
            moved(pe, "comb", NE // 2 - 1)
            with pe.Fori(0, NE // 4) as it:
                def up(j):
                    for i in range(4):
                        n = s0 + 3 * j + i // 2
                        if i % 2 == 0:
                            q, r = divmod(n, RING)
                            pe.wait_ge(landed[r], it * 48 + 16 * (q + 1))
                        w = view(n, KT, 512)
                        if i < 2:
                            pe.wait_ge(freed["A"], it * 8 + (fa + 2 * (j - 1) + i + 1))
                        else:
                            pe.wait_ge(freed["V"], it * 8 + (fv + 2 * (j - 1) + i - 2 + 1))
                        b = ring[:, (m0 + 4 * j + i) % RB, :]
                        ins = fmajor(b, w, hT, 2 * (i % 2) * P, 2)
                        full(ins)

                for j in range(4):
                    up(j)
                    n = s0 + 3 * j + 2
                    q, r = divmod(n, RING)
                    pe.wait_ge(landed[r], it * 48 + 16 * (q + 1))
                    w = view(n, 4, D)
                    pe.wait_ge(freed["V"], it * 8 + (fv + 2 * (j + 1)))
                    for kt in range(4):
                        for m in range(KT):
                            ins = pe.matmul(acc[:, m, :], w[:, kt, m * P:(m + 1) * P], hid[:, j % 2, kt, :], start=False, stop=True,
                                            skip_group_check=True)
                    done(ins)
            pe.wait_ge(G["sq_ready"], 4)
            norm_sum("norm", 3, sq)
            for l in range(2):
                nt = 8 if l == 0 else 6
                heads = MOBA_H if l == 0 else DIL_H
                pe.wait_ge(G["h_ready"], (4 + 2 * l) * KT)
                tile_at = 0
                for s in range(nt // 2):
                    w = arrive(f"qkv{l}", s, KT, 512)
                    for i in range(2):
                        ins = fmajor(bank(f"qk{l}", 2 * s + i), w, xT, 2 * i * P, 2)
                        full(ins)
                moved(pe, f"qk{l}", nt - 1)
                for i in range(nt):
                    b = bank(f"rot{l}", i)
                    for j in range(2):
                        ins = pe.matmul(b[:, j * T:(j + 1) * T], C("rot"), qk_raw[:, 2 * i + j, :], start=True, stop=True)
                    full(ins)
                vs = nt // 2
                w2 = 512 if l == 0 else 256
                wa = arrive(f"qkv{l}", vs, KT, 512)
                wb = arrive(f"qkv{l}", vs + 1, KT, w2)
                for tt in range(TT):
                    full(tmajor(bank(f"val{l}", 2 * tt), wa, xT, tt))
                    ins = tmajor(bank(f"val{l}", 2 * tt + 1), wb, xT, tt, n=w2)
                    full(ins)
                moved(pe, f"val{l}", 3)
                pe.wait_ge(G["rot_ready"], nt if l == 0 else 8 + nt)
                sets = SETS[l]
                k0 = 0 if l == 0 else len(SETS[0])

                def scores(i):
                    for j, h in enumerate(sets[i]):
                        b = bank(f"sc{l}", (i, j))
                        o = HD * (h % 2)
                        q_, k_ = qk[o:o + HD, h // 2, :], qk[o:o + HD, nt + h // 2, :]
                        pe.matmul(b[:, 0:P], q_[:, 0:P], k_[:, 0:P], start=True, stop=True)
                        full(pe.matmul(b[:, P:SC_W], q_[:, P:T], k_, start=True, stop=True))

                scores(0)
                for i in range(len(sets)):
                    k = k0 + i
                    if i + 1 < len(sets):
                        scores(i + 1)
                    pe.wait_ge(G["p_ready"], k + 1)
                    for j in range(len(sets[i])):
                        b = bank(f"pt{l}", (i, j))
                        for c in range(3):
                            ins = pe.transpose(b[:, c * P:(c + 1) * P], sc[:, k % 2, j, c * P:(c + 1) * P], ident)
                        full(ins)
                    for j, h in enumerate(sets[i]):
                        moved(pe, f"pt{l}", (i, j))
                        b = bank(f"pv{l}", (i, j))
                        o = HD * (h % 2)
                        hv = slice(h * HD, (h + 1) * HD)
                        pe.matmul(b[o:o + HD, 0:P], vt[:, 0, hv], pT[:, j, 0:P], start=True, stop=True)
                        pe.matmul(b[o:o + HD, P:T], vt[:, 0, hv], pT[:, j, P:2 * P], start=True, stop=False)
                        full(pe.matmul(b[o:o + HD, P:T], vt[:, 1, hv], pT[:, j, 2 * P:3 * P], start=False, stop=True))
                moved(pe, f"pv{l}", (len(sets) - 1, len(sets[-1]) - 1))
                ks = heads * HD // P
                for s in range(2):
                    w = arrive(f"proj{l}", s, ks, 512)
                    for i in range(2):
                        ins = fmajor(bank(f"proj{l}", 2 * s + i), w, attT, 2 * i * P, 2, ks=ks)
                        full(ins)
                pe.wait_ge(G["resid_ready"], 3 + 2 * l)
                norm_sum("mean", 2 * l, xT)
                pe.wait_ge(G["sq_ready"], 5 + 2 * l)
                norm_sum("norm", 4 + 2 * l, sq)
                pe.wait_ge(G["h_ready"], (5 + 2 * l) * KT)
                for s in range(FF // 512):
                    w = arrive(f"ff_in{l}", s, KT, 512)
                    for i in range(2):
                        ins = fmajor(bank(f"ff{l}", 2 * s + i), w, xT, 2 * i * P, 2)
                        full(ins)
                for s in range(FF // 512):
                    w = arrive(f"ff_out{l}", s, 4, D)
                    pe.wait_ge(G["ff_ready"], (FF // 256) * l + 2 * s + 2)
                    for kt in range(4):
                        for m in range(KT):
                            ins = pe.matmul(acc[:, m, :], w[:, kt, m * P:(m + 1) * P], hff[:, 4 * s + kt, :],
                                            start=(s == 0 and kt == 0 and m % 2 == 0), stop=(s == FF // 512 - 1 and kt == 3), skip_group_check=True)
                    done(ins)
                pe.wait_ge(G["resid_ready"], 4 + 2 * l)
                norm_sum("mean", 2 * l + 1, xT)
                pe.wait_ge(G["sq_ready"], 6 + 2 * l)
                norm_sum("norm", 5 + 2 * l, sq)
            pe.wait_ge(G["h_ready"], 8 * KT)
            for i in range(4):
                tt, q = divmod(i, 2)
                b = bank("out", i)
                for j in range(4):
                    ins = pe.transpose(b[:, j * P:(j + 1) * P], xT[:, 4 * q + j, tt * P:(tt + 1) * P], ident)
                full(ins)


_INS = ["x", "c", "ctx", "c_ctx", "w_mod", "b_mod", "norm1_g", "norm2_g", "w_in", "gla_a2_f", "gla_ab_f", "gla_a2_b",
        "gla_ab_b", "gla_onorm_g", "pool_w", "pool_scale", "w_pool_br", "w_gla_br", "w_o", "router_grp_w", "router_grp_b",
        "router_exp_w", "router_exp_b", "moe_w1", "moe_w3", "moe_w2", "final_norm_g", "moba_w_qkv_2", "moba_w_o_2",
        "dil_w_qkv_2", "dil_w_o_2", "mlp_w_in_2", "mlp_w_out_2", "ln_mix_g_2", "ln_mix_b_2", "ln_mlp_g_2", "ln_mlp_b_2"]


def kernel(**inputs):
    from concourse import bacc
    from concourse.bass_utils import run_bass_kernel_spmd

    nc = bacc.Bacc("TRN2", target_bir_lowering=False, num_devices=1)
    arrays = {name: np.ascontiguousarray(inputs[name]) for name in _INS}
    arrays["consts"] = constants()[1]
    arrays["masks"] = score_masks()
    args = {name: nc.dram_tensor("in_" + name, v.shape, mybir.dt.from_np(v.dtype), kind="ExternalInput").ap()
            for name, v in arrays.items()}
    out = nc.dram_tensor("out_x", (1, T, D), mybir.dt.float32, kind="ExternalOutput").ap()
    build(nc, args, out)
    r = run_bass_kernel_spmd(nc, [{"in_" + name: v for name, v in arrays.items()}], core_ids=[0])
    return r.results[0]["out_x"]
```

```python
import numpy as np

import concourse.bass as bass
from concourse import mybir
from contextlib import ExitStack

P = 128
D = 1024
KT = D // P
T = 256
TT = T // P
CH = 64
NCH = T // CH
NH = 4
HV = 256
DK = NH * P
RANK = 16
POOLG = 4
WINDOWS = (2, 4, 8, 16)
NE, NG, EG = 32, 4, 8
DE = 512
FF = 4096
SLAB = 4096
HD = 64
MOBA_H, DIL_H, DIL_SLOTS = 16, 12, 4
DIL = ((128, 1), (512, 4), (2048, 16))
EPS, LN_EPS = 1e-6, 1e-5
ALPHA = 4.0 ** 0.25
GATE_NORM = 16.0
NEG = -1e30
SLOTS = 32
CAP = SLOTS
SC_W = 384


def constants():
    s, t = np.arange(P)[:, None], np.arange(P)[None, :]
    chunk = (s // CH) == (t // CH)
    inv = 1.0 / GATE_NORM
    parts = {
        "ident": s == t,
        "ones": np.ones((P, P)),
        "cum_f": (chunk & (s <= t)) * inv, "cum_b": (chunk & (s >= t)) * inv,
        "rem_f": (chunk & (s > t)) * inv, "rem_b": (chunk & (s < t)) * inv,
        "suf": (s > t) * inv, "pre": (s < t) * inv, "all": np.full((P, P), inv),
    }
    for g, w in enumerate(WINDOWS):
        lo = np.clip(t % CH - w // 2, 0, CH)
        hi = np.clip(t % CH + w // 2, 0, CH)
        inside = chunk & (s % CH >= lo) & (s % CH < hi)
        parts[f"pool{g}"] = inside / (hi - lo) - (s == t)
    half = HD // 2
    rot = np.zeros((P, P))
    for i in range(P):
        if i % HD < half:
            rot[i + half, i] = -1.0
        else:
            rot[i - half, i] = 1.0
    parts["rot"] = rot
    freq = (1.0 / (10000.0 ** (np.arange(0, HD, 2, dtype=np.float32) / HD))).astype(np.float32)
    ang = np.arange(T, dtype=np.float32)[:, None] * freq[None, :]
    parts["cos"] = np.tile(np.cos(ang).astype(np.float32).T, (4, 1))
    parts["sin"] = np.tile(np.sin(ang).astype(np.float32).T, (4, 1))
    parts["sel"] = (s[:, :1] % 32 == np.arange(2)[None, :]) * 1.0
    parts["sel"] = np.broadcast_to(parts["sel"], (P, 2))
    parts["slot"] = np.broadcast_to(t % SLOTS, (P, P))
    parts["fold"] = (s % SLOTS) == (t % SLOTS)
    parts["zero"] = np.zeros((P, P))
    parts["desc4"] = np.broadcast_to(np.arange(4, 0, -1.0), (P, 4))
    parts["desc8"] = np.broadcast_to(np.arange(8, 0, -1.0), (P, 8))
    at, cols, n = {}, [], 0
    for name, a in parts.items():
        a = np.asarray(a, np.float32)
        at[name] = (n, a.shape[1])
        cols.append(a)
        n += a.shape[1]
    return at, np.ascontiguousarray(np.concatenate(cols, 1), np.float32)


def score_masks():
    out = []
    for span, dil in ((T, 1),) + tuple((w // d, d) for w, d in DIL):
        q, k = np.arange(T)[:, None], np.arange(T)[None, :]
        dist = q - k
        ok = (dist >= 0) & (dist % dil == 0) & (dist // dil <= span)
        m = np.where(ok, 0.0, NEG).astype(np.float32)
        out.append(np.concatenate([m[:P, :P], m[P:, :]], 1))
    return np.ascontiguousarray(np.stack(out, 1), np.float32)


CONST_AT, _ = constants()


VEC_ROWS = (("c", KT), ("c_ctx", KT), ("b_mod", 6 * KT), ("norm1_g", KT), ("norm2_g", KT),
            ("final_norm_g", KT), ("pool_scale", POOLG), ("gla_onorm_g", HV // P))
LN_ROWS = (("ln_mix_g_2", 2 * KT), ("ln_mix_b_2", 2 * KT), ("ln_mlp_g_2", 2 * KT), ("ln_mlp_b_2", 2 * KT))
COL, _n = {}, 0
for _name, _k in VEC_ROWS + LN_ROWS:
    COL[_name] = (_n, _k)
    _n += _k
NVEC = sum(k for _, k in VEC_ROWS)
NLN = sum(k for _, k in LN_ROWS)

SETS = ([(h,) for h in range(MOBA_H)], [tuple(j + DIL_SLOTS * g for g in range(3)) for j in range(DIL_SLOTS)])


EXPERTS_PER_TURN = 4
TURNS = NE // EXPERTS_PER_TURN
TURN = [("x", 0, "A"), ("x", 1, "V"), ("w", 0, "A"), ("w", 1, "V")]
TURN += [(kind, j, o) for j in range(EXPERTS_PER_TURN)
         for kind, o in (("up1", "A"), ("up3", "V"), ("t1", "A"), ("t3", "V"), ("down0", "A"), ("down1", "V"))]
TURN_AT = {(kind, j): n for n, (kind, j, _) in enumerate(TURN)}


def slab_plan():
    order = [("mod", s) for s in range(4)]
    order += [("w_in", 2), ("w_in", 3), ("w_in", 4), ("w_in", 1), ("w_in", 0), ("w_in", 5), ("w_in", 6)]
    order += [("w_in", s) for s in range(7, 11)]
    order += [("mod", s) for s in range(4, 12)]
    order += [("pool_br", 0), ("gla_br", 0), ("gla_br", 1), ("w_o", 0), ("w_o", 1)]
    order += [("moe", s) for s in range(3 * NE)]
    for l in range(2):
        order += [(f"qkv{l}", s) for s in range(6 if l == 0 else 5)]
        order += [(f"proj{l}", s) for s in range(2)]
        order += [(f"ff_in{l}", s) for s in range(FF // 512)]
        order += [(f"ff_out{l}", s) for s in range(FF // 512)]
    return {key: n for n, key in enumerate(order)}


def bank_plan():
    order = [("vectors", 0, "V")]
    order += [("x_tiles", i, "A") for i in range(4)] + [("c_tiles", i, "V") for i in range(4)]
    for s in range(4):
        order += [("mod_rows", s, "A"), ("mod_cols", s, "V")]
    order += [("norm", 0, "A"), ("norm", 1, "A")]
    order += [("lr", i, "A") for i in range(2)]
    order += [("z", i, "V") for i in range(8)]
    order += [("cum", i, "A") for i in range(4)]
    order += [("remx", i, "A") for i in range(4)]
    order += [("remc", i, "A") for i in range(4)]
    order += [("kT", i, "V") for i in range(2)] + [("kc", i, "V") for i in range(2)] + [("ktok", i, "V") for i in range(2)]
    for s in range(2):
        order += [("v", 4 * s + i, "A") for i in range(4)]
    order += [("qT", i, "V") for i in range(2)]
    for h in range(NH):
        order += [("s0", h, "A"), ("sT", h, "V")]
        order += [("kv", (h, n, d), "V") for n in range(NCH - 1) for d in range(2)]
        order += [("o", h, "A")]
    order += [("u", i, "A") for i in range(2)] + [("pool", i, "V") for i in range(2)] + [("y1", i, "V") for i in range(2)]
    order += [("g", i, "A") for i in range(4)]
    order += [("oT", i, "V") for i in range(4)]
    order += [("gate", i, "A") for i in range(8)]
    for s in range(4, 12):
        order += [("mod_rows", s, "A"), ("mod_cols", s, "V")]
    order += [("ypool", i, "V") for i in range(4)]
    order += [("ygla", i, "V") for i in range(4)]
    order += [("mix", i, "V") for i in range(4)]
    order += [("norm", 2, "A")]
    order += [("router", 0, "V")]
    order += [("ttok", i, "A") for i in range(4)]
    order += [("rank", 0, "V")]
    order += [("moe", (turn, kind, j), o) for turn in range(TURNS) for kind, j, o in TURN]
    order += [("norm", 3, "A")]
    for l in range(2):
        nt = 8 if l == 0 else 6
        order += [(f"qk{l}", i, "A") for i in range(nt)]
        order += [(f"rot{l}", i, "V") for i in range(nt)]
        order += [(f"val{l}", i, "A") for i in range(4)]
        sets = SETS[l]
        order += [(f"sc{l}", (0, j), "V") for j in range(len(sets[0]))]
        for i in range(len(sets)):
            if i + 1 < len(sets):
                order += [(f"sc{l}", (i + 1, j), "V") for j in range(len(sets[i]))]
            for j in range(len(sets[i])):
                order += [(f"pt{l}", (i, j), "A")]
            for j in range(len(sets[i])):
                order += [(f"pv{l}", (i, j), "A")]
        order += [(f"proj{l}", i, "V") for i in range(4)]
        order += [("mean", 2 * l, "V"), ("norm", 4 + 2 * l, "A")]
        order += [(f"ff{l}", i, "A") for i in range(FF // 256)]
        order += [("mean", 2 * l + 1, "V"), ("norm", 5 + 2 * l, "A")]
    order += [("out", i, "A") for i in range(4)]
    return order


SLAB_AT = slab_plan()
_ORDER = bank_plan()
SLABS = list(SLAB_AT)
BANK_AT = {(name, i): n for n, (name, i, _) in enumerate(_ORDER)}
OWNER = [o for _, _, o in _ORDER]


def build(nc, a, out):
    F32 = mybir.dt.float32
    U32 = mybir.dt.uint32
    ALU = mybir.AluOpType
    ACT = mybir.ActivationFunctionType
    AX = mybir.AxisListType

    ctx = ExitStack()
    with ctx:
        def sem(name):
            return ctx.enter_context(nc.semaphore(name))

        def sb(name, shape):
            return ctx.enter_context(nc.sbuf_tensor(name, shape, F32))

        NC = sum(w for _, w in CONST_AT.values())
        const = sb("const", [P, NC])

        def C(name):
            o, w = CONST_AT[name]
            return const[:, o:o + w]

        ident, ones = C("ident"), C("ones")
        K1 = 1024
        ARENA = 45 * K1
        arena = sb("arena", [P, ARENA])

        def at(o, *dims):
            n = int(np.prod(dims))
            assert o + n <= ARENA
            names = " ".join(f"x{i}" for i in range(len(dims)))
            v = arena[:, o:o + n]
            if len(dims) == 1:
                return v
            return v.rearrange(f"p ({names}) -> p {names}", **{f"x{i}": d for i, d in enumerate(dims)})

        RING = 4
        slot = [at(SLAB * i, SLAB) for i in range(RING)]
        xT = at(16 * K1, KT, T)
        hT = at(18 * K1, KT, T)
        sq = at(20 * K1, KT, T)
        cT = at(22 * K1, KT, T)
        L = at(24 * K1, 8, DK)
        S = at(24 * K1, 2, NCH, HV)
        sTm = at(26 * K1, 4, P)
        y1 = at(27 * K1, POOLG, T)
        dec = at(28 * K1, 2, 2, NH, T)
        xtok = at(28 * K1, TT, D)
        ctok = at(30 * K1, TT, D)
        gates = at(28 * K1, 2 * KT, T)
        remx = at(32 * K1, 2, TT, DK)
        remc = at(34 * K1, 2, TT, DK)
        ktok = at(36 * K1, TT, DK)
        kT = at(37 * K1, NH, T)
        vx = at(38 * K1, TT, D)
        vc = at(40 * K1, TT, D)
        gT = at(40 * K1, KT, T)
        otok = at(42 * K1, TT, D)
        utok = at(22 * K1, TT, DK)
        pooled = at(23 * K1, POOLG, T)
        mod_row = at(44 * K1, 2, 512)
        az = at(20 * K1, DK)
        ez = at(20 * K1 + DK, DK)
        ttok = at(22 * K1, TT, D)
        o_ = 24 * K1
        pick = at(o_, TT, EXPERTS_PER_TURN * SLOTS)
        put = at(o_ + 256, EXPERTS_PER_TURN, TT, P)
        putT = at(o_ + 1280, EXPERTS_PER_TURN, T)
        xs = at(o_ + 2304, KT, EXPERTS_PER_TURN, SLOTS)
        h1 = at(o_ + 3328, DE)
        h3 = at(o_ + 3840, DE)
        s1 = at(o_ + 4352, 4, SLOTS)
        hidT = at(o_ + 4480, 4, SLOTS)
        ys = at(o_ + 4608, D)
        dslab = [at((30 + 4 * j) * K1, SLAB) for j in range(3)]
        dhid = at(42 * K1, 4, T)
        dsilu = at(43 * K1, 4, T)
        dcol = at(44 * K1, TT, P)
        dcomb = at(44 * K1 + 256, T)
        qk_raw = at(22 * K1, 16, T)
        qk = at(26 * K1, 16, T)
        vt = at(30 * K1, TT, D)
        attT = at(32 * K1, KT, T)
        sc = at(34 * K1, 2, 3, SC_W)
        pT = at(37 * K1, 3, SC_W)
        masks = at(39 * K1, 4, SC_W)
        hff = at(22 * K1, FF // P, T)

        w_lr = sb("w_lr", [P, KT, 2 * RANK])
        w_pool = sb("w_pool", [P, POOLG, P])
        w_rt = sb("w_rt", [P, KT, NG + NE])
        a2 = at(42 * K1, 2, DK)[0:RANK]
        ab = at(43 * K1, 2, DK)[0:1]
        rb = sb("rb", [1, NG + NE])
        rows = sb("rows", [P, 2, P])
        cols = sb("cols", [P, NVEC + NLN])
        scol = sb("scol", [P, KT, 32])
        mod = sb("mod", [P, 6 * KT, 2])
        scale1 = sb("scale1", [P, 3, KT])
        std = sb("std", [P, T])
        lrT = at(36 * K1, 4, T)[0:RANK]
        decay = sb("decay", [P, 2, NH, NCH])
        oss = sb("oss", [P, TT, NH])
        orstd = sb("orstd", [P, TT, NH])
        oeps = sb("eps", [P, 2])
        lg = sb("lg", [P, TT, NG + NE])
        r4 = sb("r4", [P, 4, TT, NG])
        r8 = sb("r8", [P, 6, TT, EG])
        r1 = sb("r1", [P, 12, TT])
        r32 = sb("r32", [P, TT, NG, EG])
        comb = sb("comb", [P, TT, NE])
        chosen = sb("chosen", [P, TT, NE])
        pos = sb("pos", [P, TT, NE])
        over = sb("over", [P, TT, NE])
        n_over = sb("n_over", [P, 2])
        flag = ctx.enter_context(nc.sbuf_tensor("flag", [P, 1], mybir.dt.int32))
        mx = sb("mx", [P, 2, TT])
        ssum = sb("ssum", [P, 2, TT])
        rsum = sb("rsum", [P, 2, TT])

        RB = 4
        OPENED = 2
        ring = ctx.enter_context(nc.psum_tensor("ring", [P, RB, 512], F32))
        acc = ctx.enter_context(nc.psum_tensor("acc", [P, KT, T], F32))

        consts_in = sem("consts_in")
        smalls_in = sem("smalls_in")
        tokens_in = sem("tokens_in")
        masks_in = sem("masks_in")
        landed = [sem(f"slab_landed{i}") for i in range(RING)]
        used = sem("slab_used")
        bank_full = sem("bank_full")
        freed = {"V": sem("bank_freed_by_vector"), "A": sem("bank_freed_by_scalar")}
        d_landed = sem("dense_slabs_landed")
        d_used = sem("dense_expert_used")
        d_full = sem("dense_bank_full")
        d_act = sem("dense_scalar_done")
        d_vec = sem("dense_hidden_ready")
        v_step = sem("vector_step")
        a_step = sem("scalar_step")
        names = "chosen_ready flag_ready pick_ready put_ready dcol_ready dsilu_scaled ff_ready scol_zero scol_ready sq_ready rstd_read h_ready ez_ready ostd_ready on_ready z_ready resid_ready lg_diff rexp_ready comb_ready rot_ready max_ready exp_ready p_ready out_stored eps_ready".split()
        G = {n: sem(n) for n in names}

        def bank_of(name, i):
            return ring[:, BANK_AT[name, i] % RB, :]

        def freed_by(g):
            return freed[OWNER[g]], sum(o == OWNER[g] for o in OWNER[:g + 1])

        def moved(eng, name, i):
            eng.wait_ge(*freed_by(BANK_AT[name, i]))

        m0 = BANK_AT["moe", (0, "x", 0)]

        def turn_bank(kind, j):
            return ring[:, (m0 + TURN_AT[kind, j]) % RB, :]

        def turn_full(it, kind, j):
            return it * len(TURN) + (m0 + TURN_AT[kind, j] + 1)

        def turn_moved(eng, it, kind, j, back=0):
            g = TURN_AT[kind, j]
            o = TURN[g][2]
            per = sum(x[2] == o for x in TURN)
            before = sum(x == o for x in OWNER[:m0]) - back * per + sum(x[2] == o for x in TURN[:g + 1])
            eng.wait_ge(freed[o], it * per + before)

        def d_bank(n):
            return ring[:, n % RB, :]

        def last_pt(k):
            l, i = (0, k) if k < len(SETS[0]) else (1, k - len(SETS[0]))
            return f"pt{l}", (i, len(SETS[l][i]) - 1)

        def slab_freed(n):
            name, s = SLABS[n]
            if name == "moe":
                e, j = divmod(s, 3)
                turn, e = divmod(e, EXPERTS_PER_TURN)
                return bank_full, BANK_AT["moe", (turn, ("up1", "up3", "down1")[j], e)] + 1
            if name[:-1] == "ff_out":
                return used, OPENED + NE + (FF // 512) * int(name[-1]) + s + 1
            if name == "w_in":
                bank_use = {0: ("u", 1), 1: ("qT", 1), 2: ("kc", 1), 3: ("v", 3), 4: ("v", 7), 5: ("g", 1), 6: ("g", 3)}.get(s)
                bank_use = bank_use or ("gate", 2 * (s - 7) + 1)
            elif name == "mod":
                bank_use = ("mod_rows", s)
            elif name[:-1] == "qkv":
                nt = 8 if name[-1] == "0" else 6
                bank_use = ("qk" + name[-1], 2 * s + 1) if s < nt // 2 else ("val" + name[-1], 3)
            elif name[:-1] == "ff_in":
                bank_use = ("ff" + name[-1], 2 * s + 1)
            elif name == "pool_br":
                bank_use = ("ypool", 3)
            else:
                bank_use = ({"gla_br": "ygla", "w_o": "mix"}.get(name, name), 2 * s + 1)
            return bank_full, BANK_AT[bank_use] + 1

        def w_in(s):
            return a["w_in"][0][:, 512 * s:512 * s + 512].rearrange("(k p) n -> p k n", p=P)

        def slab_source(name, s):
            if name == "mod":
                return a["w_mod"][0][:, 512 * s:512 * s + 512].rearrange("(k p) n -> p k n", p=P)
            if name == "w_in":
                return w_in(s)
            if name == "pool_br":
                return a["w_pool_br"][0].rearrange("(k p) n -> p k n", p=P)
            if name in ("gla_br", "w_o"):
                w = a["w_gla_br" if name == "gla_br" else "w_o"][0]
                return w[:, 512 * s:512 * s + 512].rearrange("(k p) n -> p k n", p=P)
            l = int(name[-1])
            if name[:-1] == "qkv":
                w = a[("moba", "dil")[l] + "_w_qkv_2"][0]
                return w[:, 512 * s:min(512 * s + 512, w.shape[1])].rearrange("(k p) n -> p k n", p=P)
            if name[:-1] == "proj":
                w = a[("moba", "dil")[l] + "_w_o_2"][0]
                return w[:, 512 * s:512 * s + 512].rearrange("(k p) n -> p k n", p=P)
            if name[:-1] == "ff_in":
                return a["mlp_w_in_2"][l][:, 512 * s:512 * s + 512].rearrange("(k p) n -> p k n", p=P)
            return a["mlp_w_out_2"][l][512 * s:512 * s + 512, :].rearrange("(k p) n -> p k n", p=P)

        def view(n, k, w):
            return slot[n % RING][:, 0:k * w].rearrange("p (k n) -> p k n", k=k)

        block = ctx.enter_context(nc.Block())

        @block.sync
        def _(sp):
            def load(n, src):
                if n >= RING:
                    sp.wait_ge(*slab_freed(n - RING))
                sp.dma_start(view(n, src.shape[1], src.shape[2]), src).then_inc(landed[n % RING], 16)

            def expert_source(j, e):
                w = a[("moe_w1", "moe_w3", "moe_w2")[j]][0]
                return w[bass.ds(e, 1), :, :].rearrange("e (k p) n -> p (e k) n", p=P)

            moe0, n_moe, per = SLAB_AT["moe", 0], 3 * NE, 12
            for (name, s), n in SLAB_AT.items():
                if (name, s) == ("qkv0", RING):
                    sp.wait_ge(G["flag_ready"], 1)
                    with sp.If(sp.value_load(flag[0:1, 0:1]) > 0):
                        with sp.Fori(0, NE) as e:
                            sp.wait_ge(d_used, e + 1)
                            for j in range(3):
                                src = expert_source(j, e)
                                sp.dma_start(dslab[j].rearrange("p (k n) -> p k n", k=src.shape[1]), src).then_inc(d_landed, 16)
                if name != "moe":
                    load(n, slab_source(name, s))
                elif s < RING or s >= n_moe - per + RING:
                    load(n, expert_source(s % 3, s // 3))
                elif s == RING:
                    with sp.Fori(0, NE // 4 - 1) as it:
                        for j in range(RING, RING + per):
                            what, before = slab_freed(moe0 + j - RING)
                            sp.wait_ge(what, it * len(TURN) + before)
                            src = expert_source(j % 3, it * 4 + j // 3)
                            sp.dma_start(view(moe0 + j, src.shape[1], src.shape[2]), src).then_inc(landed[(moe0 + j) % RING], 16)
            for tt in range(TT):
                moved(sp, "out", 2 * tt + 1)
                sp.dma_start(out[0][tt * P:(tt + 1) * P, :], xtok[:, tt, :]).then_inc(G["out_stored"], 16)
            sp.wait_ge(G["out_stored"], 16 * TT)

        SMALLS = []

        @block.scalar
        def _(act):
            n_step = [0]

            def link(ins):
                n_step[0] += 1
                ins.then_inc(a_step, 1)
                act.wait_ge(a_step, n_step[0])

            def take(name, i):
                act.wait_ge(bank_full, BANK_AT[name, i] + 1)
                return bank_of(name, i)

            def free(ins):
                ins.then_inc(freed["A"], 1)

            act.dma_start(const[:, :], a["consts"]).then_inc(consts_in, 16)

            def small(dst, src):
                act.dma_start(dst, src).then_inc(smalls_in, 16)
                SMALLS.append(1)

            for table, r, base in ((VEC_ROWS, 0, 0), (LN_ROWS, 1, NVEC)):
                for name, n in table:
                    o = COL[name][0] - base
                    src = a[name]
                    while len(src.shape) > 1 and src.shape[0] == 1:
                        src = src[0]
                    if len(src.shape) == 2:
                        src = src.rearrange("l (r p) -> (l r) p", p=P)
                    else:
                        src = src.rearrange("(r p) -> r p", p=P)
                    small(rows[o:o + n, r, :], src)
            for tt in range(TT):
                act.dma_start(xtok[:, tt, :], a["x"][0][tt * P:(tt + 1) * P, :]).then_inc(tokens_in, 16)
                act.dma_start(ctok[:, tt, :], a["ctx"][0][tt * P:(tt + 1) * P, :]).then_inc(tokens_in, 16)
            small(w_lr[:, :, :], a["w_in"][0][:, 5632:5664].rearrange("(k p) n -> p k n", p=P))
            small(w_pool[:, :, :], a["pool_w"][0].rearrange("g c e -> c g e"))
            small(w_rt[:, :, 0:NG], a["router_grp_w"][0].rearrange("(k p) n -> p k n", p=P))
            small(w_rt[:, :, NG:], a["router_exp_w"][0].rearrange("(k p) n -> p k n", p=P))
            for d, name in enumerate("fb"):
                small(a2[:, d, :], a["gla_a2_" + name][0])
                small(ab[0:1, d, :], a["gla_ab_" + name])
            small(rb[0:1, 0:NG], a["router_grp_b"])
            small(rb[0:1, NG:], a["router_exp_b"])

            def square(src, k):
                act.activation(sq, src, ACT.Square).then_inc(G["sq_ready"], 1)

            def norm_std(k, eps):
                b = take("norm", k)
                ins = act.activation(std[:, :], b[:, 0:T], ACT.Sqrt, bias=oeps[:, eps:eps + 1], scale=1.0 / D)
                ins.then_inc(freed["A"], 1)

            def mod_rows(s):
                b = take("mod_rows", s)
                ins = act.activation(mod_row[:, s % 2, :], b, ACT.Copy)
                ins.then_inc(freed["A"], 1)

            moved(act, "vectors", 0)
            act.wait_ge(G["scol_zero"], 1)
            act.activation(scol[:, :, 0:2], cols[:, 0:2 * KT].rearrange("p (r k) -> p k r", r=2), ACT.Silu).then_inc(G["scol_ready"], 1)
            for i in range(4):
                tt, q = divmod(i, 2)
                b = take("x_tiles", i).rearrange("p (k t) -> p k t", k=4)
                ins = act.activation(xT[:, 4 * q:4 * q + 4, tt * P:(tt + 1) * P], b, ACT.Copy)
                ins.then_inc(freed["A"], 1)
            for s in range(4):
                mod_rows(s)
            act.wait_ge(G["eps_ready"], 1)
            moved(act, "c_tiles", 3)
            square(cT, 0)
            norm_std(0, 0)
            act.wait_ge(G["rstd_read"], 1)
            moved(act, "x_tiles", 3)
            square(xT, 1)
            norm_std(1, 0)
            for i in range(2):
                b = take("lr", i)
                ins = act.activation(lrT[:, 2 * i:2 * i + 2, :], b[0:RANK, :].rearrange("p (d t) -> p d t", d=2), ACT.Copy)
                ins.then_inc(freed["A"], 1)
            for i in range(8):
                b = take("z", i)
                if i:
                    moved(act, "z", i - 1)
                link(act.activation(az, b, ACT.Abs))
                link(act.activation(ez, az, ACT.Exp, scale=-1.0))
                act.activation(ez, ez, ACT.Ln, bias=1.0).then_inc(G["ez_ready"], 1)
            for i in range(4):
                d, hp = divmod(i, 2)
                b = take("cum", i).rearrange("p (h t) -> p h t", h=2)
                act.activation(dec[:, 0, d, 2 * hp:2 * hp + 2, :], b, ACT.Exp)
                ins = act.activation(dec[:, 1, d, 2 * hp:2 * hp + 2, :], b, ACT.Exp, scale=-1.0)
                ins.then_inc(freed["A"], 1)
            for name, dst in (("remx", remx), ("remc", remc)):
                for i in range(4):
                    d, tt = divmod(i, 2)
                    ins = act.activation(dst[:, d, tt, :], take(name, i), ACT.Exp)
                    ins.then_inc(freed["A"], 1)
            for s in range(2):
                for i in range(4):
                    dst = (vx, vc)[i // 2]
                    ins = act.activation(dst[:, i % 2, 512 * s:512 * s + 512], take("v", 4 * s + i), ACT.Copy)
                    ins.then_inc(freed["A"], 1)
            for h in range(NH):
                b = take("s0", h).rearrange("p (d v) -> p d v", d=2)
                if h:
                    act.wait_ge(bank_full, BANK_AT["o", h - 1] + 1)
                act.activation(S[:, 0, 0, :], b[:, 0, :], ACT.Copy)
                ins = act.activation(S[:, 1, NCH - 1, :], b[:, 1, :], ACT.Copy)
                ins.then_inc(freed["A"], 1)
                b = take("o", h).rearrange("p (a v) -> p a v", a=TT)
                ins = act.activation(otok[:, :, h * HV:(h + 1) * HV], b, ACT.Copy)
                ins.then_inc(freed["A"], 1)
                moved(act, "o", h)
                for tt in range(TT):
                    link(act.activation(sq[:, 0, :], otok[:, tt, h * HV:(h + 1) * HV], ACT.Square, accum_out=oss[:, tt, h:h + 1]))
            act.activation(orstd[:, :, :], oss[:, :, :], ACT.Sqrt, bias=oeps[:, 0:1], scale=1.0 / HV).then_inc(G["ostd_ready"], 1)
            for i in range(2):
                ins = act.activation(utok[:, i, :], take("u", i), ACT.Copy)
                ins.then_inc(freed["A"], 1)
            for i in range(4):
                ins = act.activation(gT[:, 2 * i:2 * i + 2, :], take("g", i).rearrange("p (k t) -> p k t", k=2), ACT.Silu)
                ins.then_inc(freed["A"], 1)
            for i in range(8):
                ins = act.activation(gates[:, 2 * i:2 * i + 2, :], take("gate", i).rearrange("p (k t) -> p k t", k=2), ACT.Sigmoid)
                ins.then_inc(freed["A"], 1)
            for s in range(4, 12):
                mod_rows(s)
            act.wait_ge(G["resid_ready"], 1)
            square(xT, 2)
            norm_std(2, 0)
            act.wait_ge(G["lg_diff"], 1)
            act.activation(r4[:, 1, :, :], r4[:, 0, :, :], ACT.Exp).then_inc(G["rexp_ready"], 1)
            act.wait_ge(G["lg_diff"], 2)
            act.activation(r1[:, 6, :], r1[:, 5, :], ACT.Exp).then_inc(G["rexp_ready"], 1)
            for i in range(4):
                tt, q = divmod(i, 2)
                act.activation(ttok[:, tt, 512 * q:512 * q + 512], take("ttok", i), ACT.Copy).then_inc(freed["A"], 1)
            with act.Fori(0, TURNS) as it:
                def out_of(kind, j, dst, b, func=ACT.Copy):
                    act.wait_ge(bank_full, turn_full(it, kind, j))
                    act.activation(dst, b, func).then_inc(freed["A"], 1)

                out_of("x", 0, xs[:, 0:4, :, :], turn_bank("x", 0).rearrange("p (k j s) -> p k j s", k=4, j=EXPERTS_PER_TURN))
                out_of("w", 0, putT[:, 0:2, :], turn_bank("w", 0).rearrange("p (j t) -> p j t", j=2))
                for j in range(EXPERTS_PER_TURN):
                    out_of("up1", j, h1, turn_bank("up1", j))
                    out_of("t1", j, s1, turn_bank("t1", j).rearrange("p (k s) -> p k s", k=4)[:, :, 0:SLOTS], ACT.Silu)
                    out_of("down0", j, ys[:, 0:512], turn_bank("down0", j))
            act.wait_ge(G["flag_ready"], 1)
            with act.If(act.value_load(flag[0:1, 0:1]) > 0):
                with act.Fori(0, NE) as e:
                    act.wait_ge(d_full, e * 5 + 1)
                    act.activation(dcomb, d_bank(0)[:, 0:T], ACT.Copy).then_inc(d_act, 1)
                    for i in range(2):
                        act.wait_ge(d_full, e * 5 + (2 + 2 * i))
                        act.activation(dsilu[:, 2 * i:2 * i + 2, :], d_bank(1 + 2 * i).rearrange("p (k t) -> p k t", k=2), ACT.Silu).then_inc(d_act, 1)
            act.wait_ge(G["resid_ready"], 2)
            square(xT, 3)
            norm_std(3, 0)
            act.dma_start(masks, a["masks"]).then_inc(masks_in, 16)
            hq = [0]
            for l in range(2):
                nt = 8 if l == 0 else 6
                for i in range(nt):
                    ins = act.activation(qk_raw[:, 2 * i:2 * i + 2, :], take(f"qk{l}", i).rearrange("p (k t) -> p k t", k=2), ACT.Copy)
                    ins.then_inc(freed["A"], 1)
                for i in range(4):
                    tt, s = i // 2, i % 2
                    w = 512 if l == 0 or s == 0 else 256
                    ins = act.activation(vt[:, tt, 512 * s:512 * s + w], take(f"val{l}", i)[:, 0:w], ACT.Copy)
                    ins.then_inc(freed["A"], 1)
                sets = SETS[l]
                m0_ = 0 if l == 0 else len(SETS[0])

                def exps(i):
                    k = m0_ + i
                    act.wait_ge(G["max_ready"], k + 1)
                    n = len(sets[i])
                    s_ = sc[:, k % 2, 0:n, :]
                    act.activation(s_[:, :, 0:P], s_[:, :, 0:P], ACT.Exp, scale=HD ** -0.5, bias=mx[:, k % 2, 0:1],
                                   accum_out=ssum[:, k % 2, 0:1])
                    act.activation(s_[:, :, P:SC_W], s_[:, :, P:SC_W], ACT.Exp, scale=HD ** -0.5, bias=mx[:, k % 2, 1:2],
                                   accum_out=ssum[:, k % 2, 1:2]).then_inc(G["exp_ready"], 1)

                exps(0)
                for i in range(len(sets)):
                    if i + 1 < len(sets):
                        exps(i + 1)
                    for j in range(len(sets[i])):
                        ins = act.activation(pT[:, j, :], take(f"pt{l}", (i, j))[:, 0:SC_W], ACT.Copy)
                        ins.then_inc(freed["A"], 1)
                    for j, h in enumerate(sets[i]):
                        o = HD * (h % 2)
                        b = take(f"pv{l}", (i, j))
                        ins = act.activation(attT[o:o + HD, h // 2, :], b[o:o + HD, 0:T], ACT.Copy)
                        ins.then_inc(freed["A"], 1)
                for half in range(2):
                    moved(act, "mean", 2 * l + half)
                    square(xT, 0)
                    norm_std(4 + 2 * l + half, 1)
                    for i in range(FF // 256 if half == 0 else 0):
                        b = take(f"ff{l}", i).rearrange("p (k t) -> p k t", k=2)
                        act.activation(hff[:, 2 * i:2 * i + 2, :], b, ACT.Relu).then_inc(freed["A"], 1)
            for i in range(4):
                tt, q = divmod(i, 2)
                ins = act.activation(xtok[:, tt, 512 * q:512 * q + 512], take("out", i), ACT.Copy)
                ins.then_inc(freed["A"], 1)

        NSM = len(SMALLS)

        @block.vector
        def _(dve):
            n_step = [0]

            def link(ins):
                n_step[0] += 1
                ins.then_inc(v_step, 1)
                dve.wait_ge(v_step, n_step[0])

            def take(name, i):
                dve.wait_ge(bank_full, BANK_AT[name, i] + 1)
                return bank_of(name, i)

            dve.memset(scol[:, :, :], 0.0).then_inc(G["scol_zero"], 1)
            dve.memset(oeps[:, 0:1], EPS)
            dve.memset(oeps[:, 1:2], LN_EPS).then_inc(G["eps_ready"], 1)
            b = take("vectors", 0)
            ins = dve.tensor_copy(cols[:, :], b[:, 0:NVEC + NLN])
            ins.then_inc(freed["V"], 1)

            def col(name, k, n=1):
                o = COL[name][0] + k
                return cols[:, o:o + n]

            for i in range(4):
                tt, q = divmod(i, 2)
                b = take("c_tiles", i).rearrange("p (k t) -> p k t", k=4)
                ins = dve.tensor_copy(cT[:, 4 * q:4 * q + 4, tt * P:(tt + 1) * P], b)
                ins.then_inc(freed["V"], 1)

            moved(dve, "vectors", 0)

            def mod_cols(s):
                b = take("mod_cols", s)
                ins = dve.tensor_tensor(mod[:, 4 * s:4 * s + 4, :], b[:, 0:8].rearrange("p (k r) -> p k r", r=2),
                                        col("b_mod", 4 * s, 4).unsqueeze(2).to_broadcast([P, 4, 2]), ALU.add)
                ins.then_inc(freed["V"], 1)

            for s in range(4):
                mod_cols(s)
            moved(dve, "mod_cols", 3)

            def gain(k, name, chunk, r):
                dve.scalar_tensor_tensor(scale1[:, k, :], mod[:, KT * chunk:KT * chunk + KT, r], 1.0, col(name, 0, KT),
                                         ALU.add, ALU.mult).then_inc(v_step, 1)
                n_step[0] += 1

            gain(0, "norm1_g", 1, 0)
            gain(1, "norm1_g", 1, 1)
            dve.wait_ge(v_step, n_step[0])

            def normed(k, src, dst, scale, shift):
                moved(dve, "norm", k)
                link(dve.reciprocal(std[:, :], std[:, :]))
                link(dve.tensor_tensor(sq, src, std[:, :].unsqueeze(1).to_broadcast([P, KT, T]), ALU.mult))
                for kt in range(KT):
                    if shift is None:
                        ins = dve.tensor_scalar(dst[:, kt, :], sq[:, kt, :], scale(kt), None, ALU.mult)
                    else:
                        ins = dve.tensor_scalar(dst[:, kt, :], sq[:, kt, :], scale(kt), shift(kt), ALU.mult, ALU.add)
                    ins.then_inc(G["h_ready"], 1)
                dve.wait_ge(G["h_ready"], KT * (k + 1))

            normed(0, cT, cT, lambda kt: scale1[:, 1, kt:kt + 1], lambda kt: mod[:, kt, 1:2])
            dve.sem_inc(G["rstd_read"], 1)
            normed(1, xT, hT, lambda kt: scale1[:, 0, kt:kt + 1], lambda kt: mod[:, kt, 0:1])

            for i in range(8):
                b = take("z", i)
                dve.wait_ge(G["ez_ready"], i + 1)
                ins = dve.scalar_tensor_tensor(L[:, i, :], b, 0.0, ez, ALU.min, ALU.subtract)
                ins.then_inc(freed["V"], 1)
            for i in range(2):
                ins = dve.tensor_copy(kT[:, 2 * i:2 * i + 2, :], take("kT", i).rearrange("p (h t) -> p h t", h=2))
                ins.then_inc(freed["V"], 1)
            moved(dve, "kT", 1)
            moved(dve, "cum", 3)
            for d in range(2):
                o = CH - 1 if d == 0 else 0
                dve.tensor_copy(decay[:, d, :, :], dec[:, 0, d, :, :].rearrange("p h (n t) -> p h n t", n=NCH)[:, :, :, o])
                link(dve.tensor_tensor(dec[:, 1, d, :, :], dec[:, 1, d, :, :], kT, ALU.mult))
            for i in range(2):
                b = take("kc", i)
                moved(dve, "remc", 3)
                link(dve.tensor_tensor(remc[:, 0, i, :], remc[:, 0, i, :], b, ALU.mult))
                ins = dve.tensor_tensor(remc[:, 1, i, :], remc[:, 1, i, :], b, ALU.mult)
                ins.then_inc(freed["V"], 1)
            for i in range(2):
                b = take("ktok", i)
                moved(dve, "remx", 3)
                link(dve.tensor_tensor(remx[:, 0, i, :], remx[:, 0, i, :], b, ALU.mult))
                ins = dve.tensor_tensor(remx[:, 1, i, :], remx[:, 1, i, :], b, ALU.mult)
                ins.then_inc(freed["V"], 1)
            for i in range(2):
                b = take("qT", i).rearrange("p (h t) -> p h t", h=2)
                for d in range(2):
                    v = dec[:, 0, d, 2 * i:2 * i + 2, :]
                    ins = dve.scalar_tensor_tensor(v, b, float(np.float32(P ** -0.5)), v, ALU.mult, ALU.mult)
                ins.then_inc(freed["V"], 1)
            moved(dve, "ktok", 1)
            dve.wait_ge(bank_full, BANK_AT["remc", 3] + 1)
            link(dve.memset(sTm, 0.0))
            for h in range(NH):
                b = take("sT", h).rearrange("p (c i) -> p c i", c=4)
                if h:
                    dve.wait_ge(bank_full, BANK_AT["o", h - 1] + 1)
                for c in range(4):
                    m = C("cum_f" if c < 2 else "cum_b").bitcast(U32)
                    ins = dve.copy_predicated(sTm[:, c, :], m, b[:, c, :])
                ins.then_inc(freed["V"], 1)
                moved(dve, "s0", h)
                for n in range(NCH - 1):
                    f, r = n, NCH - 1 - n
                    for d, c, to in ((0, f, f + 1), (1, r, r - 1)):
                        b = take("kv", (h, n, d))[:, 0:HV]
                        if n:
                            moved(dve, "kv", (h, n - 1, d))
                        ins = dve.scalar_tensor_tensor(S[:, d, to, :], S[:, d, c, :], decay[:, d, h, c:c + 1], b, ALU.mult, ALU.add)
                        ins.then_inc(freed["V"], 1)
            dve.wait_ge(G["ostd_ready"], 1)
            link(dve.reciprocal(orstd[:, :, :], orstd[:, :, :]))
            for tt in range(TT):
                v = otok[:, tt, :].rearrange("p (h v) -> p h v", h=NH)
                dve.tensor_tensor(v, v, orstd[:, tt, :].unsqueeze(2).to_broadcast([P, NH, HV]), ALU.mult).then_inc(G["on_ready"], 1)
            for i in range(2):
                ins = dve.tensor_copy(pooled[:, 2 * i:2 * i + 2, :], take("pool", i).rearrange("p (g t) -> p g t", g=2))
                ins.then_inc(freed["V"], 1)
            for i in range(2):
                b = take("y1", i).rearrange("p (g t) -> p g t", g=2)
                dve.tensor_scalar(y1[:, 2 * i, :], b[:, 0, :], col("pool_scale", 2 * i), None, ALU.mult)
                ins = dve.tensor_scalar(y1[:, 2 * i + 1, :], b[:, 1, :], col("pool_scale", 2 * i + 1), None, ALU.mult)
                ins.then_inc(freed["V"], 1)
            for i in range(4):
                tt, q = divmod(i, 2)
                b = take("oT", i).rearrange("p (k r t) -> p k r t", k=2, r=2)
                moved(dve, "g", 3)
                for r in range(2):
                    v = gT[:, 4 * q:4 * q + 4, tt * P:(tt + 1) * P].rearrange("p (k r) t -> p k r t", r=2)[:, :, r, :]
                    ins = dve.scalar_tensor_tensor(v, b[:, :, r, :], col("gla_onorm_g", r), v, ALU.mult, ALU.mult)
                ins.then_inc(freed["V"], 1)
            for s in range(4, 12):
                mod_cols(s)
            moved(dve, "mod_cols", 11)
            gain(2, "norm2_g", 4, 0)
            moved(dve, "gate", 7)
            for i in range(4):
                b = take("ypool", i).rearrange("p (k t) -> p k t", k=2)
                ins = dve.tensor_tensor(sq[:, 2 * i:2 * i + 2, :], b, gates[:, 2 * i:2 * i + 2, :], ALU.mult)
                ins.then_inc(freed["V"], 1)
            for i in range(4):
                b = take("ygla", i).rearrange("p (k t) -> p k t", k=2)
                v = gates[:, KT + 2 * i:KT + 2 * i + 2, :]
                ins = dve.tensor_tensor(v, b, v, ALU.mult)
                ins.then_inc(freed["V"], 1)
                moved(dve, "ygla", i)
                z = sq[:, 2 * i:2 * i + 2, :]
                dve.tensor_tensor(z, z, v, ALU.add).then_inc(G["z_ready"], 1)
            for i in range(4):
                b = take("mix", i).rearrange("p (k t) -> p k t", k=2)
                for r in range(2):
                    kt = 2 * i + r
                    ins = dve.scalar_tensor_tensor(xT[:, kt, :], b[:, r, :], mod[:, 2 * KT + kt, 0:1], xT[:, kt, :], ALU.mult, ALU.add)
                ins.then_inc(freed["V"], 1)
            moved(dve, "mix", 3)
            dve.sem_inc(G["resid_ready"], 1)
            normed(2, xT, hT, lambda kt: scale1[:, 2, kt:kt + 1], lambda kt: mod[:, 3 * KT + kt, 0:1])

            b = take("router", 0)[:, 0:TT * (NG + NE)].rearrange("p (a n) -> p a n", a=TT)
            ins = dve.tensor_copy(lg[:, :, :], b)
            ins.then_inc(freed["V"], 1)
            moved(dve, "router", 0)

            def bc(ap, n):
                return ap.unsqueeze(2).to_broadcast([P, TT, n])

            def first_max(vals, n, m, eq, key, km):
                link(dve.tensor_reduce(m, vals, AX.X, ALU.max))
                link(dve.tensor_tensor(eq, vals, bc(m, n), ALU.is_equal))
                d = C(f"desc{n}").unsqueeze(1).to_broadcast([P, TT, n])
                link(dve.tensor_tensor(key, eq, d, ALU.mult))
                link(dve.tensor_reduce(km, key, AX.X, ALU.max))
                link(dve.tensor_tensor(eq, d, bc(km, n), ALU.is_equal))

            lgg = lg[:, :, 0:NG]
            first_max(lgg, NG, r1[:, 0, :], r4[:, 2, :, :], r4[:, 3, :, :], r1[:, 1, :])
            dve.tensor_tensor(r4[:, 0, :, :], lgg, bc(r1[:, 0, :], NG), ALU.subtract).then_inc(G["lg_diff"], 1)
            grp = r4[:, 2, :, :]
            lge = lg[:, :, NG:].rearrange("p a (g e) -> p a g e", g=NG)
            for tt in range(TT):
                link(dve.tensor_tensor(r32[:, tt, :, :], lge[:, tt, :, :], grp[:, tt, :].unsqueeze(2).to_broadcast([P, NG, EG]), ALU.mult))
            ing = r8[:, 0, :, :]
            for tt in range(TT):
                link(dve.tensor_reduce(ing[:, tt, :], r32[:, tt, :, :].rearrange("p g e -> p e g"), AX.X, ALU.add))
            one, two = r8[:, 1, :, :], r8[:, 2, :, :]

            def by_group(dst, tt, in_group, then):
                dve.tensor_tensor(dst[:, tt, :].rearrange("p (g e) -> p g e", g=NG), in_group[:, tt, :].unsqueeze(1).to_broadcast([P, NG, EG]),
                                  grp[:, tt, :].unsqueeze(2).to_broadcast([P, NG, EG]), ALU.mult).then_inc(then, 1)

            first_max(ing, EG, r1[:, 2, :], one, r8[:, 3, :, :], r1[:, 3, :])
            link(dve.scalar_tensor_tensor(r8[:, 4, :, :], one, -3.0e38, ing, ALU.mult, ALU.add))
            first_max(r8[:, 4, :, :], EG, r1[:, 4, :], two, r8[:, 3, :, :], r1[:, 3, :])
            dve.tensor_tensor(r1[:, 5, :], r1[:, 4, :], r1[:, 2, :], ALU.subtract).then_inc(G["lg_diff"], 1)
            both = r8[:, 5, :, :]
            link(dve.tensor_tensor(both, one, two, ALU.add))
            link(dve.tensor_scalar(both, both, GATE_NORM, None, ALU.mult))
            for tt in range(TT):
                by_group(chosen, tt, both, G["chosen_ready"])
            dve.wait_ge(G["rexp_ready"], 2)
            link(dve.tensor_reduce(r1[:, 7, :], r4[:, 1, :, :], AX.X, ALU.add))
            link(dve.scalar_tensor_tensor(r1[:, 8, :], r1[:, 6, :], 1.0, r1[:, 7, :], ALU.add, ALU.mult))
            link(dve.reciprocal(r1[:, 9, :], r1[:, 8, :]))
            link(dve.tensor_tensor(r1[:, 10, :], r1[:, 9, :], r1[:, 6, :], ALU.mult))
            link(dve.tensor_tensor(one, one, bc(r1[:, 9, :], EG), ALU.mult))
            link(dve.tensor_tensor(two, two, bc(r1[:, 10, :], EG), ALU.mult))
            link(dve.tensor_tensor(one, one, two, ALU.add))
            for tt in range(TT):
                by_group(comb, tt, one, G["comb_ready"])
            b = take("rank", 0)
            rank = b[:, 0:TT * NE].rearrange("p (a e) -> p a e", a=TT)
            dve.wait_ge(G["chosen_ready"], 2)
            dve.wait_ge(G["comb_ready"], 2)
            link(dve.tensor_reduce(n_over[:, 0:1], b[:, TT * NE:(TT + 1) * NE], AX.X, ALU.max))
            link(dve.tensor_scalar(chosen[:, :, :], chosen[:, :, :], 1.0 / GATE_NORM, None, ALU.mult))
            ins = dve.scalar_tensor_tensor(pos[:, :, :], rank, 1.0, chosen[:, :, :], ALU.add, ALU.mult)
            ins.then_inc(freed["V"], 1)
            moved(dve, "rank", 0)
            link(dve.tensor_scalar(pos[:, :, :], pos[:, :, :], 1.0, None, ALU.subtract))
            link(dve.tensor_scalar(over[:, :, :], pos[:, :, :], float(CAP), None, ALU.is_ge))
            link(dve.scalar_tensor_tensor(pos[:, :, :], over[:, :, :], -float(2 * T), pos[:, :, :], ALU.mult, ALU.add))
            link(dve.tensor_tensor(over[:, :, :], over[:, :, :], comb[:, :, :], ALU.mult))
            dve.tensor_scalar(flag[:, :], n_over[:, 0:1], float(CAP), None, ALU.is_gt).then_inc(G["flag_ready"], 1)
            slot_row = C("slot")
            with dve.Fori(0, TURNS) as it:
                for j in range(EXPERTS_PER_TURN):
                    for tt in range(TT):
                        e_ = bass.ds(it * EXPERTS_PER_TURN + j, 1)
                        dve.tensor_scalar(pick[:, tt, SLOTS * j:SLOTS * (j + 1)], slot_row[:, 0:SLOTS], pos[:, tt, e_], None,
                                          ALU.is_equal).then_inc(G["pick_ready"], 1)
                for j in range(EXPERTS_PER_TURN):
                    for tt in range(TT):
                        e_ = bass.ds(it * EXPERTS_PER_TURN + j, 1)
                        dve.tensor_scalar(put[:, j, tt, :], slot_row, pos[:, tt, e_], comb[:, tt, e_], ALU.is_equal,
                                          ALU.mult).then_inc(G["put_ready"], 1)

                def out_of(kind, j, dst, b):
                    dve.wait_ge(bank_full, turn_full(it, kind, j))
                    dve.tensor_copy(dst, b).then_inc(freed["V"], 1)

                out_of("x", 1, xs[:, 4:8, :, :], turn_bank("x", 1).rearrange("p (k j s) -> p k j s", k=4, j=EXPERTS_PER_TURN))
                out_of("w", 1, putT[:, 2:4, :], turn_bank("w", 1).rearrange("p (j t) -> p j t", j=2))
                for j in range(EXPERTS_PER_TURN):
                    out_of("up3", j, h3, turn_bank("up3", j))
                    dve.wait_ge(bank_full, turn_full(it, "t3", j))
                    turn_moved(dve, it, "t1", j)
                    b = turn_bank("t3", j).rearrange("p (k s) -> p k s", k=4)[:, :, 0:SLOTS]
                    dve.tensor_tensor(hidT, s1, b, ALU.mult).then_inc(freed["V"], 1)
                    out_of("down1", j, ys[:, 512:1024], turn_bank("down1", j))
            dve.wait_ge(used, OPENED + NE)
            dve.wait_ge(G["flag_ready"], 1)
            with dve.If(dve.value_load(flag[0:1, 0:1]) > 0):
                dve.sem_inc(d_used, 1)
                with dve.Fori(0, NE) as e:
                    dve.wait_ge(d_used, e + 1)
                    dve.tensor_copy(dcol, over[:, :, bass.ds(e, 1)].to_broadcast([P, TT, P])).then_inc(G["dcol_ready"], 1)
                    for i in range(2):
                        dve.wait_ge(d_act, e * 3 + (2 + i))
                        v = dsilu[:, 2 * i:2 * i + 2, :]
                        dve.tensor_tensor(v, v, dcomb.unsqueeze(1).to_broadcast([P, 2, T]), ALU.mult).then_inc(G["dsilu_scaled"], 1)
                        dve.wait_ge(G["dsilu_scaled"], e * 2 + (i + 1))
                        dve.wait_ge(d_full, e * 5 + (3 + 2 * i))
                        b = d_bank(2 + 2 * i).rearrange("p (k t) -> p k t", k=2)
                        dve.tensor_tensor(dhid[:, 2 * i:2 * i + 2, :], v, b, ALU.mult).then_inc(d_vec, 1)
                dve.wait_ge(d_used, NE + 1)
            for kt in range(KT):
                ins = dve.scalar_tensor_tensor(xT[:, kt, :], acc[:, kt, :], mod[:, 5 * KT + kt, 0:1], xT[:, kt, :], ALU.mult, ALU.add)
            ins.then_inc(G["resid_ready"], 1)
            dve.wait_ge(G["resid_ready"], 2)
            normed(3, xT, xT, lambda kt: col("final_norm_g", kt), None)

            def centred(k):
                b = take("mean", k)[:, 0:T].unsqueeze(1).to_broadcast([P, KT, T])
                ins = dve.scalar_tensor_tensor(xT, b, -1.0 / D, xT, ALU.mult, ALU.add)
                ins.then_inc(freed["V"], 1)

            for l in range(2):
                nt = 8 if l == 0 else 6
                ntile = 2 * nt
                moved(dve, f"qk{l}", nt - 1)
                ct = C("cos").unsqueeze(1)
                st = C("sin").unsqueeze(1)
                for i in range(nt):
                    b = take(f"rot{l}", i).rearrange("p (k t) -> p k t", k=2)
                    r_, q_ = qk_raw[:, 2 * i:2 * i + 2, :], qk[:, 2 * i:2 * i + 2, :]
                    dve.tensor_tensor(r_, r_, ct.to_broadcast([P, 2, T]), ALU.mult)
                    ins = dve.tensor_tensor(q_, b, st.to_broadcast([P, 2, T]), ALU.mult)
                    ins.then_inc(freed["V"], 1)
                    moved(dve, f"rot{l}", i)
                    dve.tensor_tensor(q_, q_, r_, ALU.add).then_inc(G["rot_ready"], 1)
                sets = SETS[l]
                k0 = 0 if l == 0 else len(SETS[0])
                if l == 0:
                    dve.wait_ge(masks_in, 16)

                def maxes(i):
                    k = k0 + i
                    n = len(sets[i])
                    s_ = sc[:, k % 2, 0:n, :]
                    for j in range(n):
                        b = take(f"sc{l}", (i, j))[:, 0:SC_W]
                        if k >= 2 and j == 0:
                            moved(dve, *last_pt(k - 2))
                        ins = dve.tensor_tensor(s_[:, j, :], b, masks[:, 0 if l == 0 else 1 + j, :], ALU.add)
                        ins.then_inc(freed["V"], 1)
                    moved(dve, f"sc{l}", (i, n - 1))
                    dve.tensor_reduce(mx[:, k % 2, 0:1], s_[:, :, 0:P], AX.XY, ALU.max)
                    link(dve.tensor_reduce(mx[:, k % 2, 1:2], s_[:, :, P:SC_W], AX.XY, ALU.max))
                    dve.tensor_scalar(mx[:, k % 2, :], mx[:, k % 2, :], -(HD ** -0.5), None, ALU.mult).then_inc(G["max_ready"], 1)

                def probs(i):
                    k = k0 + i
                    n = len(sets[i])
                    s_ = sc[:, k % 2, 0:n, :]
                    dve.wait_ge(G["exp_ready"], k + 1)
                    link(dve.reciprocal(rsum[:, k % 2, :], ssum[:, k % 2, :]))
                    dve.tensor_scalar(s_[:, :, 0:P], s_[:, :, 0:P], rsum[:, k % 2, 0:1], None, ALU.mult)
                    dve.tensor_scalar(s_[:, :, P:SC_W], s_[:, :, P:SC_W], rsum[:, k % 2, 1:2], None, ALU.mult).then_inc(G["p_ready"], 1)

                maxes(0)
                for i in range(len(sets)):
                    if i + 1 < len(sets):
                        maxes(i + 1)
                    probs(i)
                for i in range(4):
                    b = take(f"proj{l}", i).rearrange("p (k t) -> p k t", k=2)
                    v = xT[:, 2 * i:2 * i + 2, :]
                    ins = dve.scalar_tensor_tensor(v, v, ALPHA, b, ALU.mult, ALU.add)
                    ins.then_inc(freed["V"], 1)
                moved(dve, f"proj{l}", 3)
                dve.sem_inc(G["resid_ready"], 1)
                centred(2 * l)
                normed(4 + 2 * l, xT, xT, lambda kt: col("ln_mix_g_2", KT * l + kt), lambda kt: col("ln_mix_b_2", KT * l + kt))
                for i in range(FF // 256):
                    moved(dve, f"ff{l}", i)
                    v = hff[:, 2 * i:2 * i + 2, :]
                    dve.tensor_tensor(v, v, v, ALU.mult).then_inc(G["ff_ready"], 1)
                dve.wait_ge(*slab_freed(SLAB_AT[f"ff_out{l}", FF // 512 - 1]))
                ins = dve.scalar_tensor_tensor(xT, xT, ALPHA, acc[:, :, :], ALU.mult, ALU.add)
                ins.then_inc(G["resid_ready"], 1)
                dve.wait_ge(G["resid_ready"], 4 + 2 * l)
                centred(2 * l + 1)
                normed(5 + 2 * l, xT, xT, lambda kt: col("ln_mlp_g_2", KT * l + kt), lambda kt: col("ln_mlp_b_2", KT * l + kt))

        @block.tensor
        def _(pe):
            def bank(name, i):
                g = BANK_AT[name, i]
                if g >= RB:
                    pe.wait_ge(*freed_by(g - RB))
                return bank_of(name, i)

            def arrive(name, s, k, w):
                n = SLAB_AT[name, s]
                pe.wait_ge(landed[n % RING], 16 * (n // RING + 1))
                return view(n, k, w)

            def full(ins):
                ins.then_inc(bank_full, 1)

            def done(ins):
                ins.then_inc(used, 1)

            def turn(name, i, src, tt, q):
                b = bank(name, i)
                for j in range(4):
                    kt = 4 * q + j
                    ins = pe.transpose(b[:, j * P:(j + 1) * P], src[:, tt, kt * P:(kt + 1) * P], ident)
                full(ins)

            def fmajor(b, w, x, m0, n, ks=KT):
                for j in range(n):
                    for kt in range(ks):
                        ins = pe.matmul(b[:, j * T:(j + 1) * T], w[:, kt, m0 + j * P:m0 + (j + 1) * P], x[:, kt, :],
                                        start=(kt == 0), stop=(kt == ks - 1))
                return ins

            def tmajor(b, w, x, tt, ks=KT, n=512):
                for kt in range(ks):
                    ins = pe.matmul(b[:, 0:n], x[:, kt, tt * P:(tt + 1) * P], w[:, kt, 0:n], start=(kt == 0), stop=(kt == ks - 1))
                return ins

            pe.wait_ge(consts_in, 16)
            pe.wait_ge(smalls_in, 16 * NSM)
            b = bank("vectors", 0)
            pe.transpose(b[:, 0:NVEC], rows[0:NVEC, 0, :], ident[0:NVEC, 0:NVEC])
            full(pe.transpose(b[:, NVEC:NVEC + NLN], rows[0:NLN, 1, :], ident[0:NLN, 0:NLN]))
            pe.wait_ge(tokens_in, 16 * 2 * TT)
            for i in range(4):
                turn("x_tiles", i, xtok, *divmod(i, 2))
            for i in range(4):
                turn("c_tiles", i, ctok, *divmod(i, 2))

            def modulate(s):
                if s == 0:
                    pe.wait_ge(G["scol_ready"], 1)
                w = arrive("mod", s, KT, 512)
                b = bank("mod_rows", s)
                for half in range(2):
                    for g in range(4):
                        kt = 4 * half + g
                        ins = pe.matmul(b[32 * g:32 * g + 32, :], scol[:, kt, :], w[:, kt, :], start=(half == 0), stop=(half == 1))
                ins.then_inc(bank_full, 1)
                moved(pe, "mod_rows", s)
                b = bank("mod_cols", s)
                for j in range(4):
                    ins = pe.matmul(b[:, 2 * j:2 * j + 2], mod_row[:, s % 2, j * P:(j + 1) * P], C("sel"), start=True, stop=True)
                full(ins)

            for s in range(4):
                modulate(s)

            def norm_sum(name, k, src):
                b = bank(name, k)
                for kt in range(KT):
                    ins = pe.matmul(b[:, 0:T], ones, src[:, kt, :], start=(kt == 0), stop=(kt == KT - 1))
                full(ins)

            for k in range(2):
                pe.wait_ge(G["sq_ready"], k + 1)
                norm_sum("norm", k, sq)
            pe.wait_ge(G["h_ready"], 2 * KT)
            for i, src in enumerate((hT, cT)):
                b = bank("lr", i)
                for d in range(2):
                    for kt in range(KT):
                        ins = pe.matmul(b[0:RANK, d * T:(d + 1) * T], w_lr[:, kt, d * RANK:(d + 1) * RANK], src[:, kt, :],
                                        start=(kt == 0), stop=(kt == KT - 1))
                full(ins)
            moved(pe, "lr", 1)
            for i in range(8):
                st, tt = divmod(i, 2)
                d = st % 2
                b = bank("z", i)
                pe.matmul(b, lrT[:, st, tt * P:(tt + 1) * P], a2[:, d, :], start=True, stop=False)
                full(pe.matmul(b, ones[0:1, :], ab[0:1, d, :], start=False, stop=True))
            moved(pe, "z", 3)
            for i in range(4):
                d, hp = divmod(i, 2)
                b = bank("cum", i)
                for j in range(2):
                    for tt in range(TT):
                        h = 2 * hp + j
                        ins = pe.matmul(b[:, j * T + tt * P:j * T + (tt + 1) * P], L[:, 2 * d + tt, h * P:(h + 1) * P],
                                        C("cum_" + "fb"[d]), start=True, stop=True)
                full(ins)
            for i in range(4):
                d, tt = divmod(i, 2)
                full(pe.matmul(bank("remx", i), C("rem_" + "fb"[d]), L[:, 2 * d + tt, :], start=True, stop=True))
            moved(pe, "z", 7)
            for i in range(4):
                d, tt = divmod(i, 2)
                b = bank("remc", i)
                other = (d == 0 and tt == 0) or (d == 1 and tt == 1)
                ins = pe.matmul(b, C(("suf", "pre")[d]), L[:, 4 + 2 * d + tt, :], start=True, stop=not other)
                if other:
                    ins = pe.matmul(b, C("all"), L[:, 4 + 2 * d + 1 - tt, :], start=False, stop=True)
                full(ins)
            w = arrive("w_in", 2, KT, 512)
            for i in range(2):
                full(fmajor(bank("kT", i), w, hT, 2 * i * P, 2))
            for i in range(2):
                ins = tmajor(bank("kc", i), w, cT, i)
                full(ins)
            moved(pe, "kT", 1)
            for i in range(2):
                b = bank("ktok", i)
                for h in range(NH):
                    ins = pe.transpose(b[:, h * P:(h + 1) * P], kT[:, h, i * P:(i + 1) * P], ident)
                full(ins)
            for s in range(2):
                w = arrive("w_in", 3 + s, KT, 512)
                for i in range(4):
                    ins = tmajor(bank("v", 4 * s + i), w, (hT, cT)[i // 2], i % 2)
                    full(ins)
            w = arrive("w_in", 1, KT, 512)
            for i in range(2):
                ins = fmajor(bank("qT", i), w, hT, 2 * i * P, 2)
                full(ins)
            moved(pe, "v", 7)
            moved(pe, "ktok", 1)
            moved(pe, "qT", 1)
            for h in range(NH):
                hk, hv = slice(h * P, (h + 1) * P), slice(h * HV, (h + 1) * HV)
                b = bank("s0", h)
                for d in range(2):
                    for tt in range(TT):
                        ins = pe.matmul(b[:, d * HV:(d + 1) * HV], remc[:, d, tt, hk], vc[:, tt, hv], start=(tt == 0), stop=(tt == 1))
                full(ins)
                b = bank("sT", h)
                for d in range(2):
                    for tt in range(TT):
                        t_ = slice(tt * P, (tt + 1) * P)
                        ins = pe.matmul(b[:, (2 * d + tt) * P:(2 * d + tt + 1) * P], dec[:, 1, d, h, t_], dec[:, 0, d, h, t_],
                                        start=True, stop=True)
                full(ins)
                for n in range(NCH - 1):
                    for d in range(2):
                        c = n if d == 0 else NCH - 1 - n
                        tt, o = c // 2, CH * (c % 2)
                        b = bank("kv", (h, n, d))
                        full(pe.matmul(b[:, 0:HV], remx[o:o + CH, d, tt, hk], vx[o:o + CH, tt, hv], start=True, stop=True))
                moved(pe, "sT", h)
                moved(pe, "kv", (h, NCH - 2, 1))
                moved(pe, "s0", h)
                b = bank("o", h)
                for tt in range(TT):
                    bo = b[:, tt * HV:(tt + 1) * HV]
                    for d in range(2):
                        pe.matmul(bo, sTm[:, 2 * d + tt, :], vx[:, tt, hv], start=(d == 0), stop=False, skip_group_check=True)
                    for d in range(2):
                        for c in range(2):
                            n = 2 * tt + c
                            ins = pe.matmul(b[CH * c:CH * (c + 1), tt * HV:(tt + 1) * HV], dec[:, 0, d, h, n * CH:(n + 1) * CH],
                                            S[:, d, n, :], start=False, stop=(d == 1), skip_group_check=True)
                full(ins)
            w = arrive("w_in", 0, KT, 512)
            for i in range(2):
                ins = tmajor(bank("u", i), w, hT, i)
                full(ins)
            moved(pe, "u", 1)
            for i in range(2):
                b = bank("pool", i)
                for j in range(2):
                    g = 2 * i + j
                    for tt in range(TT):
                        ins = pe.matmul(b[:, j * T + tt * P:j * T + (tt + 1) * P], utok[:, tt, g * P:(g + 1) * P], C(f"pool{g}"),
                                        start=True, stop=True)
                full(ins)
            moved(pe, "pool", 1)
            for i in range(2):
                b = bank("y1", i)
                for j in range(2):
                    g = 2 * i + j
                    ins = pe.matmul(b[:, j * T:(j + 1) * T], w_pool[:, g, :], pooled[:, g, :], start=True, stop=True)
                full(ins)
            for s in range(2):
                w = arrive("w_in", 5 + s, KT, 512)
                for i in range(2):
                    ins = fmajor(bank("g", 2 * s + i), w, hT, 2 * i * P, 2)
                    full(ins)
            pe.wait_ge(G["on_ready"], 2)
            for i in range(4):
                turn("oT", i, otok, *divmod(i, 2))
            for s in range(4):
                w = arrive("w_in", 7 + s, KT, 512)
                for i in range(2):
                    ins = fmajor(bank("gate", 2 * s + i), w, hT, 2 * i * P, 2)
                    full(ins)
            for s in range(4, 12):
                modulate(s)
            w = arrive("pool_br", 0, POOLG, D)
            moved(pe, "y1", 1)
            for i in range(4):
                ins = fmajor(bank("ypool", i), w, y1, 2 * i * P, 2, ks=POOLG)
                full(ins)
            moved(pe, "oT", 3)
            for s in range(2):
                w = arrive("gla_br", s, KT, 512)
                for i in range(2):
                    ins = fmajor(bank("ygla", 2 * s + i), w, gT, 2 * i * P, 2)
                    full(ins)
            pe.wait_ge(G["z_ready"], 4)
            for s in range(2):
                w = arrive("w_o", s, KT, 512)
                for i in range(2):
                    ins = fmajor(bank("mix", 2 * s + i), w, sq, 2 * i * P, 2)
                    full(ins)
            pe.wait_ge(G["sq_ready"], 3)
            norm_sum("norm", 2, sq)
            pe.wait_ge(G["h_ready"], 3 * KT)
            b = bank("router", 0)
            for tt in range(TT):
                br = b[:, tt * (NG + NE):(tt + 1) * (NG + NE)]
                for kt in range(KT):
                    pe.matmul(br, hT[:, kt, tt * P:(tt + 1) * P], w_rt[:, kt, :], start=(kt == 0), stop=False)
                ins = pe.matmul(br, ones[0:1, :], rb[0:1, :], start=False, stop=True)
            full(ins)
            for i in range(4):
                tt, q = divmod(i, 2)
                b = bank("ttok", i)
                for j in range(4):
                    ins = pe.transpose(b[:, j * P:(j + 1) * P], hT[:, 4 * q + j, tt * P:(tt + 1) * P], ident)
                full(ins)
            pe.wait_ge(G["chosen_ready"], 2)
            b = bank("rank", 0)
            pe.matmul(b[:, 0:NE], C("pre"), chosen[:, 0, :], start=True, stop=True)
            pe.matmul(b[:, NE:2 * NE], C("pre"), chosen[:, 1, :], start=True, stop=False)
            pe.matmul(b[:, NE:2 * NE], C("all"), chosen[:, 0, :], start=False, stop=True)
            pe.matmul(b[:, 2 * NE:3 * NE], C("all"), chosen[:, 0, :], start=True, stop=False)
            full(pe.matmul(b[:, 2 * NE:3 * NE], C("all"), chosen[:, 1, :], start=False, stop=True))

            def open_acc(k):
                for j in range(4):
                    ins = pe.matmul(acc[:, 2 * j:2 * j + 2, :], zrow, zmov, start=True, stop=False, skip_group_check=True)
                ins.then_inc(used, OPENED)

            zrow, zmov = C("zero")[:, 0:P], hT[:, 0:2, :]
            open_acc(0)
            s0 = SLAB_AT["moe", 0]
            moved(pe, "rank", 0)
            moved(pe, "ttok", 3)
            with pe.Fori(0, TURNS) as it:
                def t_bank(kind, j):
                    g = TURN_AT[kind, j] - RB
                    prev = TURN[g]
                    turn_moved(pe, it, prev[0], prev[1], back=int(g < 0))
                    return turn_bank(kind, j)

                def t_slab(j, part, k, w):
                    n = s0 + 3 * j + part
                    pe.wait_ge(landed[n % RING], it * 48 + 16 * (n // RING + 1))
                    return view(n, k, w)

                pe.wait_ge(G["pick_ready"], it * 8 + 8)
                for q in range(2):
                    b = t_bank("x", q)
                    for kt in range(4):
                        for tt in range(TT):
                            f = (4 * q + kt) * P
                            ins = pe.matmul(b[:, kt * P:(kt + 1) * P], ttok[:, tt, f:f + P], pick[:, tt, :], start=(tt == 0), stop=(tt == 1))
                    full(ins)
                pe.wait_ge(G["put_ready"], it * 8 + 8)
                for q in range(2):
                    b = t_bank("w", q)
                    for j in range(2):
                        for tt in range(TT):
                            o = j * T + tt * P
                            ins = pe.transpose(b[:, o:o + P], put[:, 2 * q + j, tt, :], ident)
                    full(ins)
                for j in range(EXPERTS_PER_TURN):
                    for part, kind in enumerate(("up1", "up3")):
                        w = t_slab(j, part, KT, DE)
                        b = t_bank(kind, j)
                        if j == 0 and part == 0:
                            turn_moved(pe, it, "x", 0)
                            turn_moved(pe, it, "x", 1)
                        for kt in range(KT):
                            g = kt % 4
                            ins = pe.matmul(b[32 * g:32 * g + 32, :], xs[:, kt, j, :], w[:, kt, :], start=(kt < 4), stop=(kt >= 4))
                        full(ins)
                    for src, kind, up in ((h1, "t1", "up1"), (h3, "t3", "up3")):
                        turn_moved(pe, it, up, j)
                        b = t_bank(kind, j)
                        for f in range(4):
                            ins = pe.matmul(b[:, f * P:(f + 1) * P], src[:, f * P:(f + 1) * P], C("fold"), start=True, stop=True)
                        full(ins)
                    w = t_slab(j, 2, 4, D)
                    turn_moved(pe, it, "t3", j)
                    for half in range(2):
                        b = t_bank(f"down{half}", j)
                        for f in range(4):
                            ins = pe.matmul(b[32 * f:32 * f + 32, :], hidT[:, f, :], w[:, f, 512 * half:512 * half + 512], start=True, stop=True)
                        full(ins)
                    turn_moved(pe, it, "down0", j)
                    turn_moved(pe, it, "w", j // 2)
                    for m in range(KT):
                        if m == 4:
                            turn_moved(pe, it, "down1", j)
                        ins = pe.matmul(acc[:, m, :], ys[:, m * P:(m + 1) * P], putT[:, j, :], start=False, stop=True, skip_group_check=True)
                    done(ins)
            turn_moved(pe, TURNS - 1, "down0", EXPERTS_PER_TURN - 1)
            turn_moved(pe, TURNS - 1, "down1", EXPERTS_PER_TURN - 1)
            pe.wait_ge(G["flag_ready"], 1)
            with pe.If(pe.value_load(flag[0:1, 0:1]) > 0):
                with pe.Fori(0, NE) as e:
                    pe.wait_ge(d_landed, e * 48 + 48)
                    pe.wait_ge(G["dcol_ready"], e + 1)
                    w1, w3 = (dslab[j].rearrange("p (k n) -> p k n", k=KT) for j in range(2))
                    w2 = dslab[2].rearrange("p (k n) -> p k n", k=4)
                    for tt in range(TT):
                        ins = pe.matmul(d_bank(0)[:, tt * P:(tt + 1) * P], dcol[:, tt, :], ident, start=True, stop=True)
                    ins.then_inc(d_full, 1)
                    for i in range(2):
                        if i == 1:
                            pe.wait_ge(d_act, e * 3 + 1)
                        for n, w in ((1 + 2 * i, w1), (2 + 2 * i, w3)):
                            fmajor(d_bank(n), w, hT, 2 * i * P, 2).then_inc(d_full, 1)
                    pe.wait_ge(d_vec, e * 2 + 2)
                    for kt in range(4):
                        for m in range(KT):
                            ins = pe.matmul(acc[:, m, :], w2[:, kt, m * P:(m + 1) * P], dhid[:, kt, :], start=False, stop=True,
                                            skip_group_check=True)
                    ins.then_inc(d_used, 1)

            pe.wait_ge(G["sq_ready"], 4)
            norm_sum("norm", 3, sq)
            for l in range(2):
                nt = 8 if l == 0 else 6
                heads = MOBA_H if l == 0 else DIL_H
                pe.wait_ge(G["h_ready"], (4 + 2 * l) * KT)
                tile_at = 0
                for s in range(nt // 2):
                    w = arrive(f"qkv{l}", s, KT, 512)
                    for i in range(2):
                        ins = fmajor(bank(f"qk{l}", 2 * s + i), w, xT, 2 * i * P, 2)
                        full(ins)
                moved(pe, f"qk{l}", nt - 1)
                for i in range(nt):
                    b = bank(f"rot{l}", i)
                    for j in range(2):
                        ins = pe.matmul(b[:, j * T:(j + 1) * T], C("rot"), qk_raw[:, 2 * i + j, :], start=True, stop=True)
                    full(ins)
                vs = nt // 2
                w2 = 512 if l == 0 else 256
                wa = arrive(f"qkv{l}", vs, KT, 512)
                wb = arrive(f"qkv{l}", vs + 1, KT, w2)
                for tt in range(TT):
                    full(tmajor(bank(f"val{l}", 2 * tt), wa, xT, tt))
                    ins = tmajor(bank(f"val{l}", 2 * tt + 1), wb, xT, tt, n=w2)
                    full(ins)
                moved(pe, f"val{l}", 3)
                pe.wait_ge(G["rot_ready"], nt if l == 0 else 8 + nt)
                sets = SETS[l]
                k0 = 0 if l == 0 else len(SETS[0])

                def scores(i):
                    for j, h in enumerate(sets[i]):
                        b = bank(f"sc{l}", (i, j))
                        o = HD * (h % 2)
                        q_, k_ = qk[o:o + HD, h // 2, :], qk[o:o + HD, nt + h // 2, :]
                        pe.matmul(b[:, 0:P], q_[:, 0:P], k_[:, 0:P], start=True, stop=True)
                        full(pe.matmul(b[:, P:SC_W], q_[:, P:T], k_, start=True, stop=True))

                scores(0)
                for i in range(len(sets)):
                    k = k0 + i
                    if i + 1 < len(sets):
                        scores(i + 1)
                    pe.wait_ge(G["p_ready"], k + 1)
                    for j in range(len(sets[i])):
                        b = bank(f"pt{l}", (i, j))
                        for c in range(3):
                            ins = pe.transpose(b[:, c * P:(c + 1) * P], sc[:, k % 2, j, c * P:(c + 1) * P], ident)
                        full(ins)
                    for j, h in enumerate(sets[i]):
                        moved(pe, f"pt{l}", (i, j))
                        b = bank(f"pv{l}", (i, j))
                        o = HD * (h % 2)
                        hv = slice(h * HD, (h + 1) * HD)
                        pe.matmul(b[o:o + HD, 0:P], vt[:, 0, hv], pT[:, j, 0:P], start=True, stop=True)
                        pe.matmul(b[o:o + HD, P:T], vt[:, 0, hv], pT[:, j, P:2 * P], start=True, stop=False)
                        full(pe.matmul(b[o:o + HD, P:T], vt[:, 1, hv], pT[:, j, 2 * P:3 * P], start=False, stop=True))
                moved(pe, f"pv{l}", (len(sets) - 1, len(sets[-1]) - 1))
                ks = heads * HD // P
                for s in range(2):
                    w = arrive(f"proj{l}", s, ks, 512)
                    for i in range(2):
                        ins = fmajor(bank(f"proj{l}", 2 * s + i), w, attT, 2 * i * P, 2, ks=ks)
                        full(ins)
                pe.wait_ge(G["resid_ready"], 3 + 2 * l)
                norm_sum("mean", 2 * l, xT)
                pe.wait_ge(G["sq_ready"], 5 + 2 * l)
                norm_sum("norm", 4 + 2 * l, sq)
                pe.wait_ge(G["h_ready"], (5 + 2 * l) * KT)
                for s in range(FF // 512):
                    w = arrive(f"ff_in{l}", s, KT, 512)
                    for i in range(2):
                        ins = fmajor(bank(f"ff{l}", 2 * s + i), w, xT, 2 * i * P, 2)
                        full(ins)
                for s in range(FF // 512):
                    w = arrive(f"ff_out{l}", s, 4, D)
                    pe.wait_ge(G["ff_ready"], (FF // 256) * l + 2 * s + 2)
                    for kt in range(4):
                        for m in range(KT):
                            ins = pe.matmul(acc[:, m, :], w[:, kt, m * P:(m + 1) * P], hff[:, 4 * s + kt, :],
                                            start=(s == 0 and kt == 0 and m % 2 == 0), stop=(s == FF // 512 - 1 and kt == 3), skip_group_check=True)
                    done(ins)
                pe.wait_ge(G["resid_ready"], 4 + 2 * l)
                norm_sum("mean", 2 * l + 1, xT)
                pe.wait_ge(G["sq_ready"], 6 + 2 * l)
                norm_sum("norm", 5 + 2 * l, sq)
            pe.wait_ge(G["h_ready"], 8 * KT)
            for i in range(4):
                tt, q = divmod(i, 2)
                b = bank("out", i)
                for j in range(4):
                    ins = pe.transpose(b[:, j * P:(j + 1) * P], xT[:, 4 * q + j, tt * P:(tt + 1) * P], ident)
                full(ins)


_INS = ["x", "c", "ctx", "c_ctx", "w_mod", "b_mod", "norm1_g", "norm2_g", "w_in", "gla_a2_f", "gla_ab_f", "gla_a2_b",
        "gla_ab_b", "gla_onorm_g", "pool_w", "pool_scale", "w_pool_br", "w_gla_br", "w_o", "router_grp_w", "router_grp_b",
        "router_exp_w", "router_exp_b", "moe_w1", "moe_w3", "moe_w2", "final_norm_g", "moba_w_qkv_2", "moba_w_o_2",
        "dil_w_qkv_2", "dil_w_o_2", "mlp_w_in_2", "mlp_w_out_2", "ln_mix_g_2", "ln_mix_b_2", "ln_mlp_g_2", "ln_mlp_b_2"]


def kernel(**inputs):
    from concourse import bacc
    from concourse.bass_utils import run_bass_kernel_spmd

    nc = bacc.Bacc("TRN2", target_bir_lowering=False, num_devices=1)
    arrays = {name: np.ascontiguousarray(inputs[name]) for name in _INS}
    arrays["consts"] = constants()[1]
    arrays["masks"] = score_masks()
    args = {name: nc.dram_tensor("in_" + name, v.shape, mybir.dt.from_np(v.dtype), kind="ExternalInput").ap()
            for name, v in arrays.items()}
    out = nc.dram_tensor("out_x", (1, T, D), mybir.dt.float32, kind="ExternalOutput").ap()
    build(nc, args, out)
    r = run_bass_kernel_spmd(nc, [{"in_" + name: v for name, v in arrays.items()}], core_ids=[0])
    return r.results[0]["out_x"]
```

```python
import numpy as np

import concourse.bass as bass
from concourse import mybir
from contextlib import ExitStack

P = 128
D = 1024
KT = D // P
T = 256
TT = T // P
CH = 64
NCH = T // CH
NH = 4
HV = 256
DK = NH * P
RANK = 16
POOLG = 4
WINDOWS = (2, 4, 8, 16)
NE, NG, EG = 32, 4, 8
DE = 512
FF = 4096
SLAB = 4096
HD = 64
MOBA_H, DIL_H, DIL_SLOTS = 16, 12, 4
DIL = ((128, 1), (512, 4), (2048, 16))
EPS, LN_EPS = 1e-6, 1e-5
ALPHA = 4.0 ** 0.25
GATE_NORM = 16.0
NEG = -1e30
SLOTS = 32
CAP = SLOTS
SC_W = 384


def constants():
    s, t = np.arange(P)[:, None], np.arange(P)[None, :]
    chunk = (s // CH) == (t // CH)
    inv = 1.0 / GATE_NORM
    parts = {
        "ident": s == t,
        "ones": np.ones((P, P)),
        "cum_f": (chunk & (s <= t)) * inv, "cum_b": (chunk & (s >= t)) * inv,
        "rem_f": (chunk & (s > t)) * inv, "rem_b": (chunk & (s < t)) * inv,
        "suf": (s > t) * inv, "pre": (s < t) * inv, "all": np.full((P, P), inv),
    }
    for g, w in enumerate(WINDOWS):
        lo = np.clip(t % CH - w // 2, 0, CH)
        hi = np.clip(t % CH + w // 2, 0, CH)
        inside = chunk & (s % CH >= lo) & (s % CH < hi)
        parts[f"pool{g}"] = inside / (hi - lo) - (s == t)
    half = HD // 2
    rot = np.zeros((P, P))
    for i in range(P):
        if i % HD < half:
            rot[i + half, i] = -1.0
        else:
            rot[i - half, i] = 1.0
    parts["rot"] = rot
    freq = (1.0 / (10000.0 ** (np.arange(0, HD, 2, dtype=np.float32) / HD))).astype(np.float32)
    ang = np.arange(T, dtype=np.float32)[:, None] * freq[None, :]
    parts["cos"] = np.tile(np.cos(ang).astype(np.float32).T, (4, 1))
    parts["sin"] = np.tile(np.sin(ang).astype(np.float32).T, (4, 1))
    parts["sel"] = (s[:, :1] % 32 == np.arange(2)[None, :]) * 1.0
    parts["sel"] = np.broadcast_to(parts["sel"], (P, 2))
    parts["slot"] = np.broadcast_to(t % SLOTS, (P, P))
    parts["fold"] = (s % SLOTS) == (t % SLOTS)
    parts["zero"] = np.zeros((P, P))
    parts["desc4"] = np.broadcast_to(np.arange(4, 0, -1.0), (P, 4))
    parts["desc8"] = np.broadcast_to(np.arange(8, 0, -1.0), (P, 8))
    at, cols, n = {}, [], 0
    for name, a in parts.items():
        a = np.asarray(a, np.float32)
        at[name] = (n, a.shape[1])
        cols.append(a)
        n += a.shape[1]
    return at, np.ascontiguousarray(np.concatenate(cols, 1), np.float32)


def score_masks():
    out = []
    for span, dil in ((T, 1),) + tuple((w // d, d) for w, d in DIL):
        q, k = np.arange(T)[:, None], np.arange(T)[None, :]
        dist = q - k
        ok = (dist >= 0) & (dist % dil == 0) & (dist // dil <= span)
        m = np.where(ok, 0.0, NEG).astype(np.float32)
        out.append(np.concatenate([m[:P, :P], m[P:, :]], 1))
    return np.ascontiguousarray(np.stack(out, 1), np.float32)


CONST_AT, _ = constants()


VEC_ROWS = (("c", KT), ("c_ctx", KT), ("b_mod", 6 * KT), ("norm1_g", KT), ("norm2_g", KT),
            ("final_norm_g", KT), ("pool_scale", POOLG), ("gla_onorm_g", HV // P))
LN_ROWS = (("ln_mix_g_2", 2 * KT), ("ln_mix_b_2", 2 * KT), ("ln_mlp_g_2", 2 * KT), ("ln_mlp_b_2", 2 * KT))
COL, _n = {}, 0
for _name, _k in VEC_ROWS + LN_ROWS:
    COL[_name] = (_n, _k)
    _n += _k
NVEC = sum(k for _, k in VEC_ROWS)
NLN = sum(k for _, k in LN_ROWS)

SETS = ([(h,) for h in range(MOBA_H)], [tuple(j + DIL_SLOTS * g for g in range(3)) for j in range(DIL_SLOTS)])


EXPERTS_PER_TURN = 4
TURNS = NE // EXPERTS_PER_TURN
TURN = [("x", 0, "A"), ("x", 1, "V"), ("w", 0, "A"), ("w", 1, "V")]
TURN += [(kind, j, o) for j in range(EXPERTS_PER_TURN)
         for kind, o in (("up1", "A"), ("up3", "V"), ("t1", "A"), ("t3", "V"), ("down0", "A"), ("down1", "V"))]
TURN_AT = {(kind, j): n for n, (kind, j, _) in enumerate(TURN)}


def slab_plan():
    order = [("mod", s) for s in range(4)]
    order += [("w_in", 2), ("w_in", 3), ("w_in", 4), ("w_in", 1), ("w_in", 0)]
    order += [("mod", 4), ("w_in", 5), ("mod", 5), ("w_in", 6), ("mod", 6)]
    for s in range(4):
        order += [("w_in", 7 + s), ("mod", 7 + s)]
    order += [("pool_br", 0), ("mod", 11), ("gla_br", 0), ("gla_br", 1), ("w_o", 0), ("w_o", 1)]
    order += [("moe", s) for s in range(3 * NE)]
    for l in range(2):
        order += [(f"qkv{l}", s) for s in range(6 if l == 0 else 5)]
        order += [(f"proj{l}", s) for s in range(2)]
        order += [(f"ff_in{l}", s) for s in range(FF // 512)]
        order += [(f"ff_out{l}", s) for s in range(FF // 512)]
    return {key: n for n, key in enumerate(order)}


def bank_plan():
    order = [("c_tiles", i, "V") for i in range(4)] + [("x_tiles", i, "A") for i in range(4)]
    order += [("vectors", 0, "V")]
    order += [("norm", 0, "A"), ("norm", 1, "A")]
    for s in range(4):
        order += [("mod_rows", s, "A")] + [("mod_cols", s - 1, "V")] * (s > 0)
    order += [("mod_cols", 3, "V")]
    order += [("lr", i, "A") for i in range(2)]
    order += [("z", i, "V") for i in range(8)]
    order += [("cum", i, "A") for i in range(4)]
    order += [("remx", i, "A") for i in range(4)]
    order += [("remc", i, "A") for i in range(4)]
    order += [("kT", i, "V") for i in range(2)] + [("kc", i, "V") for i in range(2)] + [("ktok", i, "V") for i in range(2)]
    for s in range(2):
        order += [("v", 4 * s + i, "A") for i in range(4)]
    order += [("qT", i, "V") for i in range(2)]
    for h in range(NH):
        order += [("s0", h, "A"), ("sT", h, "V")]
        order += [("kv", (h, n, d), "V") for n in range(NCH - 1) for d in range(2)]
        order += [("o", h, "A")]
    order += [("u", i, "A") for i in range(2)] + [("pool", i, "V") for i in range(2)] + [("y1", i, "V") for i in range(2)]
    for s in range(4, 6):
        order += [("mod_rows", s, "A"), ("g", 2 * (s - 4), "A"), ("mod_cols", s, "V"), ("g", 2 * (s - 4) + 1, "A")]
    order += [("mod_rows", 6, "A"), ("oT", 0, "V"), ("oT", 1, "V"), ("mod_cols", 6, "V"), ("oT", 2, "V"), ("oT", 3, "V")]
    for s in range(7, 11):
        order += [("gate", 2 * (s - 7), "A")]
        order += [("mod_cols", s - 1, "V")] * (s > 7)
        order += [("gate", 2 * (s - 7) + 1, "A"), ("mod_rows", s, "A")]
    order += [("ypool", 0, "V"), ("mod_cols", 10, "V")] + [("ypool", i, "V") for i in range(1, 4)]
    order += [("mod_rows", 11, "A"), ("ygla", 0, "V"), ("mod_cols", 11, "V")] + [("ygla", i, "V") for i in range(1, 4)]
    order += [("mix", i, "V") for i in range(4)]
    order += [("norm", 2, "A")]
    order += [("router", 0, "V")]
    order += [("ttok", i, "A") for i in range(4)]
    order += [("rank", 0, "V")]
    order += [("moe", (turn, kind, j), o) for turn in range(TURNS) for kind, j, o in TURN]
    order += [("norm", 3, "A")]
    for l in range(2):
        nt = 8 if l == 0 else 6
        nv = 4 if l == 0 else 3
        for i in range(nt):
            order += [(f"qk{l}", i, "A")]
            order += [(f"rot{l}", i - 1, "V")] * (i > 0)
        order += [(f"val{l}", 0, "A"), (f"rot{l}", nt - 1, "V")]
        order += [(f"val{l}", i, "A") for i in range(1, nv - 1)]
        sets = SETS[l]
        n, heads = len(sets), range(len(sets[0]))
        for t in range(n + 2):
            order += [(f"sc{l}", (t, j), "V") for j in heads if t < n]
            order += [(f"val{l}", nv - 1, "A")] * (t == 0)
            order += [(f"pt{l}", (t - 1, j), "A") for j in heads if 1 <= t <= n]
            order += [(f"pv{l}", (t - 2, j), "V") for j in heads if t >= 2]
        order += [(f"proj{l}", i, "V") for i in range(4)]
        order += [("mean", 2 * l, "V"), ("norm", 4 + 2 * l, "A")]
        order += [(f"ff{l}", i, "A") for i in range(FF // 256)]
        order += [("mean", 2 * l + 1, "V"), ("norm", 5 + 2 * l, "A")]
    order += [("out", i, "A") for i in range(4)]
    return order


SLAB_AT = slab_plan()
_ORDER = bank_plan()
SLABS = list(SLAB_AT)
RING, MOE_RING = 4, 6
SLOT_OF, NTH, BEFORE, _held = [], [], [], {}
for _n, (_name, _s) in enumerate(SLABS):
    _slot = _s % MOE_RING if _name == "moe" else (_n if _n < SLAB_AT["moe", 0] else _n - SLAB_AT["qkv0", 0]) % RING
    SLOT_OF.append(_slot)
    NTH.append(_held.get(_slot, (0, None))[0] + 1)
    BEFORE.append(_held.get(_slot, (0, None))[1])
    _held[_slot] = (NTH[-1], _n)
HALVES = [("w_in", s, u) for s in range(5, 11) for u in range(2)]
HALVES += [(name, s, u) for name in ("gla_br", "w_o") for s in range(2) for u in range(2)]
MIXER_HALVES = len(HALVES)
HALVES += [(name, s, u) for name, s in SLABS[SLAB_AT["qkv0", 0]:] for u in range(1 if (name, s) == ("qkv1", 4) else 2)]
HALF_AT = {key: n for n, key in enumerate(HALVES)}
WB = 2
BANK_AT = {(name, i): n for n, (name, i, _) in enumerate(_ORDER)}
OWNER = [o for _, _, o in _ORDER]


def build(nc, a, out):
    F32 = mybir.dt.float32
    F32R = mybir.dt.float32r
    U32 = mybir.dt.uint32
    ALU = mybir.AluOpType
    ACT = mybir.ActivationFunctionType
    AX = mybir.AxisListType

    ctx = ExitStack()
    with ctx:
        def sem(name):
            return ctx.enter_context(nc.semaphore(name))

        def sb(name, shape):
            return ctx.enter_context(nc.sbuf_tensor(name, shape, F32))

        NC = sum(w for _, w in CONST_AT.values())
        const = sb("const", [P, NC])

        def C(name):
            o, w = CONST_AT[name]
            return const[:, o:o + w]

        ident, ones = C("ident"), C("ones")
        K1 = 1024
        ARENA = 44 * K1 + 9 * SC_W
        arena_at = -(-nc.sbuf_base // 32) * 32
        slots_mem = sb("slots", [P, 16 * K1])
        arena = sb("arena", [P, ARENA - 16 * K1])

        def at(o, *dims):
            n = int(np.prod(dims))
            assert o + n <= ARENA
            names = " ".join(f"x{i}" for i in range(len(dims)))
            v = slots_mem[:, o:o + n] if o + n <= 16 * K1 else arena[:, o - 16 * K1:o - 16 * K1 + n]
            if len(dims) == 1:
                return v
            return v.rearrange(f"p ({names}) -> p {names}", **{f"x{i}": d for i, d in enumerate(dims)})

        slot = [at(SLAB * i, SLAB) for i in range(RING)] + [at((32 + 4 * i) * K1, SLAB) for i in range(MOE_RING - RING)]
        xT = at(16 * K1, KT, T)
        hT = at(18 * K1, KT, T)
        sq = at(20 * K1, KT, T)
        cT = at(22 * K1, KT, T)
        L = at(24 * K1, 8, DK)
        S = at(24 * K1, 2, NCH, HV)
        sTm = at(26 * K1, 4, P)
        y1 = at(27 * K1, POOLG, T)
        dec = at(28 * K1, 2, 2, NH, T)
        xtok = at(28 * K1, TT, D)
        ctok = at(30 * K1, TT, D)
        gates = at(28 * K1, 2 * KT, T)
        remx = at(32 * K1, 2, TT, DK)
        remc = at(34 * K1, 2, TT, DK)
        kT = at(37 * K1, NH, T)
        vx = at(38 * K1, TT, D)
        vc = at(40 * K1, TT, D)
        gT = at(40 * K1, KT, T)
        otok = at(42 * K1, TT, D)
        utok = at(24 * K1, TT, DK)
        pooled = at(25 * K1, POOLG, T)
        osq = at(26 * K1 + 512, HV)
        mod_row = at(44 * K1, 2, 512)
        ez = [at(o * K1, 4, DK) for o in (20, 34)]
        sq2 = at(22 * K1, KT, T)
        ttok = at(22 * K1, TT, D)
        o_ = 24 * K1
        pick = at(o_, TT, EXPERTS_PER_TURN * SLOTS)
        put = at(o_ + 256, EXPERTS_PER_TURN, TT, P)
        putT = at(o_ + 1280, EXPERTS_PER_TURN, T)
        xs = at(o_ + 2304, KT, EXPERTS_PER_TURN, SLOTS)
        h1 = at(o_ + 3328, DE)
        h3 = at(o_ + 3840, DE)
        s1 = at(o_ + 4352, 4, SLOTS)
        hidT = at(o_ + 4480, 4, SLOTS)
        ys = at(o_ + 4608, D)
        dslab = [at((30 + 4 * j) * K1, SLAB) for j in range(3)]
        dhid = at(42 * K1, 4, T)
        dsilu = at(43 * K1, 4, T)
        dcol = at(44 * K1, TT, P)
        dcomb = at(44 * K1 + 256, T)
        def split_at(name, o, *dims):
            t = nc.alloc_sbuf_tensor_at(name, [P, int(np.prod(dims))], F32R, offset=arena_at + 4 * o)
            names = " ".join(f"x{i}" for i in range(len(dims)))
            return t[:, :].rearrange(f"p ({names}) -> p {names}", **{f"x{i}": d for i, d in enumerate(dims)})

        xhi = split_at("xhi", 18 * K1, KT, T)
        xlo = split_at("xlo", 22 * K1, KT, T)
        whi = split_at("whi", 24 * K1, WB, SLAB // 2)
        wlo = split_at("wlo", 28 * K1, WB, SLAB // 2)
        qk_raw = at(32 * K1, 16, T)
        qk = at(36 * K1, 16, T)
        vt = at(40 * K1, TT, D)
        atthi = split_at("atthi", 42 * K1, KT, T)
        attlo = split_at("attlo", 32 * K1, KT, T)
        pT = at(33 * K1 + 512, 6, SC_W)
        sc = at(44 * K1, 2, 3, SC_W)
        masks = at(44 * K1 + 6 * SC_W, 3, SC_W)
        hsq = at(44 * K1, 2, 512)
        hffhi = split_at("hffhi", 32 * K1, FF // P, T)
        HLO = 16
        hfflo_a = split_at("hfflo_a", 40 * K1, HLO, T)
        hfflo_b = split_at("hfflo_b", 20 * K1, 8, T)
        hfflo_c = split_at("hfflo_c", 45 * K1, 8, T)

        hhi = split_at("hhi", 22 * K1, KT, T)
        hlo = split_at("hlo", 20 * K1, KT, T)
        w1hi = split_at("w1hi", 32 * K1, WB, SLAB // 2)
        w1lo = split_at("w1lo", 36 * K1, WB, SLAB // 2)
        ghi = split_at("ghi", 42 * K1, KT, T)
        glo = split_at("glo", 40 * K1, KT, T)
        zhi = split_at("zhi", 18 * K1, KT, T)
        zlo = split_at("zlo", 20 * K1, KT, T)

        def hfflo(i, n=1):
            t, i = (hfflo_a, i) if i < HLO else (hfflo_b, i - HLO) if i < HLO + 8 else (hfflo_c, i - HLO - 8)
            return t[:, i:i + n, :]

        w_pool = at(45 * K1, POOLG, P)
        w_lr = at(45 * K1 + 512, KT, 2 * RANK)
        w_rt = at(45 * K1 + 768, KT, NG + NE)
        a2 = at(42 * K1, 2, DK)[0:RANK + 1]
        rb = sb("rb", [1, NG + NE])
        rows = sb("rows", [P, 2, P])
        cols = sb("cols", [P, NVEC + NLN])
        scol = at(45 * K1 + 1056, KT, 32)
        mod = sb("mod", [P, 6 * KT, 2])
        scale1 = sb("scale1", [P, 3, KT])
        std = sb("std", [P, T])
        lrT = at(36 * K1, 4, T)[0:RANK + 1]
        decay = sb("decay", [P, 2, NH, NCH])
        oss = sb("oss", [P, TT, NH])
        orstd = sb("orstd", [P, TT, NH])
        oeps = sb("eps", [P, 2])
        lg = sb("lg", [P, TT, NG + NE])
        r4 = sb("r4", [P, 4, TT, NG])
        r8 = sb("r8", [P, 6, TT, EG])
        r1 = sb("r1", [P, 12, TT])
        r32 = sb("r32", [P, TT, NG, EG])
        comb = sb("comb", [P, TT, NE])
        chosen = sb("chosen", [P, TT, NE])
        pos = sb("pos", [P, TT, NE])
        over = sb("over", [P, TT, NE])
        n_over = sb("n_over", [P, 2])
        flag = ctx.enter_context(nc.sbuf_tensor("flag", [P, 1], mybir.dt.int32))
        mx = sb("mx", [P, 2, TT])
        ssum = sb("ssum", [P, 2, TT])
        rsum = sb("rsum", [P, 2, TT])

        RB = 4
        OPENED = 2
        ring = ctx.enter_context(nc.psum_tensor("ring", [P, RB, 512], F32))
        acc = ctx.enter_context(nc.psum_tensor("acc", [P, KT, T], F32))

        consts_in = sem("consts_in")
        smalls_in = sem("smalls_in")
        ident_in = sem("identity_in")
        rows_in = sem("rows_in")
        tokens_in = {"x": sem("x_in"), "ctx": sem("ctx_in")}
        masks_in = sem("masks_in")
        landed = [sem(f"slab_landed{i}") for i in range(MOE_RING)]
        used = sem("slab_used")
        bank_full = sem("bank_full")
        freed = {"V": sem("bank_freed_by_vector"), "A": sem("bank_freed_by_scalar")}
        d_landed = sem("dense_slabs_landed")
        d_used = sem("dense_expert_used")
        d_full = sem("dense_bank_full")
        d_act = sem("dense_scalar_done")
        d_vec = sem("dense_hidden_ready")
        v_step = sem("vector_step")
        a_step = sem("scalar_step")
        names = "acc_pair hhi_ready hlo_ready ghi_ready glo_ready zhi_ready zlo_ready abs_ready L_ready lr_ones whi_ready split_ready xhi_ready xlo_ready acc_out cen_ready atthi_ready chosen_ready flag_ready pick_ready put_ready dcol_ready dsilu_scaled ff_ready scol_zero scol_ready sq_ready rstd_read h_ready ez_ready ostd_ready on_ready z_ready lg_diff rexp_ready comb_ready rot_ready max_ready exp_ready p_ready out_stored eps_ready".split()
        G = {n: sem(n) for n in names}

        def bank_of(name, i):
            return ring[:, BANK_AT[name, i] % RB, :]

        def freed_by(g):
            return freed[OWNER[g]], sum(o == OWNER[g] for o in OWNER[:g + 1])

        def moved(eng, name, i):
            eng.wait_ge(*freed_by(BANK_AT[name, i]))

        m0 = BANK_AT["moe", (0, "x", 0)]

        def turn_bank(kind, j):
            return ring[:, (m0 + TURN_AT[kind, j]) % RB, :]

        def turn_full(it, kind, j):
            return it * len(TURN) + (m0 + TURN_AT[kind, j] + 1)

        def turn_moved(eng, it, kind, j, back=0):
            g = TURN_AT[kind, j]
            o = TURN[g][2]
            per = sum(x[2] == o for x in TURN)
            before = sum(x == o for x in OWNER[:m0]) - back * per + sum(x[2] == o for x in TURN[:g + 1])
            eng.wait_ge(freed[o], it * per + before)

        def finished(h):
            name, s, u = HALVES[h]
            if h < MIXER_HALVES:
                mixer_use = {"gla_br": ("ygla", 2 * s + u), "w_o": ("mix", 2 * s + u),
                             "w_in": ("g", 2 * (s - 5) + u) if s < 7 else ("gate", 2 * (s - 7) + u)}
                return bank_full, BANK_AT[mixer_use[name]] + 1
            l, i = int(name[-1]), 2 * s + u
            if name[:-1] == "ff_out":
                return used, OPENED + NE + 2 * (FF // 512) * l + i + 1
            if name[:-1] == "ff_in":
                name = f"ff{l}"
            elif name[:-1] == "qkv":
                nt = 8 if l == 0 else 6
                name, i = (f"qk{l}", i) if i < nt else (f"val{l}", i - nt)
            return bank_full, BANK_AT[name, i] + 1

        def half_of(h):
            name, s, u = HALVES[h]
            src = slab_source(name, s)
            k, w = src.shape[1], src.shape[2]
            raw = view(SLAB_AT[name, s], k, w)
            raw = raw[:, 2 * u:2 * u + 2, :] if name[:-1] == "ff_out" else raw[:, :, 256 * u:256 * u + 256]
            k, w = raw.shape[1], raw.shape[2]
            hi, lo = (t[:, h % WB, 0:k * w].rearrange("p (k n) -> p k n", k=k) for t in ((w1hi, w1lo) if h < MIXER_HALVES else (whi, wlo)))
            return raw, hi, lo

        def d_bank(n):
            return ring[:, n % RB, :]

        def pT_of(l, k, j):
            return pT[:, 4 + k % 2 if l == 0 else 3 * (k % 2) + j, :]

        def last_pt(k):
            l, i = (0, k) if k < len(SETS[0]) else (1, k - len(SETS[0]))
            return f"pt{l}", (i, len(SETS[l][i]) - 1)

        def slab_freed(n):
            name, s = SLABS[n]
            if name == "moe":
                e, j = divmod(s, 3)
                turn, e = divmod(e, EXPERTS_PER_TURN)
                return bank_full, BANK_AT["moe", (turn, ("up1", "up3", "down1")[j], e)] + 1
            if (name, s, 0) in HALF_AT:
                return G["split_ready"], max(h for h, (nm, s_, _) in enumerate(HALVES) if (nm, s_) == (name, s)) + 1
            if name == "w_in":
                bank_use = {0: ("u", 1), 1: ("qT", 1), 2: ("kc", 1), 3: ("v", 3), 4: ("v", 7)}[s]
            else:
                bank_use = ("mod_rows", s) if name == "mod" else ("ypool", 3)
            return bank_full, BANK_AT[bank_use] + 1

        def w_in(s):
            return a["w_in"][0][:, 512 * s:512 * s + 512].rearrange("(k p) n -> p k n", p=P)

        def slab_source(name, s):
            if name == "mod":
                return a["w_mod"][0][:, 512 * s:512 * s + 512].rearrange("(k p) n -> p k n", p=P)
            if name == "w_in":
                return w_in(s)
            if name == "pool_br":
                return a["w_pool_br"][0].rearrange("(k p) n -> p k n", p=P)
            if name in ("gla_br", "w_o"):
                w = a["w_gla_br" if name == "gla_br" else "w_o"][0]
                return w[:, 512 * s:512 * s + 512].rearrange("(k p) n -> p k n", p=P)
            l = int(name[-1])
            if name[:-1] == "qkv":
                w = a[("moba", "dil")[l] + "_w_qkv_2"][0]
                return w[:, 512 * s:min(512 * s + 512, w.shape[1])].rearrange("(k p) n -> p k n", p=P)
            if name[:-1] == "proj":
                w = a[("moba", "dil")[l] + "_w_o_2"][0]
                return w[:, 512 * s:512 * s + 512].rearrange("(k p) n -> p k n", p=P)
            if name[:-1] == "ff_in":
                return a["mlp_w_in_2"][l][:, 512 * s:512 * s + 512].rearrange("(k p) n -> p k n", p=P)
            return a["mlp_w_out_2"][l][512 * s:512 * s + 512, :].rearrange("(k p) n -> p k n", p=P)

        def view(n, k, w):
            return slot[SLOT_OF[n]][:, 0:k * w].rearrange("p (k n) -> p k n", k=k)

        block = ctx.enter_context(nc.Block())

        @block.sync
        def _(sp):
            def load(n, src):
                if BEFORE[n] is not None:
                    sp.wait_ge(*slab_freed(BEFORE[n]))
                elif n >= RING:
                    sp.wait_ge(*finished(MIXER_HALVES - 1))
                sp.dma_start(view(n, src.shape[1], src.shape[2]), src).then_inc(landed[SLOT_OF[n]], 16)

            def expert_source(j, e):
                w = a[("moe_w1", "moe_w3", "moe_w2")[j]][0]
                return w[bass.ds(e, 1), :, :].rearrange("e (k p) n -> p (e k) n", p=P)

            sp.dma_start(ident, a["consts"][:, 0:P]).then_inc(ident_in, 16)
            for dst, name in ((ctok, "ctx"), (xtok, "x")):
                sp.dma_start(dst, a[name][0].rearrange("(a p) n -> p a n", p=P)).then_inc(tokens_in[name], 16)
            for table, r, base in ((VEC_ROWS, 0, 0), (LN_ROWS, 1, NVEC)):
                for name, n in table:
                    o = COL[name][0] - base
                    src = a[name]
                    while len(src.shape) > 1 and src.shape[0] == 1:
                        src = src[0]
                    if len(src.shape) == 2:
                        src = src.rearrange("l (r p) -> (l r) p", p=P)
                    else:
                        src = src.rearrange("(r p) -> r p", p=P)
                    sp.dma_start(rows[o:o + n, r, :], src).then_inc(rows_in, 16)
            sp.dma_start(const[:, P:], a["consts"][:, P:]).then_inc(consts_in, 16)
            moe0, n_moe, per = SLAB_AT["moe", 0], 3 * NE, 12
            for (name, s), n in SLAB_AT.items():
                if (name, s) == ("qkv0", RING):
                    sp.wait_ge(G["flag_ready"], 1)
                    with sp.If(sp.value_load(flag[0:1, 0:1]) > 0):
                        with sp.Fori(0, NE) as e:
                            sp.wait_ge(d_used, e + 1)
                            for j in range(3):
                                src = expert_source(j, e)
                                sp.dma_start(dslab[j].rearrange("p (k n) -> p k n", k=src.shape[1]), src).then_inc(d_landed, 16)
                if name != "moe":
                    load(n, slab_source(name, s))
                elif s < MOE_RING or s >= n_moe - per + MOE_RING:
                    load(n, expert_source(s % 3, s // 3))
                elif s == MOE_RING:
                    with sp.Fori(0, NE // 4 - 1) as it:
                        for j in range(MOE_RING, MOE_RING + per):
                            what, before = slab_freed(moe0 + j - MOE_RING)
                            sp.wait_ge(what, it * len(TURN) + before)
                            src = expert_source(j % 3, it * 4 + j // 3)
                            sp.dma_start(view(moe0 + j, src.shape[1], src.shape[2]), src).then_inc(landed[SLOT_OF[moe0 + j]], 16)
            for i in range(4):
                q, tt = divmod(i, 2)
                moved(sp, "out", i)
                f = slice(512 * q, 512 * q + 512)
                sp.dma_start(out[0][tt * P:(tt + 1) * P, f], xtok[:, tt, f]).then_inc(G["out_stored"], 16)
            sp.wait_ge(G["out_stored"], 16 * 4)

        SMALLS = []

        @block.scalar
        def _(act):
            n_step = [0]

            def link(ins):
                n_step[0] += 1
                ins.then_inc(a_step, 1)
                act.wait_ge(a_step, n_step[0])

            def take(name, i):
                act.wait_ge(bank_full, BANK_AT[name, i] + 1)
                return bank_of(name, i)

            def free(ins):
                ins.then_inc(freed["A"], 1)

            def small(dst, src):
                act.dma_start(dst, src).then_inc(smalls_in, 16)
                SMALLS.append(1)

            act.wait_ge(tokens_in["x"], 16)
            small(w_lr[:, :, :], a["w_in"][0][:, 5632:5664].rearrange("(k p) n -> p k n", p=P))
            small(w_pool[:, :, :], a["pool_w"][0].rearrange("g c e -> c g e"))
            small(w_rt[:, :, 0:NG], a["router_grp_w"][0].rearrange("(k p) n -> p k n", p=P))
            small(w_rt[:, :, NG:], a["router_exp_w"][0].rearrange("(k p) n -> p k n", p=P))
            for d, name in enumerate("fb"):
                small(a2[0:RANK, d, :], a["gla_a2_" + name][0])
                small(a2[RANK:RANK + 1, d, :], a["gla_ab_" + name])
            small(rb[0:1, 0:NG], a["router_grp_b"])
            small(rb[0:1, NG:], a["router_exp_b"])

            def square(src, k):
                act.activation(sq, src, ACT.Square).then_inc(G["sq_ready"], 1)

            def squares(dst, ready):
                for i in range(4):
                    ready(i)
                    act.activation(dst[:, 2 * i:2 * i + 2, :], xT[:, 2 * i:2 * i + 2, :], ACT.Square).then_inc(G["sq_ready"], 1)

            def norm_std(k, eps):
                b = take("norm", k)
                ins = act.activation(std[:, :], b[:, 0:T], ACT.Sqrt, bias=oeps[:, eps:eps + 1], scale=1.0 / D)
                ins.then_inc(freed["A"], 1)

            def mod_rows(s):
                b = take("mod_rows", s)
                ins = act.activation(mod_row[:, s % 2, :], b, ACT.Copy)
                ins.then_inc(freed["A"], 1)

            def split_hi(h):
                if h >= len(HALVES):
                    return
                name, s, _ = HALVES[h]
                n = SLAB_AT[name, s]
                act.wait_ge(landed[SLOT_OF[n]], 16 * NTH[n])
                if h >= WB:
                    act.wait_ge(*finished(h - WB))
                raw, hi, _ = half_of(h)
                act.activation(hi, raw, ACT.Copy).then_inc(G["whi_ready"], 1)

            for i in range(4):
                tt, q = divmod(i, 2)
                b = take("x_tiles", i).rearrange("p (k t) -> p k t", k=4)
                ins = act.activation(xT[:, 4 * q:4 * q + 4, tt * P:(tt + 1) * P], b, ACT.Copy)
                ins.then_inc(freed["A"], 1)
            act.wait_ge(G["eps_ready"], 1)
            moved(act, "c_tiles", 3)
            square(cT, 0)
            norm_std(0, 0)
            moved(act, "vectors", 0)
            act.wait_ge(G["scol_zero"], 1)
            act.activation(scol[:, :, 0:2], cols[:, 0:2 * KT].rearrange("p (r k) -> p k r", r=2), ACT.Silu).then_inc(G["scol_ready"], 1)
            act.wait_ge(bank_full, BANK_AT["norm", 0] + 1)
            moved(act, "x_tiles", 3)
            square(xT, 1)
            act.wait_ge(G["rstd_read"], 1)
            norm_std(1, 0)
            for s in range(4):
                mod_rows(s)
            act.wait_ge(G["lr_ones"], 1)
            for i in range(2):
                b = take("lr", i)
                ins = act.activation(lrT[0:RANK, 2 * i:2 * i + 2, :], b[0:RANK, :].rearrange("p (d t) -> p d t", d=2), ACT.Copy)
                ins.then_inc(freed["A"], 1)
            for half in range(2):
                for i in range(4):
                    act.activation(ez[half][:, i, :], take("z", 4 * half + i), ACT.Abs).then_inc(G["abs_ready"], 1)
                act.wait_ge(G["abs_ready"], 4 * half + 4)
                link(act.activation(ez[half], ez[half], ACT.Exp, scale=-1.0))
                act.activation(ez[half], ez[half], ACT.Ln, bias=1.0).then_inc(G["ez_ready"], 1)
            for i in range(4):
                d, hp = divmod(i, 2)
                b = take("cum", i).rearrange("p (h t) -> p h t", h=2)
                act.activation(dec[:, 0, d, 2 * hp:2 * hp + 2, :], b, ACT.Exp)
                ins = act.activation(dec[:, 1, d, 2 * hp:2 * hp + 2, :], b, ACT.Exp, scale=-1.0)
                ins.then_inc(freed["A"], 1)
            for name, dst in (("remx", remx), ("remc", remc)):
                for i in range(4):
                    d, tt = divmod(i, 2)
                    ins = act.activation(dst[:, d, tt, :], take(name, i), ACT.Exp)
                    ins.then_inc(freed["A"], 1)
            for s in range(2):
                for i in range(4):
                    dst = (vx, vc)[i // 2]
                    ins = act.activation(dst[:, i % 2, 512 * s:512 * s + 512], take("v", 4 * s + i), ACT.Copy)
                    ins.then_inc(freed["A"], 1)
            act.activation(hhi, hT, ACT.Copy).then_inc(G["hhi_ready"], 1)
            for h in range(NH):
                b = take("s0", h).rearrange("p (d v) -> p d v", d=2)
                if h:
                    act.wait_ge(bank_full, BANK_AT["o", h - 1] + 1)
                act.activation(S[:, 0, 0, :], b[:, 0, :], ACT.Copy)
                ins = act.activation(S[:, 1, NCH - 1, :], b[:, 1, :], ACT.Copy)
                ins.then_inc(freed["A"], 1)
                b = take("o", h).rearrange("p (a v) -> p a v", a=TT)
                ins = act.activation(otok[:, :, h * HV:(h + 1) * HV], b, ACT.Copy)
                ins.then_inc(freed["A"], 1)
                moved(act, "o", h)
                for tt in range(TT):
                    link(act.activation(osq, otok[:, tt, h * HV:(h + 1) * HV], ACT.Square, accum_out=oss[:, tt, h:h + 1]))
            act.activation(orstd[:, :, :], oss[:, :, :], ACT.Sqrt, bias=oeps[:, 0:1], scale=1.0 / HV).then_inc(G["ostd_ready"], 1)
            for i in range(2):
                ins = act.activation(utok[:, i, :], take("u", i), ACT.Copy)
                ins.then_inc(freed["A"], 1)
                split_hi(i)
            for i in range(4):
                if i % 2 == 0:
                    mod_rows(4 + i // 2)
                b = take("g", i)
                split_hi(i + WB)
                ins = act.activation(gT[:, 2 * i:2 * i + 2, :], b.rearrange("p (k t) -> p k t", k=2), ACT.Silu)
                ins.then_inc(freed["A"], 1)
            mod_rows(6)
            for i in range(8):
                b = take("gate", i)
                split_hi(4 + i + WB)
                ins = act.activation(gates[:, 2 * i:2 * i + 2, :], b.rearrange("p (k t) -> p k t", k=2), ACT.Sigmoid)
                ins.then_inc(freed["A"], 1)
                if i % 2:
                    mod_rows(7 + i // 2)
                if i == 1:
                    moved(act, "oT", 3)
                    act.activation(ghi, gT, ACT.Copy).then_inc(G["ghi_ready"], 1)
            mod_rows(11)
            for i in range(4):
                split_hi(12 + i + WB)
                act.wait_ge(G["z_ready"], i + 1)
                v = slice(2 * i, 2 * i + 2)
                act.activation(zhi[:, v, :], sq[:, v, :], ACT.Copy).then_inc(G["zhi_ready"], 1)
            for h in range(16 + WB, MIXER_HALVES):
                split_hi(h)
            squares(sq2, lambda i: moved(act, "mix", i))
            norm_std(2, 0)
            act.wait_ge(G["lg_diff"], 1)
            act.activation(r4[:, 1, :, :], r4[:, 0, :, :], ACT.Exp).then_inc(G["rexp_ready"], 1)
            act.wait_ge(G["lg_diff"], 2)
            act.activation(r1[:, 6, :], r1[:, 5, :], ACT.Exp).then_inc(G["rexp_ready"], 1)
            for i in range(4):
                tt, q = divmod(i, 2)
                act.activation(ttok[:, tt, 512 * q:512 * q + 512], take("ttok", i), ACT.Copy).then_inc(freed["A"], 1)
            with act.Fori(0, TURNS) as it:
                def out_of(kind, j, dst, b, func=ACT.Copy):
                    act.wait_ge(bank_full, turn_full(it, kind, j))
                    act.activation(dst, b, func).then_inc(freed["A"], 1)

                out_of("x", 0, xs[:, 0:4, :, :], turn_bank("x", 0).rearrange("p (k j s) -> p k j s", k=4, j=EXPERTS_PER_TURN))
                out_of("w", 0, putT[:, 0:2, :], turn_bank("w", 0).rearrange("p (j t) -> p j t", j=2))
                for j in range(EXPERTS_PER_TURN):
                    out_of("up1", j, h1, turn_bank("up1", j))
                    out_of("t1", j, s1, turn_bank("t1", j).rearrange("p (k s) -> p k s", k=4)[:, :, 0:SLOTS], ACT.Silu)
                    out_of("down0", j, ys[:, 0:512], turn_bank("down0", j))
            act.wait_ge(G["flag_ready"], 1)
            with act.If(act.value_load(flag[0:1, 0:1]) > 0):
                with act.Fori(0, NE) as e:
                    act.wait_ge(d_full, e * 5 + 1)
                    act.activation(dcomb, d_bank(0)[:, 0:T], ACT.Copy).then_inc(d_act, 1)
                    for i in range(2):
                        act.wait_ge(d_full, e * 5 + (2 + 2 * i))
                        act.activation(dsilu[:, 2 * i:2 * i + 2, :], d_bank(1 + 2 * i).rearrange("p (k t) -> p k t", k=2), ACT.Silu).then_inc(d_act, 1)
            def x_high(k):
                for i in range(4):
                    act.wait_ge(G["h_ready"], KT * k + 2 * i + 2)
                    act.activation(xhi[:, 2 * i:2 * i + 2, :], xT[:, 2 * i:2 * i + 2, :], ACT.Copy).then_inc(G["xhi_ready"], 1)

            squares(sq, lambda i: act.wait_ge(G["acc_out"], i + 1))
            split_hi(MIXER_HALVES)
            norm_std(3, 0)
            x_high(3)
            split_hi(MIXER_HALVES + 1)
            for l in range(2):
                nt, nv = (8, 4) if l == 0 else (6, 3)
                h0 = HALF_AT[f"qkv{l}", 0, 0]
                if l:
                    act.wait_ge(*finished(HALF_AT["ff_out0", FF // 512 - 1, 1]))
                act.dma_start(masks[:, 0:(1, 3)[l], :], a["masks"][:, (0, 1)[l]:(1, 4)[l], :]).then_inc(masks_in, 16)
                for i in range(nt):
                    b = take(f"qk{l}", i).rearrange("p (k t) -> p k t", k=2)
                    split_hi(h0 + i + WB)
                    act.activation(qk_raw[:, 2 * i:2 * i + 2, :], b, ACT.Copy).then_inc(freed["A"], 1)
                def value(i):
                    b = take(f"val{l}", i).rearrange("p (a n) -> p a n", a=TT)
                    act.activation(vt[:, :, 256 * i:256 * i + 256], b, ACT.Copy).then_inc(freed["A"], 1)

                for i in range(nv - 1):
                    if i < nv - WB:
                        split_hi(h0 + nt + i + WB)
                    value(i)
                sets = SETS[l]
                k0 = 0 if l == 0 else len(SETS[0])

                def exps(i):
                    k = k0 + i
                    act.wait_ge(G["max_ready"], k + 1)
                    s_ = sc[:, k % 2, 0:len(sets[i]), :]
                    act.activation(s_[:, :, 0:P], s_[:, :, 0:P], ACT.Exp, scale=HD ** -0.5, bias=mx[:, k % 2, 0:1],
                                   accum_out=ssum[:, k % 2, 0:1])
                    act.activation(s_[:, :, P:SC_W], s_[:, :, P:SC_W], ACT.Exp, scale=HD ** -0.5, bias=mx[:, k % 2, 1:2],
                                   accum_out=ssum[:, k % 2, 1:2]).then_inc(G["exp_ready"], 1)

                n = len(sets)
                for t in range(n + 2):
                    if 1 <= t <= n:
                        for j in range(len(sets[0])):
                            act.activation(pT_of(l, t - 1, j), take(f"pt{l}", (t - 1, j))[:, 0:SC_W], ACT.Copy).then_inc(freed["A"], 1)
                    if t >= 2:
                        for j, h in enumerate(sets[t - 2]):
                            o = HD * (h % 2)
                            b = take(f"pv{l}", (t - 2, j))
                            act.activation(atthi[o:o + HD, h // 2, :], b[o:o + HD, 0:T], ACT.Copy).then_inc(G["atthi_ready"], 1)
                    if t < n:
                        exps(t)
                    else:
                        split_hi(h0 + nt + nv + t - n)
                    if t == 0:
                        value(nv - 1)
                h1_ = h0 + nt + nv
                for i in range(4 - 1):
                    split_hi(h1_ + i + WB)
                for half in range(2):
                    def centred_ready(i):
                        if i < 3:
                            act.wait_ge(G["cen_ready"], 3 * (2 * l + half) + i + 1)
                        else:
                            moved(act, "mean", 2 * l + half)

                    squares(sq, centred_ready)
                    h_next = HALF_AT[f"ff_in{l}", 0, 0] if half == 0 else HALF_AT.get(("qkv1", 0, 0), 0) if l == 0 else len(HALVES)
                    norm_std(4 + 2 * l + half, 1)
                    if (l, half) != (1, 1):
                        x_high(4 + 2 * l + half)
                    split_hi(h_next + 1)
                    if half == 0:
                        hf = HALF_AT[f"ff_in{l}", 0, 0]
                        for i in range(FF // 256):
                            b = take(f"ff{l}", i)
                            split_hi(hf + i + WB)
                            if i >= 2:
                                act.wait_ge(G["ff_ready"], (FF // 256) * l + i - 1)
                            act.activation(hsq[:, i % 2, :], b, ACT.Relu).then_inc(freed["A"], 1)
                        for i in range(FF // 256 - 1):
                            split_hi(hf + FF // 256 + i + WB)
            for i in range(4):
                q, tt = divmod(i, 2)
                ins = act.activation(xtok[:, tt, 512 * q:512 * q + 512], take("out", i), ACT.Copy)
                ins.then_inc(freed["A"], 1)

        NSM = len(SMALLS)

        @block.vector
        def _(dve):
            n_step = [0]

            def link(ins):
                n_step[0] += 1
                ins.then_inc(v_step, 1)
                dve.wait_ge(v_step, n_step[0])

            def take(name, i):
                dve.wait_ge(bank_full, BANK_AT[name, i] + 1)
                return bank_of(name, i)

            def split_lo(h):
                if h >= len(HALVES):
                    return
                raw, hi, lo = half_of(h)
                dve.wait_ge(G["whi_ready"], h + 1)
                dve.tensor_tensor(lo, raw, hi.bitcast(F32), ALU.subtract).then_inc(G["split_ready"], 1)

            dve.memset(lrT[:, :, :], 1.0).then_inc(G["lr_ones"], 1)
            dve.memset(scol[:, :, :], 0.0).then_inc(G["scol_zero"], 1)
            dve.memset(oeps[:, 0:1], EPS)
            dve.memset(oeps[:, 1:2], LN_EPS).then_inc(G["eps_ready"], 1)
            def col(name, k, n=1):
                o = COL[name][0] + k
                return cols[:, o:o + n]

            for i in range(4):
                tt, q = divmod(i, 2)
                b = take("c_tiles", i).rearrange("p (k t) -> p k t", k=4)
                ins = dve.tensor_copy(cT[:, 4 * q:4 * q + 4, tt * P:(tt + 1) * P], b)
                ins.then_inc(freed["V"], 1)

            b = take("vectors", 0)
            dve.tensor_copy(cols[:, :], b[:, 0:NVEC + NLN]).then_inc(freed["V"], 1)
            moved(dve, "vectors", 0)

            def mod_cols(s):
                b = take("mod_cols", s)
                ins = dve.tensor_tensor(mod[:, 4 * s:4 * s + 4, :], b[:, 0:8].rearrange("p (k r) -> p k r", r=2),
                                        col("b_mod", 4 * s, 4).unsqueeze(2).to_broadcast([P, 4, 2]), ALU.add)
                ins.then_inc(freed["V"], 1)

            def gain(k, name, chunk, r):
                dve.scalar_tensor_tensor(scale1[:, k, :], mod[:, KT * chunk:KT * chunk + KT, r], 1.0, col(name, 0, KT),
                                         ALU.add, ALU.mult).then_inc(v_step, 1)
                n_step[0] += 1

            def normed(k, src, dst):
                moved(dve, "norm", k)
                link(dve.reciprocal(std[:, :], std[:, :]))
                link(dve.tensor_tensor(dst, src, std[:, :].unsqueeze(1).to_broadcast([P, KT, T]), ALU.mult))

            def affine(src, dst, scale, shift):
                for kt in range(KT):
                    dve.tensor_scalar(dst[:, kt, :], src[:, kt, :], scale(kt), shift(kt), ALU.mult, ALU.add).then_inc(G["h_ready"], 1)

            moved(dve, "c_tiles", 3)
            normed(0, cT, cT)
            dve.sem_inc(G["rstd_read"], 1)
            normed(1, xT, sq)
            for s in range(4):
                mod_cols(s)
            moved(dve, "mod_cols", 3)
            gain(0, "norm1_g", 1, 0)
            gain(1, "norm1_g", 1, 1)
            dve.wait_ge(v_step, n_step[0])
            affine(sq, hT, lambda kt: scale1[:, 0, kt:kt + 1], lambda kt: mod[:, kt, 0:1])
            affine(cT, cT, lambda kt: scale1[:, 1, kt:kt + 1], lambda kt: mod[:, kt, 1:2])

            for i in range(8):
                b = take("z", i)
                dve.wait_ge(G["abs_ready"], i + 1)
                dve.tensor_scalar(L[:, i, :], b, 0.0, None, ALU.min).then_inc(freed["V"], 1)
            for half in range(2):
                moved(dve, "z", 4 * half + 3)
                dve.wait_ge(G["ez_ready"], half + 1)
                for st in (2 * half, 2 * half + 1):
                    v = L[:, 2 * st:2 * st + 2, :]
                    dve.tensor_tensor(v, v, ez[half][:, 2 * (st % 2):2 * (st % 2) + 2, :], ALU.subtract).then_inc(G["L_ready"], 1)
            for i in range(2):
                ins = dve.tensor_copy(kT[:, 2 * i:2 * i + 2, :], take("kT", i).rearrange("p (h t) -> p h t", h=2))
                ins.then_inc(freed["V"], 1)
            moved(dve, "kT", 1)
            moved(dve, "cum", 3)
            for d in range(2):
                o = CH - 1 if d == 0 else 0
                dve.tensor_copy(decay[:, d, :, :], dec[:, 0, d, :, :].rearrange("p h (n t) -> p h n t", n=NCH)[:, :, :, o])
                link(dve.tensor_tensor(dec[:, 1, d, :, :], dec[:, 1, d, :, :], kT, ALU.mult))
            for i in range(2):
                b = take("kc", i)
                moved(dve, "remc", 3)
                link(dve.tensor_tensor(remc[:, 0, i, :], remc[:, 0, i, :], b, ALU.mult))
                ins = dve.tensor_tensor(remc[:, 1, i, :], remc[:, 1, i, :], b, ALU.mult)
                ins.then_inc(freed["V"], 1)
            for i in range(2):
                b = take("ktok", i)
                moved(dve, "remx", 3)
                link(dve.tensor_tensor(remx[:, 0, i, :], remx[:, 0, i, :], b, ALU.mult))
                ins = dve.tensor_tensor(remx[:, 1, i, :], remx[:, 1, i, :], b, ALU.mult)
                ins.then_inc(freed["V"], 1)
            for i in range(2):
                b = take("qT", i).rearrange("p (h t) -> p h t", h=2)
                for d in range(2):
                    v = dec[:, 0, d, 2 * i:2 * i + 2, :]
                    ins = dve.scalar_tensor_tensor(v, b, float(np.float32(P ** -0.5)), v, ALU.mult, ALU.mult)
                ins.then_inc(freed["V"], 1)
            moved(dve, "ktok", 1)
            dve.wait_ge(bank_full, BANK_AT["remc", 3] + 1)
            link(dve.memset(sTm, 0.0))
            dve.wait_ge(G["hhi_ready"], 1)
            dve.tensor_tensor(hlo, hT, hhi.bitcast(F32), ALU.subtract).then_inc(G["hlo_ready"], 1)
            for h in range(NH):
                b = take("sT", h).rearrange("p (c i) -> p c i", c=4)
                if h:
                    dve.wait_ge(bank_full, BANK_AT["o", h - 1] + 1)
                for c in range(4):
                    m = C("cum_f" if c < 2 else "cum_b").bitcast(U32)
                    ins = dve.copy_predicated(sTm[:, c, :], m, b[:, c, :])
                ins.then_inc(freed["V"], 1)
                moved(dve, "s0", h)
                for n in range(NCH - 1):
                    f, r = n, NCH - 1 - n
                    for d, c, to in ((0, f, f + 1), (1, r, r - 1)):
                        b = take("kv", (h, n, d))[:, 0:HV]
                        if n:
                            moved(dve, "kv", (h, n - 1, d))
                        ins = dve.scalar_tensor_tensor(S[:, d, to, :], S[:, d, c, :], decay[:, d, h, c:c + 1], b, ALU.mult, ALU.add)
                        ins.then_inc(freed["V"], 1)
            dve.wait_ge(G["ostd_ready"], 1)
            link(dve.reciprocal(orstd[:, :, :], orstd[:, :, :]))
            for tt in range(TT):
                v = otok[:, tt, :].rearrange("p (h v) -> p h v", h=NH)
                dve.tensor_tensor(v, v, orstd[:, tt, :].unsqueeze(2).to_broadcast([P, NH, HV]), ALU.mult).then_inc(G["on_ready"], 1)
            for i in range(2):
                split_lo(i)
            for i in range(2):
                ins = dve.tensor_copy(pooled[:, 2 * i:2 * i + 2, :], take("pool", i).rearrange("p (g t) -> p g t", g=2))
                ins.then_inc(freed["V"], 1)
            for i in range(2):
                b = take("y1", i).rearrange("p (g t) -> p g t", g=2)
                dve.tensor_scalar(y1[:, 2 * i, :], b[:, 0, :], col("pool_scale", 2 * i), None, ALU.mult)
                ins = dve.tensor_scalar(y1[:, 2 * i + 1, :], b[:, 1, :], col("pool_scale", 2 * i + 1), None, ALU.mult)
                ins.then_inc(freed["V"], 1)
            for s in range(4, 6):
                split_lo(2 * (s - 4) + WB)
                mod_cols(s)
                split_lo(2 * (s - 4) + WB + 1)
            for i in range(4):
                if i == 2:
                    mod_cols(6)
                tt, q = divmod(i, 2)
                b = take("oT", i).rearrange("p (k r t) -> p k r t", k=2, r=2)
                moved(dve, "g", 3)
                for r in range(2):
                    v = gT[:, 4 * q:4 * q + 4, tt * P:(tt + 1) * P].rearrange("p (k r) t -> p k r t", r=2)[:, :, r, :]
                    ins = dve.scalar_tensor_tensor(v, b[:, :, r, :], col("gla_onorm_g", r), v, ALU.mult, ALU.mult)
                ins.then_inc(freed["V"], 1)
            for s in range(7, 11):
                split_lo(4 + 2 * (s - 7) + WB)
                if s > 7:
                    mod_cols(s - 1)
                split_lo(4 + 2 * (s - 7) + 1 + WB)
                if s == 7:
                    dve.wait_ge(G["ghi_ready"], 1)
                    dve.tensor_tensor(glo, gT, ghi.bitcast(F32), ALU.subtract).then_inc(G["glo_ready"], 1)
            moved(dve, "mod_cols", 9)
            gain(2, "norm2_g", 4, 0)
            moved(dve, "gate", 7)
            for i in range(4):
                b = take("ypool", i).rearrange("p (k t) -> p k t", k=2)
                ins = dve.tensor_tensor(sq[:, 2 * i:2 * i + 2, :], b, gates[:, 2 * i:2 * i + 2, :], ALU.mult)
                ins.then_inc(freed["V"], 1)
                if i == 0:
                    mod_cols(10)

            def z_low(i):
                dve.wait_ge(G["zhi_ready"], i + 1)
                v = slice(2 * i, 2 * i + 2)
                dve.tensor_tensor(zlo[:, v, :], sq[:, v, :], zhi[:, v, :].bitcast(F32), ALU.subtract).then_inc(G["zlo_ready"], 1)

            for i in range(4):
                b = take("ygla", i).rearrange("p (k t) -> p k t", k=2)
                split_lo(12 + i + WB)
                v = gates[:, KT + 2 * i:KT + 2 * i + 2, :]
                ins = dve.tensor_tensor(v, b, v, ALU.mult)
                ins.then_inc(freed["V"], 1)
                moved(dve, "ygla", i)
                z = sq[:, 2 * i:2 * i + 2, :]
                dve.tensor_tensor(z, z, v, ALU.add).then_inc(G["z_ready"], 1)
                if i == 0:
                    mod_cols(11)
                else:
                    z_low(i - 1)
            z_low(3)
            for i in range(4):
                b = take("mix", i).rearrange("p (k t) -> p k t", k=2)
                if i < WB:
                    split_lo(16 + i + WB)
                for r in range(2):
                    kt = 2 * i + r
                    ins = dve.scalar_tensor_tensor(xT[:, kt, :], b[:, r, :], mod[:, 2 * KT + kt, 0:1], xT[:, kt, :], ALU.mult, ALU.add)
                ins.then_inc(freed["V"], 1)
            moved(dve, "mix", 3)
            normed(2, xT, sq)
            affine(sq, hT, lambda kt: scale1[:, 2, kt:kt + 1], lambda kt: mod[:, 3 * KT + kt, 0:1])

            b = take("router", 0)[:, 0:TT * (NG + NE)].rearrange("p (a n) -> p a n", a=TT)
            ins = dve.tensor_copy(lg[:, :, :], b)
            ins.then_inc(freed["V"], 1)
            moved(dve, "router", 0)

            def bc(ap, n):
                return ap.unsqueeze(2).to_broadcast([P, TT, n])

            def first_max(vals, n, m, eq, key, km):
                link(dve.tensor_reduce(m, vals, AX.X, ALU.max))
                link(dve.tensor_tensor(eq, vals, bc(m, n), ALU.is_equal))
                d = C(f"desc{n}").unsqueeze(1).to_broadcast([P, TT, n])
                link(dve.tensor_tensor(key, eq, d, ALU.mult))
                link(dve.tensor_reduce(km, key, AX.X, ALU.max))
                link(dve.tensor_tensor(eq, d, bc(km, n), ALU.is_equal))

            lgg = lg[:, :, 0:NG]
            first_max(lgg, NG, r1[:, 0, :], r4[:, 2, :, :], r4[:, 3, :, :], r1[:, 1, :])
            dve.tensor_tensor(r4[:, 0, :, :], lgg, bc(r1[:, 0, :], NG), ALU.subtract).then_inc(G["lg_diff"], 1)
            grp = r4[:, 2, :, :]
            lge = lg[:, :, NG:].rearrange("p a (g e) -> p a g e", g=NG)
            for tt in range(TT):
                link(dve.tensor_tensor(r32[:, tt, :, :], lge[:, tt, :, :], grp[:, tt, :].unsqueeze(2).to_broadcast([P, NG, EG]), ALU.mult))
            ing = r8[:, 0, :, :]
            for tt in range(TT):
                link(dve.tensor_reduce(ing[:, tt, :], r32[:, tt, :, :].rearrange("p g e -> p e g"), AX.X, ALU.add))
            one, two = r8[:, 1, :, :], r8[:, 2, :, :]

            def by_group(dst, tt, in_group, then):
                dve.tensor_tensor(dst[:, tt, :].rearrange("p (g e) -> p g e", g=NG), in_group[:, tt, :].unsqueeze(1).to_broadcast([P, NG, EG]),
                                  grp[:, tt, :].unsqueeze(2).to_broadcast([P, NG, EG]), ALU.mult).then_inc(then, 1)

            first_max(ing, EG, r1[:, 2, :], one, r8[:, 3, :, :], r1[:, 3, :])
            link(dve.scalar_tensor_tensor(r8[:, 4, :, :], one, -3.0e38, ing, ALU.mult, ALU.add))
            first_max(r8[:, 4, :, :], EG, r1[:, 4, :], two, r8[:, 3, :, :], r1[:, 3, :])
            dve.tensor_tensor(r1[:, 5, :], r1[:, 4, :], r1[:, 2, :], ALU.subtract).then_inc(G["lg_diff"], 1)
            both = r8[:, 5, :, :]
            link(dve.tensor_tensor(both, one, two, ALU.add))
            link(dve.tensor_scalar(both, both, GATE_NORM, None, ALU.mult))
            for tt in range(TT):
                by_group(chosen, tt, both, G["chosen_ready"])
            dve.wait_ge(G["rexp_ready"], 2)
            link(dve.tensor_reduce(r1[:, 7, :], r4[:, 1, :, :], AX.X, ALU.add))
            link(dve.scalar_tensor_tensor(r1[:, 8, :], r1[:, 6, :], 1.0, r1[:, 7, :], ALU.add, ALU.mult))
            link(dve.reciprocal(r1[:, 9, :], r1[:, 8, :]))
            link(dve.tensor_tensor(r1[:, 10, :], r1[:, 9, :], r1[:, 6, :], ALU.mult))
            link(dve.tensor_tensor(one, one, bc(r1[:, 9, :], EG), ALU.mult))
            link(dve.tensor_tensor(two, two, bc(r1[:, 10, :], EG), ALU.mult))
            link(dve.tensor_tensor(one, one, two, ALU.add))
            for tt in range(TT):
                by_group(comb, tt, one, G["comb_ready"])
            b = take("rank", 0)
            rank = b[:, 0:TT * NE].rearrange("p (a e) -> p a e", a=TT)
            dve.wait_ge(G["chosen_ready"], 2)
            dve.wait_ge(G["comb_ready"], 2)
            link(dve.tensor_reduce(n_over[:, 0:1], b[:, TT * NE:(TT + 1) * NE], AX.X, ALU.max))
            link(dve.tensor_scalar(chosen[:, :, :], chosen[:, :, :], 1.0 / GATE_NORM, None, ALU.mult))
            ins = dve.scalar_tensor_tensor(pos[:, :, :], rank, 1.0, chosen[:, :, :], ALU.add, ALU.mult)
            ins.then_inc(freed["V"], 1)
            moved(dve, "rank", 0)
            link(dve.tensor_scalar(pos[:, :, :], pos[:, :, :], 1.0, None, ALU.subtract))
            link(dve.tensor_scalar(over[:, :, :], pos[:, :, :], float(CAP), None, ALU.is_ge))
            link(dve.scalar_tensor_tensor(pos[:, :, :], over[:, :, :], -float(2 * T), pos[:, :, :], ALU.mult, ALU.add))
            link(dve.tensor_tensor(over[:, :, :], over[:, :, :], comb[:, :, :], ALU.mult))
            dve.tensor_scalar(flag[:, :], n_over[:, 0:1], float(CAP), None, ALU.is_gt).then_inc(G["flag_ready"], 1)
            slot_row = C("slot")
            with dve.Fori(0, TURNS) as it:
                for j in range(EXPERTS_PER_TURN):
                    for tt in range(TT):
                        e_ = bass.ds(it * EXPERTS_PER_TURN + j, 1)
                        dve.tensor_scalar(pick[:, tt, SLOTS * j:SLOTS * (j + 1)], slot_row[:, 0:SLOTS], pos[:, tt, e_], None,
                                          ALU.is_equal).then_inc(G["pick_ready"], 1)
                for j in range(EXPERTS_PER_TURN):
                    for tt in range(TT):
                        e_ = bass.ds(it * EXPERTS_PER_TURN + j, 1)
                        dve.tensor_scalar(put[:, j, tt, :], slot_row, pos[:, tt, e_], comb[:, tt, e_], ALU.is_equal,
                                          ALU.mult).then_inc(G["put_ready"], 1)

                def out_of(kind, j, dst, b):
                    dve.wait_ge(bank_full, turn_full(it, kind, j))
                    dve.tensor_copy(dst, b).then_inc(freed["V"], 1)

                out_of("x", 1, xs[:, 4:8, :, :], turn_bank("x", 1).rearrange("p (k j s) -> p k j s", k=4, j=EXPERTS_PER_TURN))
                out_of("w", 1, putT[:, 2:4, :], turn_bank("w", 1).rearrange("p (j t) -> p j t", j=2))
                for j in range(EXPERTS_PER_TURN):
                    out_of("up3", j, h3, turn_bank("up3", j))
                    dve.wait_ge(bank_full, turn_full(it, "t3", j))
                    turn_moved(dve, it, "t1", j)
                    b = turn_bank("t3", j).rearrange("p (k s) -> p k s", k=4)[:, :, 0:SLOTS]
                    dve.tensor_tensor(hidT, s1, b, ALU.mult).then_inc(freed["V"], 1)
                    out_of("down1", j, ys[:, 512:1024], turn_bank("down1", j))
            dve.wait_ge(used, OPENED + NE)
            dve.wait_ge(G["flag_ready"], 1)
            with dve.If(dve.value_load(flag[0:1, 0:1]) > 0):
                dve.sem_inc(d_used, 1)
                with dve.Fori(0, NE) as e:
                    dve.wait_ge(d_used, e + 1)
                    dve.tensor_copy(dcol, over[:, :, bass.ds(e, 1)].to_broadcast([P, TT, P])).then_inc(G["dcol_ready"], 1)
                    for i in range(2):
                        dve.wait_ge(d_act, e * 3 + (2 + i))
                        v = dsilu[:, 2 * i:2 * i + 2, :]
                        dve.tensor_tensor(v, v, dcomb.unsqueeze(1).to_broadcast([P, 2, T]), ALU.mult).then_inc(G["dsilu_scaled"], 1)
                        dve.wait_ge(G["dsilu_scaled"], e * 2 + (i + 1))
                        dve.wait_ge(d_full, e * 5 + (3 + 2 * i))
                        b = d_bank(2 + 2 * i).rearrange("p (k t) -> p k t", k=2)
                        dve.tensor_tensor(dhid[:, 2 * i:2 * i + 2, :], v, b, ALU.mult).then_inc(d_vec, 1)
                dve.wait_ge(d_used, NE + 1)
            for i in range(4):
                for kt in (2 * i, 2 * i + 1):
                    ins = dve.scalar_tensor_tensor(xT[:, kt, :], acc[:, kt, :], mod[:, 5 * KT + kt, 0:1], xT[:, kt, :], ALU.mult, ALU.add)
                ins.then_inc(G["acc_out"], 1)

            def normed_pairs(k, scale, shift, split=True):
                moved(dve, "norm", k)
                link(dve.reciprocal(std[:, :], std[:, :]))

                def product(i):
                    v = slice(2 * i, 2 * i + 2)
                    dve.tensor_tensor(sq[:, v, :], xT[:, v, :], std[:, :].unsqueeze(1).to_broadcast([P, 2, T]), ALU.mult).then_inc(v_step, 1)
                    n_step[0] += 1
                    return n_step[0]

                def affine(i, step):
                    dve.wait_ge(v_step, step)
                    for kt in (2 * i, 2 * i + 1):
                        if shift is None:
                            ins = dve.tensor_scalar(xT[:, kt, :], sq[:, kt, :], scale(kt), None, ALU.mult)
                        else:
                            ins = dve.tensor_scalar(xT[:, kt, :], sq[:, kt, :], scale(kt), shift(kt), ALU.mult, ALU.add)
                        ins.then_inc(G["h_ready"], 1)

                def low(i):
                    dve.wait_ge(G["xhi_ready"], 4 * (k - 3) + i + 1)
                    v = slice(2 * i, 2 * i + 2)
                    dve.tensor_tensor(xlo[:, v, :], xT[:, v, :], xhi[:, v, :].bitcast(F32), ALU.subtract).then_inc(G["xlo_ready"], 1)

                steps = [product(0), product(1)]
                affine(0, steps[0])
                affine(1, steps[1])
                for i in range(2, 4):
                    steps.append(product(i))
                    if split:
                        low(i - 2)
                    affine(i, steps[i])
                if split:
                    low(2)
                    low(3)
                dve.wait_ge(G["h_ready"], KT * (k + 1))

            split_lo(MIXER_HALVES)
            normed_pairs(3, lambda kt: col("final_norm_g", kt), None)
            split_lo(MIXER_HALVES + 1)

            def centred(k):
                b = take("mean", k)[:, 0:T].unsqueeze(1).to_broadcast([P, 2, T])
                for i in range(4):
                    v = xT[:, 2 * i:2 * i + 2, :]
                    ins = dve.scalar_tensor_tensor(v, b, -1.0 / D, v, ALU.mult, ALU.add)
                    if i < 3:
                        ins.then_inc(G["cen_ready"], 1)
                ins.then_inc(freed["V"], 1)

            for l in range(2):
                nt, nv = (8, 4) if l == 0 else (6, 3)
                h0 = HALF_AT[f"qkv{l}", 0, 0]
                ct, st = (C(n).unsqueeze(1).to_broadcast([P, 2, T]) for n in ("cos", "sin"))

                def rotary(i):
                    b = take(f"rot{l}", i).rearrange("p (k t) -> p k t", k=2)
                    r_, q_ = qk_raw[:, 2 * i:2 * i + 2, :], qk[:, 2 * i:2 * i + 2, :]
                    dve.tensor_tensor(r_, r_, ct, ALU.mult)
                    ins = dve.tensor_tensor(q_, b, st, ALU.mult)
                    ins.then_inc(freed["V"], 1)
                    moved(dve, f"rot{l}", i)
                    dve.tensor_tensor(q_, q_, r_, ALU.add).then_inc(G["rot_ready"], 1)

                for i in range(nt):
                    split_lo(h0 + i + WB)
                    if i:
                        rotary(i - 1)
                for i in range(nv - WB):
                    split_lo(h0 + nt + i + WB)
                    if i == 0:
                        rotary(nt - 1)
                sets = SETS[l]
                k0 = 0 if l == 0 else len(SETS[0])
                dve.wait_ge(masks_in, 16 * (l + 1))

                def maxes(i):
                    k = k0 + i
                    n = len(sets[i])
                    s_ = sc[:, k % 2, 0:n, :]
                    for j in range(n):
                        b = take(f"sc{l}", (i, j))[:, 0:SC_W]
                        if k >= 2 and j == 0:
                            moved(dve, *last_pt(k - 2))
                        ins = dve.tensor_tensor(s_[:, j, :], b, masks[:, j, :], ALU.add)
                        ins.then_inc(freed["V"], 1)
                    moved(dve, f"sc{l}", (i, n - 1))
                    dve.tensor_reduce(mx[:, k % 2, 0:1], s_[:, :, 0:P], AX.XY, ALU.max)
                    link(dve.tensor_reduce(mx[:, k % 2, 1:2], s_[:, :, P:SC_W], AX.XY, ALU.max))
                    dve.tensor_scalar(mx[:, k % 2, :], mx[:, k % 2, :], -(HD ** -0.5), None, ALU.mult).then_inc(G["max_ready"], 1)

                def probs(i):
                    k = k0 + i
                    n = len(sets[i])
                    s_ = sc[:, k % 2, 0:n, :]
                    dve.wait_ge(G["exp_ready"], k + 1)
                    link(dve.reciprocal(rsum[:, k % 2, :], ssum[:, k % 2, :]))
                    dve.tensor_scalar(s_[:, :, 0:P], s_[:, :, 0:P], rsum[:, k % 2, 0:1], None, ALU.mult)
                    dve.tensor_scalar(s_[:, :, P:SC_W], s_[:, :, P:SC_W], rsum[:, k % 2, 1:2], None, ALU.mult).then_inc(G["p_ready"], 1)

                def outputs(i):
                    for j, h in enumerate(sets[i]):
                        o = HD * (h % 2)
                        b = take(f"pv{l}", (i, j))
                        dve.wait_ge(G["atthi_ready"], (0 if l == 0 else MOBA_H) + len(sets[0]) * i + j + 1)
                        v = slice(o, o + HD)
                        dve.tensor_tensor(attlo[v, h // 2, :], b[v, 0:T], atthi[v, h // 2, :].bitcast(F32), ALU.subtract).then_inc(freed["V"], 1)

                n = len(sets)
                for t in range(n + 2):
                    if 1 <= t <= n:
                        probs(t - 1)
                    if t < n:
                        maxes(t)
                    if t >= 2:
                        outputs(t - 2)
                    if t >= n:
                        split_lo(h0 + nt + nv + t - n)
                h1_ = h0 + nt + nv
                for i in range(4):
                    b = take(f"proj{l}", i).rearrange("p (k t) -> p k t", k=2)
                    if i < 4 - 1:
                        split_lo(h1_ + i + WB)
                    v = xT[:, 2 * i:2 * i + 2, :]
                    ins = dve.scalar_tensor_tensor(v, v, ALPHA, b, ALU.mult, ALU.add)
                    ins.then_inc(freed["V"], 1)
                moved(dve, f"proj{l}", 3)
                centred(2 * l)
                hf = HALF_AT[f"ff_in{l}", 0, 0]
                normed_pairs(4 + 2 * l, lambda kt: col("ln_mix_g_2", KT * l + kt), lambda kt: col("ln_mix_b_2", KT * l + kt))
                split_lo(hf + 1)
                for i in range(FF // 256):
                    split_lo(hf + i + WB)
                    moved(dve, f"ff{l}", i)
                    v = hsq[:, i % 2, :]
                    v3 = v.rearrange("p (k t) -> p k t", k=2)
                    link(dve.tensor_tensor(v, v, v, ALU.mult))
                    hi = hffhi[:, 2 * i:2 * i + 2, :]
                    link(dve.tensor_copy(hi, v3))
                    dve.tensor_tensor(hfflo(2 * i, 2), v3, hi.bitcast(F32), ALU.subtract).then_inc(G["ff_ready"], 1)
                for i in range(FF // 256 - 1):
                    split_lo(hf + FF // 256 + i + WB)
                for i in range(4):
                    if i < 3:
                        dve.wait_ge(G["acc_pair"], 3 * l + i + 1)
                    else:
                        dve.wait_ge(*finished(HALF_AT[f"ff_out{l}", FF // 512 - 1, 1]))
                    v = slice(2 * i, 2 * i + 2)
                    ins = dve.scalar_tensor_tensor(xT[:, v, :], xT[:, v, :], ALPHA, acc[:, v, :], ALU.mult, ALU.add)
                    ins.then_inc(G["acc_out"], 1)
                dve.wait_ge(G["acc_out"], 4 * (l + 2))
                centred(2 * l + 1)
                normed_pairs(5 + 2 * l, lambda kt: col("ln_mlp_g_2", KT * l + kt), lambda kt: col("ln_mlp_b_2", KT * l + kt), split=(l == 0))
                if l == 0:
                    split_lo(HALF_AT["qkv1", 0, 0] + 1)

        @block.tensor
        def _(pe):
            def bank(name, i):
                g = BANK_AT[name, i]
                if g >= RB:
                    pe.wait_ge(*freed_by(g - RB))
                return bank_of(name, i)

            def arrive(name, s, k, w):
                n = SLAB_AT[name, s]
                pe.wait_ge(landed[SLOT_OF[n]], 16 * NTH[n])
                return view(n, k, w)

            def full(ins):
                ins.then_inc(bank_full, 1)

            def done(ins):
                ins.then_inc(used, 1)

            def turn(name, i, src, tt, q):
                b = bank(name, i)
                for j in range(4):
                    kt = 4 * q + j
                    ins = pe.transpose(b[:, j * P:(j + 1) * P], src[:, tt, kt * P:(kt + 1) * P], ident)
                full(ins)

            def fmajor(b, w, x, m0, n, ks=KT):
                for j in range(n):
                    for kt in range(ks):
                        ins = pe.matmul(b[:, j * T:(j + 1) * T], w[:, kt, m0 + j * P:m0 + (j + 1) * P], x[:, kt, :],
                                        start=(kt == 0), stop=(kt == ks - 1))
                return ins

            def tmajor(b, w, x, tt, ks=KT, n=512):
                for kt in range(ks):
                    ins = pe.matmul(b[:, 0:n], x[:, kt, tt * P:(tt + 1) * P], w[:, kt, 0:n], start=(kt == 0), stop=(kt == ks - 1))
                return ins

            def sum_pairs(name, k, src, ready):
                b = bank(name, k)
                for kt in range(KT):
                    if kt % 2 == 0:
                        ready(kt // 2)
                    ins = pe.matmul(b[:, 0:T], ones, src[:, kt, :], start=(kt == 0), stop=(kt == KT - 1))
                full(ins)

            def squares_ready(k):
                return lambda i: pe.wait_ge(G["sq_ready"], 2 + 4 * (k - 2) + i + 1)

            def three(o, whi_, wlo_, xhi_, xlo_, first, last):
                pe.matmul(o, whi_, xhi_, start=first, stop=False, skip_group_check=True)
                pe.matmul(o, whi_, xlo_, start=False, stop=False, skip_group_check=True)
                return pe.matmul(o, wlo_, xhi_, start=False, stop=last, skip_group_check=True)

            def weights(h):
                pe.wait_ge(G["split_ready"], h + 1)
                return half_of(h)[1:]

            def f_half(b, h, hi, lo, ks=KT, ready=None):
                wh, wl = weights(h)
                for kt in range(ks):
                    if ready and kt % 2 == 0:
                        ready(kt)
                    for j in range(2):
                        m = slice(j * P, (j + 1) * P)
                        ins = three(b[:, j * T:(j + 1) * T], wh[:, kt, m], wl[:, kt, m], hi[:, kt, :], lo[:, kt, :],
                                    kt == 0 and j == 0, kt == ks - 1)
                full(ins)

            pe.wait_ge(ident_in, 16)
            pe.wait_ge(tokens_in["ctx"], 16)
            for i in range(4):
                turn("c_tiles", i, ctok, *divmod(i, 2))
            pe.wait_ge(tokens_in["x"], 16)
            for i in range(4):
                turn("x_tiles", i, xtok, *divmod(i, 2))
            pe.wait_ge(rows_in, 16 * (len(VEC_ROWS) + len(LN_ROWS)))
            b = bank("vectors", 0)
            pe.transpose(b[:, 0:NVEC], rows[0:NVEC, 0, :], ident[0:NVEC, 0:NVEC])
            full(pe.transpose(b[:, NVEC:NVEC + NLN], rows[0:NLN, 1, :], ident[0:NLN, 0:NLN]))
            pe.wait_ge(consts_in, 16)

            def mod_rows(s):
                if s == 0:
                    pe.wait_ge(G["scol_ready"], 1)
                w = arrive("mod", s, KT, 512)
                b = bank("mod_rows", s)
                for half in range(2):
                    for g in range(4):
                        kt = 4 * half + g
                        ins = pe.matmul(b[32 * g:32 * g + 32, :], scol[:, kt, :], w[:, kt, :], start=(half == 0), stop=(half == 1))
                full(ins)

            def mod_cols(s):
                moved(pe, "mod_rows", s)
                b = bank("mod_cols", s)
                for j in range(4):
                    ins = pe.matmul(b[:, 2 * j:2 * j + 2], mod_row[:, s % 2, j * P:(j + 1) * P], C("sel"), start=True, stop=True)
                full(ins)

            def norm_sum(name, k, src):
                b = bank(name, k)
                for kt in range(KT):
                    ins = pe.matmul(b[:, 0:T], ones, src[:, kt, :], start=(kt == 0), stop=(kt == KT - 1))
                full(ins)

            for k in range(2):
                pe.wait_ge(G["sq_ready"], k + 1)
                norm_sum("norm", k, sq)
            for s in range(4):
                mod_rows(s)
                if s:
                    mod_cols(s - 1)
            mod_cols(3)
            pe.wait_ge(smalls_in, 16 * NSM)
            for i, src in enumerate((hT, cT)):
                b = bank("lr", i)
                for d in range(2):
                    for kt in range(KT):
                        pe.wait_ge(G["h_ready"], KT * i + kt + 1)
                        ins = pe.matmul(b[0:RANK, d * T:(d + 1) * T], w_lr[:, kt, d * RANK:(d + 1) * RANK], src[:, kt, :],
                                        start=(kt == 0), stop=(kt == KT - 1))
                full(ins)
            moved(pe, "lr", 1)
            for i in range(8):
                st, tt = divmod(i, 2)
                d = st % 2
                b = bank("z", i)
                full(pe.matmul(b, lrT[:, st, tt * P:(tt + 1) * P], a2[:, d, :], start=True, stop=True))
            for i in range(4):
                d, hp = divmod(i, 2)
                pe.wait_ge(G["L_ready"], d + 1)
                b = bank("cum", i)
                for j in range(2):
                    for tt in range(TT):
                        h = 2 * hp + j
                        ins = pe.matmul(b[:, j * T + tt * P:j * T + (tt + 1) * P], L[:, 2 * d + tt, h * P:(h + 1) * P],
                                        C("cum_" + "fb"[d]), start=True, stop=True)
                full(ins)
            for i in range(4):
                d, tt = divmod(i, 2)
                full(pe.matmul(bank("remx", i), C("rem_" + "fb"[d]), L[:, 2 * d + tt, :], start=True, stop=True))
            pe.wait_ge(G["L_ready"], 4)
            for i in range(4):
                d, tt = divmod(i, 2)
                b = bank("remc", i)
                other = (d == 0 and tt == 0) or (d == 1 and tt == 1)
                ins = pe.matmul(b, C(("suf", "pre")[d]), L[:, 4 + 2 * d + tt, :], start=True, stop=not other)
                if other:
                    ins = pe.matmul(b, C("all"), L[:, 4 + 2 * d + 1 - tt, :], start=False, stop=True)
                full(ins)
            w = arrive("w_in", 2, KT, 512)
            for i in range(2):
                full(fmajor(bank("kT", i), w, hT, 2 * i * P, 2))
            for i in range(2):
                ins = tmajor(bank("kc", i), w, cT, i)
                full(ins)
            moved(pe, "kT", 1)
            for i in range(2):
                b = bank("ktok", i)
                for h in range(NH):
                    ins = pe.transpose(b[:, h * P:(h + 1) * P], kT[:, h, i * P:(i + 1) * P], ident)
                full(ins)
            for s in range(2):
                w = arrive("w_in", 3 + s, KT, 512)
                for i in range(4):
                    ins = tmajor(bank("v", 4 * s + i), w, (hT, cT)[i // 2], i % 2)
                    full(ins)
            w = arrive("w_in", 1, KT, 512)
            for i in range(2):
                ins = fmajor(bank("qT", i), w, hT, 2 * i * P, 2)
                full(ins)
            moved(pe, "v", 7)
            moved(pe, "ktok", 1)
            moved(pe, "qT", 1)
            for h in range(NH):
                hk, hv = slice(h * P, (h + 1) * P), slice(h * HV, (h + 1) * HV)
                b = bank("s0", h)
                for d in range(2):
                    for tt in range(TT):
                        ins = pe.matmul(b[:, d * HV:(d + 1) * HV], remc[:, d, tt, hk], vc[:, tt, hv], start=(tt == 0), stop=(tt == 1))
                full(ins)
                b = bank("sT", h)
                for d in range(2):
                    for tt in range(TT):
                        t_ = slice(tt * P, (tt + 1) * P)
                        ins = pe.matmul(b[:, (2 * d + tt) * P:(2 * d + tt + 1) * P], dec[:, 1, d, h, t_], dec[:, 0, d, h, t_],
                                        start=True, stop=True)
                full(ins)
                for n in range(NCH - 1):
                    for d in range(2):
                        c = n if d == 0 else NCH - 1 - n
                        tt, o = c // 2, CH * (c % 2)
                        b = bank("kv", (h, n, d))
                        full(pe.matmul(b[:, 0:HV], remx[o:o + CH, d, tt, hk], vx[o:o + CH, tt, hv], start=True, stop=True))
                moved(pe, "sT", h)
                moved(pe, "kv", (h, NCH - 2, 1))
                moved(pe, "s0", h)
                b = bank("o", h)
                for tt in range(TT):
                    bo = b[:, tt * HV:(tt + 1) * HV]
                    for d in range(2):
                        pe.matmul(bo, sTm[:, 2 * d + tt, :], vx[:, tt, hv], start=(d == 0), stop=False, skip_group_check=True)
                    for d in range(2):
                        for c in range(2):
                            n = 2 * tt + c
                            ins = pe.matmul(b[CH * c:CH * (c + 1), tt * HV:(tt + 1) * HV], dec[:, 0, d, h, n * CH:(n + 1) * CH],
                                            S[:, d, n, :], start=False, stop=(d == 1), skip_group_check=True)
                full(ins)
            w = arrive("w_in", 0, KT, 512)
            for i in range(2):
                ins = tmajor(bank("u", i), w, hT, i)
                full(ins)
            moved(pe, "u", 1)
            for i in range(2):
                b = bank("pool", i)
                for j in range(2):
                    g = 2 * i + j
                    for tt in range(TT):
                        ins = pe.matmul(b[:, j * T + tt * P:j * T + (tt + 1) * P], utok[:, tt, g * P:(g + 1) * P], C(f"pool{g}"),
                                        start=True, stop=True)
                full(ins)
            moved(pe, "pool", 1)
            for i in range(2):
                b = bank("y1", i)
                for j in range(2):
                    g = 2 * i + j
                    ins = pe.matmul(b[:, j * T:(j + 1) * T], w_pool[:, g, :], pooled[:, g, :], start=True, stop=True)
                full(ins)
            for s in range(2):
                mod_rows(4 + s)
                pe.wait_ge(G["hlo_ready"], 1)
                for i in range(2):
                    f_half(bank("g", 2 * s + i), 2 * s + i, hhi, hlo)
                    if i == 0:
                        mod_cols(4 + s)
            mod_rows(6)
            pe.wait_ge(G["on_ready"], 2)
            for i in range(4):
                turn("oT", i, otok, *divmod(i, 2))
                if i == 1:
                    mod_cols(6)
            for s in range(4):
                for i in range(2):
                    f_half(bank("gate", 2 * s + i), 4 + 2 * s + i, hhi, hlo)
                    if i == 0 and s:
                        mod_cols(6 + s)
                mod_rows(7 + s)
            w = arrive("pool_br", 0, POOLG, D)
            moved(pe, "y1", 1)
            for i in range(4):
                ins = fmajor(bank("ypool", i), w, y1, 2 * i * P, 2, ks=POOLG)
                full(ins)
                if i == 0:
                    mod_cols(10)
            mod_rows(11)
            pe.wait_ge(G["glo_ready"], 1)
            for i in range(4):
                f_half(bank("ygla", i), 12 + i, ghi, glo)
                if i == 0:
                    mod_cols(11)
            for i in range(4):
                f_half(bank("mix", i), 16 + i, zhi, zlo, ready=(lambda kt: pe.wait_ge(G["zlo_ready"], kt // 2 + 1)) if i == 0 else None)
            sum_pairs("norm", 2, sq2, squares_ready(2))
            pe.wait_ge(G["h_ready"], 3 * KT)
            b = bank("router", 0)
            for tt in range(TT):
                br = b[:, tt * (NG + NE):(tt + 1) * (NG + NE)]
                for kt in range(KT):
                    pe.matmul(br, hT[:, kt, tt * P:(tt + 1) * P], w_rt[:, kt, :], start=(kt == 0), stop=False)
                ins = pe.matmul(br, ones[0:1, :], rb[0:1, :], start=False, stop=True)
            full(ins)
            for i in range(4):
                tt, q = divmod(i, 2)
                b = bank("ttok", i)
                for j in range(4):
                    ins = pe.transpose(b[:, j * P:(j + 1) * P], hT[:, 4 * q + j, tt * P:(tt + 1) * P], ident)
                full(ins)
            pe.wait_ge(G["chosen_ready"], 2)
            b = bank("rank", 0)
            pe.matmul(b[:, 0:NE], C("pre"), chosen[:, 0, :], start=True, stop=True)
            pe.matmul(b[:, NE:2 * NE], C("pre"), chosen[:, 1, :], start=True, stop=False)
            pe.matmul(b[:, NE:2 * NE], C("all"), chosen[:, 0, :], start=False, stop=True)
            pe.matmul(b[:, 2 * NE:3 * NE], C("all"), chosen[:, 0, :], start=True, stop=False)
            full(pe.matmul(b[:, 2 * NE:3 * NE], C("all"), chosen[:, 1, :], start=False, stop=True))

            def open_acc(k):
                for j in range(4):
                    ins = pe.matmul(acc[:, 2 * j:2 * j + 2, :], zrow, zmov, start=True, stop=False, skip_group_check=True)
                ins.then_inc(used, OPENED)

            zrow, zmov = C("zero")[:, 0:P], hT[:, 0:2, :]
            open_acc(0)
            s0 = SLAB_AT["moe", 0]
            moved(pe, "rank", 0)
            moved(pe, "ttok", 3)
            with pe.Fori(0, TURNS) as it:
                def t_bank(kind, j):
                    g = TURN_AT[kind, j] - RB
                    prev = TURN[g]
                    turn_moved(pe, it, prev[0], prev[1], back=int(g < 0))
                    return turn_bank(kind, j)

                def t_slab(j, part, k, w):
                    n = s0 + 3 * j + part
                    pe.wait_ge(landed[SLOT_OF[n]], it * (16 * 3 * EXPERTS_PER_TURN // MOE_RING) + 16 * NTH[n])
                    return view(n, k, w)

                pe.wait_ge(G["pick_ready"], it * 8 + 8)
                for q in range(2):
                    b = t_bank("x", q)
                    for kt in range(4):
                        for tt in range(TT):
                            f = (4 * q + kt) * P
                            ins = pe.matmul(b[:, kt * P:(kt + 1) * P], ttok[:, tt, f:f + P], pick[:, tt, :], start=(tt == 0), stop=(tt == 1))
                    full(ins)
                pe.wait_ge(G["put_ready"], it * 8 + 8)
                for q in range(2):
                    b = t_bank("w", q)
                    for j in range(2):
                        for tt in range(TT):
                            o = j * T + tt * P
                            ins = pe.transpose(b[:, o:o + P], put[:, 2 * q + j, tt, :], ident)
                    full(ins)
                for j in range(EXPERTS_PER_TURN):
                    for part, kind in enumerate(("up1", "up3")):
                        w = t_slab(j, part, KT, DE)
                        b = t_bank(kind, j)
                        if j == 0 and part == 0:
                            turn_moved(pe, it, "x", 0)
                            turn_moved(pe, it, "x", 1)
                        for kt in range(KT):
                            g = kt % 4
                            ins = pe.matmul(b[32 * g:32 * g + 32, :], xs[:, kt, j, :], w[:, kt, :], start=(kt < 4), stop=(kt >= 4))
                        full(ins)
                    for src, kind, up in ((h1, "t1", "up1"), (h3, "t3", "up3")):
                        turn_moved(pe, it, up, j)
                        b = t_bank(kind, j)
                        for f in range(4):
                            ins = pe.matmul(b[:, f * P:(f + 1) * P], src[:, f * P:(f + 1) * P], C("fold"), start=True, stop=True)
                        full(ins)
                    w = t_slab(j, 2, 4, D)
                    turn_moved(pe, it, "t3", j)
                    for half in range(2):
                        b = t_bank(f"down{half}", j)
                        for f in range(4):
                            ins = pe.matmul(b[32 * f:32 * f + 32, :], hidT[:, f, :], w[:, f, 512 * half:512 * half + 512], start=True, stop=True)
                        full(ins)
                    turn_moved(pe, it, "down0", j)
                    turn_moved(pe, it, "w", j // 2)
                    for m in range(KT):
                        if m == 4:
                            turn_moved(pe, it, "down1", j)
                        ins = pe.matmul(acc[:, m, :], ys[:, m * P:(m + 1) * P], putT[:, j, :], start=False, stop=True, skip_group_check=True)
                    done(ins)
            turn_moved(pe, TURNS - 1, "down0", EXPERTS_PER_TURN - 1)
            turn_moved(pe, TURNS - 1, "down1", EXPERTS_PER_TURN - 1)
            pe.wait_ge(G["flag_ready"], 1)
            with pe.If(pe.value_load(flag[0:1, 0:1]) > 0):
                with pe.Fori(0, NE) as e:
                    pe.wait_ge(d_landed, e * 48 + 48)
                    pe.wait_ge(G["dcol_ready"], e + 1)
                    w1, w3 = (dslab[j].rearrange("p (k n) -> p k n", k=KT) for j in range(2))
                    w2 = dslab[2].rearrange("p (k n) -> p k n", k=4)
                    for tt in range(TT):
                        ins = pe.matmul(d_bank(0)[:, tt * P:(tt + 1) * P], dcol[:, tt, :], ident, start=True, stop=True)
                    ins.then_inc(d_full, 1)
                    for i in range(2):
                        if i == 1:
                            pe.wait_ge(d_act, e * 3 + 1)
                        for n, w in ((1 + 2 * i, w1), (2 + 2 * i, w3)):
                            fmajor(d_bank(n), w, hT, 2 * i * P, 2).then_inc(d_full, 1)
                    pe.wait_ge(d_vec, e * 2 + 2)
                    for kt in range(4):
                        for m in range(KT):
                            ins = pe.matmul(acc[:, m, :], w2[:, kt, m * P:(m + 1) * P], dhid[:, kt, :], start=False, stop=True,
                                            skip_group_check=True)
                    ins.then_inc(d_used, 1)

            def x_ready(k):
                return lambda kt: pe.wait_ge(G["xlo_ready"], 4 * (k - 3) + kt // 2 + 1)

            sum_pairs("norm", 3, sq, squares_ready(3))
            for l in range(2):
                nt, nv = (8, 4) if l == 0 else (6, 3)
                h0 = HALF_AT[f"qkv{l}", 0, 0]
                def rotated(i):
                    moved(pe, f"qk{l}", i)
                    b = bank(f"rot{l}", i)
                    for j in range(2):
                        ins = pe.matmul(b[:, j * T:(j + 1) * T], C("rot"), qk_raw[:, 2 * i + j, :], start=True, stop=True)
                    full(ins)

                for i in range(nt):
                    f_half(bank(f"qk{l}", i), h0 + i, xhi, xlo, ready=x_ready(3 + 2 * l) if i == 0 else None)
                    if i:
                        rotated(i - 1)

                def values(i):
                    wh, wl = weights(h0 + nt + i)
                    b = bank(f"val{l}", i)
                    for tt in range(TT):
                        t_ = slice(tt * P, (tt + 1) * P)
                        for kt in range(KT):
                            o = b[:, tt * 256:tt * 256 + 256]
                            pe.matmul(o, xhi[:, kt, t_], wh[:, kt, :], start=(kt == 0), stop=False)
                            pe.matmul(o, xhi[:, kt, t_], wl[:, kt, :], start=False, stop=False)
                            ins = pe.matmul(o, xlo[:, kt, t_], wh[:, kt, :], start=False, stop=(kt == KT - 1))
                    full(ins)

                for i in range(nv - 1):
                    values(i)
                    if i == 0:
                        rotated(nt - 1)
                pe.wait_ge(G["rot_ready"], nt if l == 0 else 8 + nt)
                sets = SETS[l]
                k0 = 0 if l == 0 else len(SETS[0])

                def scores(i):
                    for j, h in enumerate(sets[i]):
                        b = bank(f"sc{l}", (i, j))
                        o = HD * (h % 2)
                        q_, k_ = qk[o:o + HD, h // 2, :], qk[o:o + HD, nt + h // 2, :]
                        pe.matmul(b[:, 0:P], q_[:, 0:P], k_[:, 0:P], start=True, stop=True)
                        full(pe.matmul(b[:, P:SC_W], q_[:, P:T], k_, start=True, stop=True))

                def turned(i):
                    k = k0 + i
                    pe.wait_ge(G["p_ready"], k + 1)
                    for j in range(len(sets[i])):
                        b = bank(f"pt{l}", (i, j))
                        for c in range(3):
                            ins = pe.transpose(b[:, c * P:(c + 1) * P], sc[:, k % 2, j, c * P:(c + 1) * P], ident)
                        full(ins)

                def weighted(i):
                    for j, h in enumerate(sets[i]):
                        moved(pe, f"pt{l}", (i, j))
                        b = bank(f"pv{l}", (i, j))
                        pT_ = pT_of(l, i, j)
                        o = HD * (h % 2)
                        hv = slice(h * HD, (h + 1) * HD)
                        pe.matmul(b[o:o + HD, 0:P], vt[:, 0, hv], pT_[:, 0:P], start=True, stop=True)
                        pe.matmul(b[o:o + HD, P:T], vt[:, 0, hv], pT_[:, P:2 * P], start=True, stop=False)
                        full(pe.matmul(b[o:o + HD, P:T], vt[:, 1, hv], pT_[:, 2 * P:3 * P], start=False, stop=True))

                n = len(sets)
                for t in range(n + 2):
                    if t < n:
                        scores(t)
                    if t == 0:
                        values(nv - 1)
                        moved(pe, f"val{l}", nv - 1)
                    if 1 <= t <= n:
                        turned(t - 1)
                    if t >= 2:
                        weighted(t - 2)
                moved(pe, f"pv{l}", (len(sets) - 1, len(sets[-1]) - 1))
                ks = (MOBA_H, DIL_H)[l] * HD // P
                h1_ = h0 + nt + nv
                for i in range(4):
                    f_half(bank(f"proj{l}", i), h1_ + i, atthi, attlo, ks=ks)
                sum_pairs("mean", 2 * l, xT, lambda i: moved(pe, f"proj{l}", i))
                sum_pairs("norm", 4 + 2 * l, sq, squares_ready(4 + 2 * l))
                hf = HALF_AT[f"ff_in{l}", 0, 0]
                for i in range(FF // 256):
                    f_half(bank(f"ff{l}", i), hf + i, xhi, xlo, ready=x_ready(4 + 2 * l) if i == 0 else None)
                ho = HALF_AT[f"ff_out{l}", 0, 0]
                for i in range(FF // 256):
                    wh, wl = weights(ho + i)
                    pe.wait_ge(G["ff_ready"], (FF // 256) * l + i + 1)
                    last = i == FF // 256 - 1
                    for k, m in ((k, m) for m in range(KT) for k in range(2)) if last else ((k, m) for k in range(2) for m in range(KT)):
                        kt = 2 * i + k
                        hi, lo = hffhi[:, kt, :], hfflo(kt)[:, 0, :]
                        o, c = acc[:, m, :], slice(m * P, (m + 1) * P)
                        ins = three(o, wh[:, k, c], wl[:, k, c], hi, lo, kt == 0 and m % 2 == 0, kt == FF // P - 1)
                        if last and k == 1 and m in (1, 3, 5):
                            ins.then_inc(G["acc_pair"], 1)
                    done(ins)
                sum_pairs("mean", 2 * l + 1, xT, lambda i: pe.wait_ge(G["acc_out"], 4 * (l + 1) + i + 1))
                sum_pairs("norm", 5 + 2 * l, sq, squares_ready(5 + 2 * l))
            for i in range(4):
                q, tt = divmod(i, 2)
                b = bank("out", i)
                pe.wait_ge(G["h_ready"], 7 * KT + 4 * q + 4)
                for j in range(4):
                    ins = pe.transpose(b[:, j * P:(j + 1) * P], xT[:, 4 * q + j, tt * P:(tt + 1) * P], ident)
                full(ins)


_INS = ["x", "c", "ctx", "c_ctx", "w_mod", "b_mod", "norm1_g", "norm2_g", "w_in", "gla_a2_f", "gla_ab_f", "gla_a2_b",
        "gla_ab_b", "gla_onorm_g", "pool_w", "pool_scale", "w_pool_br", "w_gla_br", "w_o", "router_grp_w", "router_grp_b",
        "router_exp_w", "router_exp_b", "moe_w1", "moe_w3", "moe_w2", "final_norm_g", "moba_w_qkv_2", "moba_w_o_2",
        "dil_w_qkv_2", "dil_w_o_2", "mlp_w_in_2", "mlp_w_out_2", "ln_mix_g_2", "ln_mix_b_2", "ln_mlp_g_2", "ln_mlp_b_2"]


def kernel(**inputs):
    from concourse import bacc
    from concourse.bass_utils import run_bass_kernel_spmd

    nc = bacc.Bacc("TRN2", target_bir_lowering=False, num_devices=1)
    arrays = {name: np.ascontiguousarray(inputs[name]) for name in _INS}
    arrays["consts"] = constants()[1]
    arrays["masks"] = score_masks()
    args = {name: nc.dram_tensor("in_" + name, v.shape, mybir.dt.from_np(v.dtype), kind="ExternalInput").ap()
            for name, v in arrays.items()}
    out = nc.dram_tensor("out_x", (1, T, D), mybir.dt.float32, kind="ExternalOutput").ap()
    build(nc, args, out)
    r = run_bass_kernel_spmd(nc, [{"in_" + name: v for name, v in arrays.items()}], core_ids=[0])
    return r.results[0]["out_x"]
```
